# Optimizing a Trainium2 kernel written in Bass

```python
import math
import jax
import jax.numpy as jnp
from jax import lax
import numpy as np

D_MODEL = 1024
BATCH = 1
SEQ = 256
DEPTH = 1
DEC_BATCH = 8
DEC_SEQ = 16
PAST_LEN = 256

CHUNK = 64
EPS = 1e-6
A_HEADS = 4
A_DK = 128
A_DV = 128
A_WIDTH = A_HEADS * A_DV
A_BLK = 16
B_HEADS = 8
B_KV_HEADS = 2
B_HD = 64
B_WIDTH = B_HEADS * B_HD
IDX_HEADS = 8
IDX_DIM = 64
TOPK_MAX = 256
Q_BLOCK = 128
ROPE_THETA = 500000.0
P_HEADS = 8
P_NKEYS = 128
P_NEXP = P_NKEYS * P_NKEYS
P_DKEY = 128
P_TOPK = 16
P_TOK_BLOCK = 128

MIX_WIDTH = A_WIDTH + B_WIDTH
SPLIT_SIZES = [A_HEADS * A_DK, A_HEADS * A_DK, A_HEADS * A_DV, A_HEADS * A_DV,
               B_HEADS * B_HD, B_KV_HEADS * B_HD, B_KV_HEADS * B_HD,
               IDX_HEADS * IDX_DIM, IDX_DIM, IDX_HEADS]
SPLIT_POINTS = [int(v) for v in np.cumsum(SPLIT_SIZES)[:-1]]
N_IN = sum(SPLIT_SIZES)

kernel_name = 'hymba_hgrn2_dsa_peer_stream_step'

def rmsnorm(x, g):
    xf = x.astype(jnp.float32)
    y = xf * lax.rsqrt(jnp.mean(xf * xf, axis=-1, keepdims=True) + EPS)
    return (y * g.astype(jnp.float32)).astype(x.dtype)

def rope_partial(x, pos):
    rot = x.shape[-1] // 4
    half = rot // 2
    inv_freq = ROPE_THETA ** (-(jnp.arange(half, dtype=jnp.float32) * 2.0 / rot))
    ang = pos.astype(jnp.float32)[:, None] * inv_freq[None, :]
    cos = jnp.cos(ang)[None, :, None, :]
    sin = jnp.sin(ang)[None, :, None, :]
    xr = x[..., :rot].astype(jnp.float32)
    x1, x2 = xr[..., :half], xr[..., half:]
    xr = jnp.concatenate([x1 * cos - x2 * sin, x2 * cos + x1 * sin], axis=-1)
    return jnp.concatenate([xr.astype(x.dtype), x[..., rot:]], axis=-1)

def project_groups(xn, w_in, lb, b_qnorm, b_knorm, idx_knorm, pos):
    B, T, _ = xn.shape
    z = jnp.einsum('btd,dn->btn', xn, w_in)
    aq, af, ai, ag, bq, bk, bv, iq, ik, iw = jnp.split(z, SPLIT_POINTS, axis=-1)
    f = lb + (1.0 - lb) * jax.nn.sigmoid(af.astype(jnp.float32))
    a_q = jax.nn.silu(aq).reshape(B, T, A_HEADS, A_DK)
    a_k = (1.0 - f).reshape(B, T, A_HEADS, A_DK)
    a_logf = jnp.log(f).reshape(B, T, A_HEADS, A_DK)
    a_v = ai.reshape(B, T, A_HEADS, A_DV)
    a_g = ag.reshape(B, T, A_HEADS, A_DV)
    b_q = rope_partial(rmsnorm(bq.reshape(B, T, B_HEADS, B_HD), b_qnorm), pos)
    b_k = rope_partial(rmsnorm(bk.reshape(B, T, B_KV_HEADS, B_HD), b_knorm), pos)
    b_v = bv.reshape(B, T, B_KV_HEADS, B_HD)
    i_q = rope_partial(iq.reshape(B, T, IDX_HEADS, IDX_DIM), pos)
    i_k = rope_partial(rmsnorm(ik.reshape(B, T, 1, IDX_DIM), idx_knorm), pos)[:, :, 0]
    i_w = iw * (IDX_HEADS ** -0.5)
    return a_q, a_k, a_logf, a_v, a_g, b_q, b_k, b_v, i_q, i_k, i_w

def hgrn2_scan(q, k, v, logf, s0):
    B, T = q.shape[0], q.shape[1]
    n_blk = -(-T // A_BLK)
    pad = n_blk * A_BLK - T

    def to_blocks(a):
        a = jnp.pad(a.astype(jnp.float32), ((0, 0), (0, pad), (0, 0), (0, 0)))
        return jnp.moveaxis(a.reshape(B, n_blk, A_BLK, a.shape[2], a.shape[3]), 1, 0)

    mask = jnp.tril(jnp.ones((A_BLK, A_BLK), dtype=bool))

    def step(S, blk):
        qc, kc, vc, gc = blk
        b = jnp.cumsum(gc, axis=1)
        b_last = b[:, -1]
        q_t = qc * jnp.exp(b)
        k_t = kc * jnp.exp(-b)
        att = jnp.where(mask, jnp.einsum('blhd,bshd->bhls', q_t, k_t), 0.0)
        o = jnp.einsum('bhls,bshv->blhv', att, vc) + jnp.einsum('blhd,bhdv->blhv', q_t, S)
        k_end = kc * jnp.exp(b_last[:, None] - b)
        S_new = S * jnp.exp(b_last)[..., None] + jnp.einsum('bshd,bshv->bhdv', k_end, vc)
        return S_new, o

    S, ob = lax.scan(step, s0, (to_blocks(q), to_blocks(k), to_blocks(v), to_blocks(logf)))
    o = jnp.moveaxis(ob, 0, 1).reshape(B, n_blk * A_BLK, A_HEADS, A_DV)[:, :T]
    return o, S

def dsa_attend(q, iq, iw, k, v, ik, q_pos, k_pos, topk):
    B, Tq = q.shape[0], q.shape[1]
    visible = (k_pos[None, :] // CHUNK) <= (q_pos[:, None] // CHUNK)
    dots = jnp.einsum('bqhd,bsd->bqhs', iq, ik).astype(jnp.float32)
    score = jnp.einsum('bqhs,bqh->bqs', jax.nn.relu(dots), iw.astype(jnp.float32)) * (IDX_DIM ** -0.5)
    score = jnp.where(visible[None], score, -jnp.inf)
    top_val, sel = lax.top_k(score, topk)
    valid = jnp.isfinite(top_val)
    gather = jax.vmap(lambda a, i: a[i])
    k_sel = gather(k, sel)
    v_sel = gather(v, sel)
    qg = q.reshape(B, Tq, B_KV_HEADS, B_HEADS // B_KV_HEADS, B_HD)
    logits = jnp.einsum('bqkgd,bqjkd->bqkgj', qg, k_sel).astype(jnp.float32) * (B_HD ** -0.5)
    logits = jnp.where(valid[:, :, None, None, :], logits, -jnp.inf)
    p = jax.nn.softmax(logits, axis=-1).astype(v.dtype)
    o = jnp.einsum('bqkgj,bqjkd->bqkgd', p, v_sel)
    return o.reshape(B, Tq, B_HEADS * B_HD)

def dsa_prompt(q, iq, iw, k, v, ik, pos, topk):
    B, T = q.shape[0], q.shape[1]
    nq = T // Q_BLOCK

    def blocks(a):
        return jnp.moveaxis(a.reshape((B, nq, Q_BLOCK) + a.shape[2:]), 1, 0)

    def one(args):
        qb, iqb, iwb, pb = args
        return dsa_attend(qb, iqb, iwb, k, v, ik, pb, pos, topk)

    out = lax.map(one, (blocks(q), blocks(iq), blocks(iw), pos.reshape(nq, Q_BLOCK)))
    return jnp.moveaxis(out, 0, 1).reshape(B, T, B_HEADS * B_HD)

def peer(xn, wq, subkeys, u, v):
    B, T, D = xn.shape
    n = B * T
    nb = -(-n // P_TOK_BLOCK)
    xf = jnp.pad(xn.reshape(n, D), ((0, nb * P_TOK_BLOCK - n), (0, 0))).reshape(nb, P_TOK_BLOCK, D)

    def block(xb):
        q = jnp.einsum('nd,dk->nk', xb, wq).reshape(P_TOK_BLOCK, P_HEADS, 2, P_DKEY // 2)
        s = jnp.einsum('nhcd,hckd->nhck', q, subkeys).astype(jnp.float32)
        sv, si = lax.top_k(s, P_TOPK)
        cand = (sv[:, :, 0, :, None] + sv[:, :, 1, None, :]).reshape(P_TOK_BLOCK, P_HEADS, P_TOPK * P_TOPK)
        cidx = (si[:, :, 0, :, None] * P_NKEYS + si[:, :, 1, None, :]).reshape(P_TOK_BLOCK, P_HEADS, P_TOPK * P_TOPK)
        fv, fi = lax.top_k(cand, P_TOPK)
        eidx = jnp.take_along_axis(cidx, fi, axis=-1)
        g = jax.nn.softmax(fv, axis=-1)
        ue = u[eidx]
        ve = v[eidx]
        act = jax.nn.gelu(jnp.einsum('nd,nhkd->nhk', xb, ue).astype(jnp.float32), approximate=False)
        return jnp.einsum('nhk,nhkd->nd', (g * act).astype(ve.dtype), ve)

    out = lax.map(block, xf).reshape(nb * P_TOK_BLOCK, D)[:n]
    return out.reshape(B, T, D)

def output_and_channel_mix(x, a_o, a_g, b_o, a_gnorm, w_o, norm2, p_wq, p_subkeys, p_u, p_v):
    B, T, _ = x.shape
    a_out = (rmsnorm(a_o.astype(x.dtype), a_gnorm) * jax.nn.silu(a_g)).reshape(B, T, A_WIDTH)
    mix = jnp.concatenate([a_out, b_o.astype(x.dtype)], axis=-1)
    h = x + jnp.einsum('btm,md->btd', mix, w_o)
    return h + peer(rmsnorm(h, norm2), p_wq, p_subkeys, p_u, p_v)

def setup_inputs(seed: int = 0) -> dict:
    key = jax.random.key(seed)
    ks = jax.random.split(key, 19)

    def nrm(k, shape, scale):
        return jax.random.normal(k, shape, jnp.float32) * scale

    def gain(k, shape):
        return 1.0 + 0.05 * jax.random.normal(k, shape, jnp.float32)

    return {
        'x_prompt': nrm(ks[0], (BATCH, SEQ, D_MODEL), 1.0),
        'x_sample': nrm(ks[1], (DEC_BATCH, DEC_SEQ, D_MODEL), 1.0),
        'cache_k': nrm(ks[2], (DEPTH, DEC_BATCH, PAST_LEN, B_KV_HEADS, B_HD), 1.0),
        'cache_v': nrm(ks[3], (DEPTH, DEC_BATCH, PAST_LEN, B_KV_HEADS, B_HD), 1.0),
        'cache_kidx': nrm(ks[4], (DEPTH, DEC_BATCH, PAST_LEN, IDX_DIM), 1.0),
        'state_hgrn': nrm(ks[5], (DEPTH, DEC_BATCH, A_HEADS, A_DK, A_DV), 0.3),
        'norm1': gain(ks[6], (DEPTH, D_MODEL)),
        'w_in': nrm(ks[7], (DEPTH, D_MODEL, N_IN), D_MODEL ** -0.5),
        'a_lb_raw': nrm(ks[8], (DEPTH + 1, A_HEADS * A_DK), 0.5),
        'a_gnorm': gain(ks[9], (DEPTH, A_DV)),
        'b_qnorm': gain(ks[10], (DEPTH, B_HD)),
        'b_knorm': gain(ks[11], (DEPTH, B_HD)),
        'idx_knorm': gain(ks[12], (DEPTH, IDX_DIM)),
        'w_o': nrm(ks[13], (DEPTH, MIX_WIDTH, D_MODEL), MIX_WIDTH ** -0.5),
        'norm2': gain(ks[14], (DEPTH, D_MODEL)),
        'p_wq': nrm(ks[15], (DEPTH, D_MODEL, P_HEADS * P_DKEY), D_MODEL ** -0.5),
        'p_subkeys': nrm(ks[16], (DEPTH, P_HEADS, 2, P_NKEYS, P_DKEY // 2), (P_DKEY // 2) ** -0.5),
        'p_u': nrm(ks[17], (DEPTH, P_NEXP, D_MODEL), D_MODEL ** -0.5),
        'p_v': nrm(ks[18], (DEPTH, P_NEXP, D_MODEL), P_HEADS ** -0.5),
    }

def reference(x_prompt, x_sample, cache_k, cache_v, cache_kidx, state_hgrn,
              norm1, w_in, a_lb_raw, a_gnorm, b_qnorm, b_knorm, idx_knorm, w_o,
              norm2, p_wq, p_subkeys, p_u, p_v):
    pos_p = jnp.arange(SEQ, dtype=jnp.int32)
    pos_s = PAST_LEN + jnp.arange(DEC_SEQ, dtype=jnp.int32)
    kpos_s = jnp.arange(PAST_LEN + DEC_SEQ, dtype=jnp.int32)
    topk_p = min(TOPK_MAX, SEQ // 4)
    topk_s = min(TOPK_MAX, (PAST_LEN + DEC_SEQ) // 4)
    lb_all = jnp.cumsum(jax.nn.softmax(a_lb_raw.astype(jnp.float32), axis=0), axis=0)

    xp, xs = x_prompt, x_sample
    nk_p, nv_p, ni_p, ns_p = [], [], [], []
    nk_s, nv_s, ni_s, ns_s = [], [], [], []
    for l in range(DEPTH):
        xn = rmsnorm(xp, norm1[l])
        a_q, a_k, a_logf, a_v, a_g, b_q, b_k, b_v, i_q, i_k, i_w = project_groups(
            xn, w_in[l], lb_all[l], b_qnorm[l], b_knorm[l], idx_knorm[l], pos_p)
        s0 = jnp.zeros((xp.shape[0], A_HEADS, A_DK, A_DV), jnp.float32)
        a_o, s_fin = hgrn2_scan(a_q, a_k, a_v, a_logf, s0)
        b_o = dsa_prompt(b_q, i_q, i_w, b_k, b_v, i_k, pos_p, topk_p)
        xp_new = output_and_channel_mix(xp, a_o, a_g, b_o, a_gnorm[l], w_o[l], norm2[l],
                                        p_wq[l], p_subkeys[l], p_u[l], p_v[l])
        nk_p.append(b_k)
        nv_p.append(b_v)
        ni_p.append(i_k)
        ns_p.append(s_fin.astype(xp.dtype))
        xp = xp_new

        xn = rmsnorm(xs, norm1[l])
        a_q, a_k, a_logf, a_v, a_g, b_q, b_k, b_v, i_q, i_k, i_w = project_groups(
            xn, w_in[l], lb_all[l], b_qnorm[l], b_knorm[l], idx_knorm[l], pos_s)
        a_o, s_fin = hgrn2_scan(a_q, a_k, a_v, a_logf, state_hgrn[l].astype(jnp.float32))
        k_all = jnp.concatenate([cache_k[l], b_k], axis=1)
        v_all = jnp.concatenate([cache_v[l], b_v], axis=1)
        ik_all = jnp.concatenate([cache_kidx[l], i_k], axis=1)
        b_o = dsa_attend(b_q, i_q, i_w, k_all, v_all, ik_all, pos_s, kpos_s, topk_s)
        xs_new = output_and_channel_mix(xs, a_o, a_g, b_o, a_gnorm[l], w_o[l], norm2[l],
                                        p_wq[l], p_subkeys[l], p_u[l], p_v[l])
        nk_s.append(b_k)
        nv_s.append(b_v)
        ni_s.append(i_k)
        ns_s.append(s_fin.astype(xs.dtype))
        xs = xs_new

    return (xp, xs,
            jnp.stack(nk_p, 0), jnp.stack(nv_p, 0), jnp.stack(ni_p, 0), jnp.stack(ns_p, 0),
            jnp.stack(nk_s, 0), jnp.stack(nv_s, 0), jnp.stack(ni_s, 0), jnp.stack(ns_s, 0))


_drawn_inputs = setup_inputs


def setup_inputs(seed=0):
    import zlib

    import numpy as np

    out = dict(_drawn_inputs(seed))
    spreads = {}
    factors = {'b_qnorm': 3.681}
    for name, (base, spread) in spreads.items():
        noise = np.random.default_rng([zlib.crc32(name.encode()), seed]).standard_normal(out[name].shape)
        drawn = base * np.exp(spread * noise) if base else spread * noise
        out[name] = jnp.asarray(drawn.astype(out[name].dtype))
    for name, factor in factors.items():
        out[name] = (out[name] * factor).astype(out[name].dtype)
    return out
```

```python
from contextlib import ExitStack

import numpy as np

import concourse.bass as bass
from concourse import mybir

F32 = mybir.dt.float32
U32 = mybir.dt.uint32
I32 = mybir.dt.int32
ALU = mybir.AluOpType
ACT = mybir.ActivationFunctionType
AX = mybir.AxisListType.X

P = 128
D = 1024
KC = D // P
NT = 3
TOK = NT * P
N_IN = 3400
EPS = 1e-6
AH = 4
AW = AH * P
BLK = 16
HD = 64
QH, KVH, IH = 8, 2, 8
NZ = 20
BD_, TS = 8, 16
PAST = 256
KS = PAST + TS
TOP_P, TOP_S = 64, 68
SPARE = 4
PH, PK, NKEY = 8, 16, 128
HEADS = NT * PH
RU = RV = 8

MASKED, PICKED, DUMMY, DROP = -3.0e38, -3.3e38, 3.0e38, -1.0e30

W_AQ, W_AF, W_AI, W_AG = (0, 512), (512, 512), (1024, 512), (1536, 512)
W_B0, W_B1, W_B2 = (2048, 512), (2560, 512), (3072, 328)
CHUNKS = ["B0", "B1", "B2", "AI", "AF", "AQ", "AG", "O0", "O1", "P0", "P1"]
WSLOTS = 3
C_ID, C_TT, C_ONE, C_SCAN, C_COS, C_SIN, C_IOTA, C_EVEN, C_ODD, C_END = (
    0, 128, 256, 384, 768, 792, 816, 832, 833, 834)


def product_order():
    o = [("xt", t, g) for t in range(NT) for g in range(2)] + [("lb",)]
    o += [("bp", t, c) for c in range(3) for t in range(NT)]
    o += [("vp", t) for t in range(NT)] + [("fp", h) for h in range(AH)]
    o += [(k, t) for t in range(NT) for k in ("tq", "ti", "tk")]
    o += [("kc", g) for g in range(4)] + [("ic", g) for g in range(4)]
    o += [("dt", 0, par, 0) for par in range(2)] + [("dt", 1, par, g) for par in range(2) for g in range(2)]
    o += [("wt",)] + [("ds", b) for b in range(BD_)]
    o += [("qp", h) for h in range(AH)] + [("gp", h) for h in range(AH)] + [("sc",)]
    o += [("lg", 0, kv, 0) for kv in range(2)] + [("pt", 0, kv, 0) for kv in range(2)] + [("pv", 0)]
    o += [("lg", 1, kv, g) for kv in range(2) for g in range(2)]
    o += [("pt", 1, kv, g) for kv in range(2) for g in range(2)] + [("pv", 1)]
    o += [("lgs", b) for b in range(BD_)] + [("pts", b) for b in range(BD_)] + [("pvs",)]
    for t in range(NT):
        o += [("ke", t), ("at", t)]
        o += [("u", t, b) for b in range(8)] + [("ot", t), ("ss", t)]
    o += [("wo", t, n) for n in range(2) for t in range(NT)]
    o += [("x2", t, g) for t in range(NT) for g in range(2)]
    o += [("sk", g) for g in range(2)] + [("qq", h) for h in range(PH)]
    o += [("se", t, c, g) for t in range(NT) for c in range(2) for g in range(2)]
    return o


ORDER = product_order()
PLACE = {name: (n % 8, n // 8 + 1) for n, name in enumerate(ORDER)}
LAST_OF_CHUNK = {"B0": ("bp", 2, 0), "B1": ("bp", 2, 1), "B2": ("bp", 2, 2), "AI": ("vp", 2), "AF": ("fp", 3),
                 "AQ": ("qp", 3), "AG": ("gp", 3), "O0": ("wo", 2, 0), "O1": ("wo", 2, 1)}


class Turns:

    def __init__(self, eng, step):
        self.eng, self.step, self.count = eng, step, {}

    def done(self, ins, sem=None, by=1):
        sem = self.step if sem is None else sem
        key = sem.name
        self.count[key] = self.count.get(key, 0) + by
        ins.then_inc(sem, by)
        self.eng.wait_ge(sem, self.count[key])


def pick(own, v, scores, top8, rounds):
    for _ in range(rounds):
        own.done(v.max(top8, scores))
        own.done(v.match_replace(out=scores, in_to_replace=top8, in_values=scores, imm_value=PICKED))


def top16(own, v, row, values, places):
    own.done(v.max(values[:, 0:8], row))
    own.done(v.max_index(places[:, 0:8], values[:, 0:8], row))
    own.done(v.match_replace(out=row, in_to_replace=values[:, 0:8], in_values=row, imm_value=PICKED))
    own.done(v.max(values[:, 8:16], row))
    own.done(v.max_index(places[:, 8:16], values[:, 8:16], row))


def trunk_kernel(nc, a):
    ctx = ExitStack()
    with ctx:
        def sb(name, cols, dt=F32, rows=P):
            return ctx.enter_context(nc.sbuf_tensor(name, [rows, cols], dt))

        def sem(name):
            return ctx.enter_context(nc.semaphore(name))

        def view(t, at, *dims):
            n = int(np.prod(dims))
            v = t[:, at:at + n]
            names = "abcd"[:len(dims)]
            if len(dims) == 1:
                return v
            return v.rearrange(f"p ({' '.join(names)}) -> p {' '.join(names)}",
                               **{k: d for k, d in zip(names, dims)})

        def wide(ap, axis, n):
            v = ap.unsqueeze(axis)
            shape = list(v.shape)
            shape[axis] = n
            return v.to_broadcast(shape)

        CST = sb("CST", C_END)
        IDENT, TTM, ONES = CST[:, C_ID:C_ID + P], CST[:, C_TT:C_TT + P], CST[:, C_ONE:C_ONE + P]
        SCAN = CST[:, C_SCAN:C_SCAN + TOK]
        COS, SIN = view(CST, C_COS, NT, 8), view(CST, C_SIN, NT, 8)
        IOTA = CST[:, C_IOTA:C_IOTA + PK]
        BMASK = sb("BMASK", P, I32)
        REP = view(sb("REP", BD_ * P), 0, BD_, P)
        GNORM = sb("GNORM", 1)
        LBRAW = sb("LBRAW", P, rows=8)
        SMALL = sb("SMALL", 512)
        VB = view(sb("VB", NT * P), 0, NT, P)
        IW = view(sb("IW", NT * IH), 0, NT, IH)
        PEN = [sb("PEN0", P), sb("PEN1", 2 * P), sb("PEN2", KS)]
        SCORE = sb("SCORE", KS + SPARE)
        TOP8 = sb("TOP8", 8)
        XNT_ = sb("XNT", KC * TOK)
        XNT = view(XNT_, 0, KC, TOK)
        X_ = sb("X", NT * D)
        X = view(X_, 0, NT, D)
        XN_ = sb("XN", NT * D)
        XN = view(XN_, 0, NT, D)
        NB = sb("NB", D)
        WR = sb("WR", WSLOTS * KC * 512)
        W = [view(WR, s * KC * 512, KC, 512) for s in range(WSLOTS)]
        HOLD = sb("HOLD", 7 * NT * AW - NT * AW)
        AIV = view(HOLD, 0, NT, AW)
        FG = view(HOLD, 1536, AH, TOK)
        SQ = view(HOLD, 3072, AH, TOK)
        SG = view(HOLD, 4608, AH, TOK)
        MIXA = view(HOLD, 6144, AH, TOK)
        MIXB = view(HOLD, 7680, AH, TOK)
        REG = sb("REG", 17152)

        ZB = view(REG, 0, NT, NZ, HD)
        KTS, IKTS = view(REG, 3840, BD_, KS), view(REG, 6016, BD_, KS)
        QBD, IQBD = view(REG, 8192, BD_, P), view(REG, 9216, BD_, P)
        QTP, IQTP = view(REG, 10240, 4, 2 * P), view(REG, 11264, 4, 2 * P)
        KTP, IKTP = view(REG, 12288, 2 * P), view(REG, 12544, 2 * P)
        WZ = view(REG, 12800, BD_, P)
        VN = view(REG, 13824, BD_, P)
        VC = view(REG, 14848, BD_, 2, P)
        WREP = view(REG, 16896, P)
        RS_ = view(REG, 0, BD_, KS)
        PTP = [view(REG, 0, 8, P), view(REG, 1024, 16, P)]
        RP = [view(X_, 0, 8, P), view(X_, 1024, 8, 2 * P)]
        PP = RP
        PS_ = view(XN_, 0, BD_, KS)
        PTS = view(X_, 0, BD_, 3, P)
        KCN, ICN = view(XN_, 0, BD_, 2, P), view(XN_, 2048, BD_, 2, HD)
        SQB = view(HOLD, 6144, NT, 12 * HD)
        GAIN = view(HOLD, 8448, 12 * HD)

        LF = view(REG, 0, AH, TOK)
        EB = view(REG, 1536, AH, TOK)
        CUM = view(REG, 3072, AH, TOK)
        KT = view(REG, 4608, AH, TOK)
        ATT = view(REG, 6144, NT, AH, P)
        ST = view(REG, 7680, BD_, AH, P)
        S = view(REG, 11776, 9, AH, P)
        KE = view(XN_, 0, 2, NT, AW)
        OSQ = view(HOLD, 1536, NT, AW)
        RSTD = view(REG, 3072, AW)
        NORMED = view(REG, 3584, AW)
        JUNK = view(REG, 4608, D)

        QP = view(REG, 0, PH, TOK)
        SKN, SKT = view(REG, 3072, 2, PH, HD), view(REG, 4096, PH, P)
        SS = [view(REG, 5120, 2, PH, NKEY), view(REG, 7168, 2, PH, NKEY)]
        CAND = view(REG, 9216, PH, PK, PK)
        OH1 = view(REG, 11776, PH * PK, PK)
        OH2 = view(REG, 13824, PH * PK, PK)
        SEL = HOLD[:, 7168:9216]
        SV, SIU, SIF = view(SEL, 0, 2, PH, PK), view(SEL, 256, 2, PH, PK), view(SEL, 512, 2, PH, PK)
        FV, FI = view(SEL, 768, PH, PK), view(SEL, 896, PH, PK)
        FPART, FPF, EPART = view(SEL, 1024, P), view(SEL, 1152, P), view(SEL, 1280, 2, P)
        EXF = view(SEL, 1536, PH, PK)
        GSUM = view(SEL, 1664, PH)
        EIDX = REG[:, 15872:15872 + HEADS * PK].bitcast(U32)
        GATE = REG[:, 16256:16256 + HEADS * PK]

        UBUF = [WR[:, s * D:(s + 1) * D] for s in range(RU)]
        VBUF = [WR[:, (RU + s) * D:(RU + s + 1) * D] for s in range(4)] + [HOLD[:, s * D:(s + 1) * D] for s in range(4)]
        DIAG = view(HOLD, 4096, PK, P)
        DJUNK = view(HOLD, 6144, D)
        STU, STV = sb("STU", 2 * PK, U32), sb("STV", 2 * PK, U32)
        DOTS, GELU, WGT = sb("DOTS", PK), sb("GELU", PK), sb("WGT", PK)
        ZERO = SMALL[:, 256:384]

        bank = [ctx.enter_context(nc.psum_tensor(f"bank{b}", [P, 512], F32)) for b in range(8)]
        full = [sem(f"full{b}") for b in range(8)]
        free = [sem(f"free{b}") for b in range(8)]

        cst_in, x_in, n1_in, lb_in, gain_in, kc_in, ic_in, vc_in, rep_in, st_in = [
            sem(n) for n in ("cst_in", "x_in", "n1_in", "lb_in", "gain_in", "kc_in", "ic_in", "vc_in", "rep_in", "st_in")]
        h_in, n2_in, sk_in, gn_in = [sem(n) for n in ("h_in", "n2_in", "sk_in", "gn_in")]
        w_in_slot = [sem(f"w_slot{s}") for s in range(WSLOTS)]
        dve_step, act_step, pool_step = sem("dve_step"), sem("act_step"), sem("pool_step")
        std1, xn_ready = sem("std1"), sem("xn_ready")
        lb_shift, lb_exp = sem("lb_shift"), sem("lb_exp")
        zb_act, zb_dve, qk_sq, qk_sum, qk_std, rope_done, wrep_done = [
            sem(n) for n in ("zb_act", "zb_dve", "qk_sq", "qk_sum", "qk_std", "rope_done", "wrep_done")]
        bd_zero, wz_ready, pen_ready = [
            sem(n) for n in ("bd_zero", "wz_ready", "pen_ready")]
        nmax, pnorm, vn_in, newkv_out = [
            sem(n) for n in ("nmax", "pnorm", "vn_in", "newkv_out")]
        mixb_ready = [sem(n) for n in ("mixb_ready")]
        f_done, logf, cum_done, e_pos, e_neg, gap_done, e_gap, key_done = [
            sem(n) for n in ("f_done", "logf", "cum_done", "e_pos", "e_neg", "gap_done", "e_gap", "key_done")]
        att_zero, osq_ready, mixa_ready, st_out = [
            sem(n) for n in ("att_zero", "osq_ready", "mixa_ready", "st_out")]
        std2, xn2_ready, ss_read = [
            sem(n) for n in ("std2", "xn2_ready", "ss_read")]
        top_ready, gate_exp, chosen = sem("top_ready"), sem("gate_exp"), sem("chosen")
        u_got = [sem(f"u_got{s}") for s in range(RU)]
        v_got = [sem(f"v_got{s}") for s in range(RV)]
        u_free, v_free, staged, go, dots_done, gelu_done, wgt_done, diag_ready = [
            sem(n) for n in ("u_free", "v_free", "staged", "go", "dots_done", "gelu_done", "wgt_done", "diag_ready")]
        y_full, y_ready, y_out = sem("y_full"), sem("y_ready"), sem("y_out")

        def take(eng, name):
            b, turn = PLACE[name]
            eng.wait_ge(full[b], turn)
            return bank[b]

        def stored(eng, name):
            b, turn = PLACE[name]
            eng.wait_ge(free[b], turn)

        def give(own, ins, name):
            b, turn = PLACE[name]
            ins.then_inc(free[b], 1)
            own.eng.wait_ge(free[b], turn)

        block = ctx.enter_context(nc.Block())

        def weight_source(chunk):
            if chunk[0] == "O":
                n = int(chunk[1]) * 512
                wa = a["w_o"][0, 0:AW, n:n + 512].rearrange("(c p) n -> p c n", p=P)
                wb = [a["w_o"][0, AW + kv * 256:AW + (kv + 1) * 256, n:n + 512].rearrange("(j d) n -> d j n", d=HD)
                      for kv in range(2)]
                return wa, wb
            if chunk[0] == "P":
                n = int(chunk[1]) * 512
                return a["p_wq"][0, :, n:n + 512].rearrange("(c p) n -> p c n", p=P), None
            at, n = {"B0": W_B0, "B1": W_B1, "B2": W_B2, "AI": W_AI, "AF": W_AF, "AQ": W_AQ, "AG": W_AG}[chunk]
            return a["w_in"][0, :, at:at + n].rearrange("(c p) n -> p c n", p=P), None

        landed, slot_count = {}, [0] * WSLOTS
        for n, chunk in enumerate(CHUNKS):
            slot_count[n % WSLOTS] += 48 if chunk[0] == "O" else 16
            landed[chunk] = (n % WSLOTS, slot_count[n % WSLOTS])

        @block.sync
        def _(sp):
            def load_weights(chunk):
                n = CHUNKS.index(chunk)
                s = n % WSLOTS
                if n >= WSLOTS:
                    take(sp, LAST_OF_CHUNK[CHUNKS[n - WSLOTS]])
                src, halves = weight_source(chunk)
                if halves is None:
                    sp.dma_start(W[s][:, :, 0:src.shape[2]], src).then_inc(w_in_slot[s], 16)
                else:
                    sp.dma_start(W[s][:, 0:4, :], src).then_inc(w_in_slot[s], 16)
                    for kv in range(2):
                        sp.dma_start(W[s][kv * HD:(kv + 1) * HD, 4:8, :], halves[kv]).then_inc(w_in_slot[s], 16)

            sp.dma_start(X[:, 0:2, :], a["x_prompt"][0].rearrange("(t p) d -> p t d", p=P)).then_inc(x_in, 16)
            sp.dma_start(X[:, 2, :], a["x_sample"].rearrange("b t d -> (b t) d")).then_inc(x_in, 16)
            sp.dma_start(CST[:, :], a["cst"]).then_inc(cst_in, 16)
            sp.dma_start(NB[:, :], a["norm1"].partition_broadcast(P).rearrange("p o d -> p (o d)")).then_inc(n1_in, 16)
            sp.dma_start(LBRAW[:, :], a["a_lb_raw"].rearrange("r (h p) -> (r h) p", p=P)).then_inc(lb_in, 16)
            load_weights("B0")
            load_weights("B1")
            load_weights("B2")
            for s, (src, n) in enumerate(((a["b_qnorm"], 8), (a["b_knorm"], 2), (a["idx_knorm"], 2))):
                at = {0: 0, 1: 8, 2: 10}[s]
                for i in range(n):
                    sp.dma_start(GAIN[:, (at + i) * HD:(at + i + 1) * HD],
                                 src.partition_broadcast(P).rearrange("p o d -> p (o d)")).then_inc(gain_in, 16)
            sp.dma_start(GNORM[:, :], a["a_gnorm"].rearrange("o p -> p o")).then_inc(gn_in, 16)
            sp.dma_start(VC, a["cache_v"][0].rearrange("b (s p) k d -> p b s (k d)", p=P)).then_inc(vc_in, 16)
            sp.dma_start(REP, a["rep"].rearrange("p (b c) -> p b c", c=P)).then_inc(rep_in, 16)
            sp.dma_start(BMASK[:, :], a["bmask"]).then_inc(rep_in, 16)
            take(sp, ("xt", 2, 1))
            take(sp, ("xt", 2, 0))
            sp.dma_start(KCN, a["cache_k"][0].rearrange("b (s p) k d -> p b s (k d)", p=P)).then_inc(kc_in, 16)
            sp.dma_start(ICN, a["cache_kidx"][0].rearrange("b (s p) d -> p b s d", p=P)).then_inc(ic_in, 16)
            sp.wait_ge(xn_ready, NT)
            sp.dma_start(NB[:, :], a["norm2"].partition_broadcast(P).rearrange("p o d -> p (o d)")).then_inc(n2_in, 16)
            for chunk in ("AI", "AF", "AQ", "AG", "O0", "O1"):
                load_weights(chunk)
            take(sp, ("pvs",))
            sp.dma_start(ST, a["state_hgrn"][0].rearrange("b h d v -> d b h v")).then_inc(st_in, 16)
            sp.dma_start(X[:, 0:2, :], a["x_prompt"][0].rearrange("(t p) d -> p t d", p=P)).then_inc(h_in, 16)
            sp.dma_start(X[:, 2, :], a["x_sample"].rearrange("b t d -> (b t) d")).then_inc(h_in, 16)
            load_weights("P0")
            load_weights("P1")
            sp.wait_ge(mixa_ready, NT)
            for c in range(2):
                sp.dma_start(SKN[:, c, :, :], a["p_subkeys"][0, :, c].rearrange("h k d -> k h d")).then_inc(sk_in, 16)

        @block.gpsimd
        def _(pool):
            own = Turns(pool, pool_step)
            own.done(nc.gpsimd.memset(QBD, 0.0), bd_zero)
            own.done(nc.gpsimd.memset(IQBD, 0.0), bd_zero)
            own.done(nc.gpsimd.memset(WZ, 0.0), bd_zero)
            pool.wait_ge(rope_done, 1)
            pool.wait_ge(zb_act, NT)
            for t in range(2):
                rows = slice(t * P, (t + 1) * P)
                pool.dma_start(a["nk_p"][rows], ZB[:, t, 8:10, :]).then_inc(newkv_out, 16)
                pool.dma_start(a["nv_p"][rows], VB[:, t, :]).then_inc(newkv_out, 16)
                pool.dma_start(a["ni_p"][rows], ZB[:, t, 10, :]).then_inc(newkv_out, 16)
            pool.dma_start(a["nk_s"], ZB[:, 2, 8:10, :]).then_inc(newkv_out, 16)
            pool.dma_start(a["nv_s"], VB[:, 2, :]).then_inc(newkv_out, 16)
            pool.dma_start(a["ni_s"], ZB[:, 2, 10, :]).then_inc(newkv_out, 16)
            for b in range(BD_):
                pool.dma_start(VN[0:TS, b, :], VB[b * TS:(b + 1) * TS, 2, :]).then_inc(vn_in, 16)
            take(pool, ("pvs",))
            own.done(nc.gpsimd.memset(ATT, 0.0), att_zero)
            own.done(nc.gpsimd.memset(ZERO, 0.0), att_zero)
            stored(pool, ("u", 1, 7))
            pool.dma_start(a["ns_p"].rearrange("h d v -> d h v"), S[:, 8, :, :]).then_inc(st_out, 16)
            stored(pool, ("u", 2, 7))
            pool.dma_start(a["ns_s"].rearrange("b h d v -> d b h v"), S[:, 0:8, :, :]).then_inc(st_out, 16)

            pool.wait_ge(chosen, NT)
            take(pool, ("se", 2, 1, 1))
            counts = {"staged": 0}

            def stage(buf, i, par):
                own_idx = EIDX[:, bass.ds(i * PK, PK)]
                nc.gpsimd.tensor_copy(buf[:, par * PK:(par + 1) * PK], own_idx).then_inc(staged, 1)

            def gather(i, kind, par, nth):
                buf, table, idx, got, freed = ((UBUF, a["p_u"], STU, u_got, u_free) if kind == "u" else
                                               (VBUF, a["p_v"], STV, v_got, v_free))
                stage(idx, i, par)
                for s in range(PK):
                    pool.wait_ge(freed, i * PK + s + 1)
                    if s == 0:
                        pool.wait_ge(staged, nth)
                    pool.sem_inc(go, 1)
                    nc.gpsimd.indirect_dma_start(
                        buf[s % RU], None, table, bass.IndirectOffsetOnAxis(idx[:, par * PK + s:par * PK + s + 1], 0)
                    ).then_inc(got[s % RU], 16)

            gather(0, "u", 0, 1)
            with pool.Fori(0, HEADS // 2 - 1) as j:
                gather(2 * j + 1, "u", 1, 4 * j + 2)
                gather(2 * j, "v", 0, 4 * j + 3)
                gather(2 * j + 2, "u", 0, 4 * j + 4)
                gather(2 * j + 1, "v", 1, 4 * j + 5)
            last = HEADS - 1
            gather(last, "u", 1, 2 * HEADS - 2)
            gather(last - 1, "v", 0, 2 * HEADS - 1)
            gather(last, "v", 1, 2 * HEADS)
            for t in range(NT):
                pool.wait_ge(y_ready, 2 * t + 2)
                pool.dma_start(a["y"][t * P:(t + 1) * P, :], X[:, t, :]).then_inc(y_out, 16)
            pool.wait_ge(newkv_out, 16 * 9)
            pool.wait_ge(st_out, 32)
            pool.wait_ge(y_out, 16 * NT)

        @block.scalar
        def _(act):
            own = Turns(act, act_step)

            def copy_out(name, out, in_=None, sem_=None, func=ACT.Copy, **kw):
                pb = take(act, name)
                give(own, nc.scalar.activation(out, pb[:, :] if in_ is None else in_(pb), func, **kw), name)

            act.wait_ge(x_in, 32)
            SS1, STD1 = SMALL[:, 0:3], SMALL[:, 3:6]
            for t in range(NT):
                own.done(nc.scalar.activation(view(XNT_, 0, D), X[:, t, :], ACT.Square, accum_out=SS1[:, t:t + 1]))
            own.done(nc.scalar.activation(STD1, SS1, ACT.Sqrt, bias=EPS, scale=1.0 / D), std1)
            for t in range(NT):
                for g in range(2):
                    pb = take(act, ("xt", t, g))
                    give(own, nc.scalar.activation(
                        XNT[:, 4 * g:4 * g + 4, t * P:(t + 1) * P], pb[:, :].rearrange("p (c n) -> p c n", c=4), ACT.Copy),
                        ("xt", t, g))
            act.wait_ge(lb_shift, 1)
            own.done(nc.scalar.activation(SMALL[:, 16:24], SMALL[:, 16:24], ACT.Exp), lb_exp)
            for t in range(NT):
                pb = take(act, ("bp", t, 0))
                give(own, nc.scalar.activation(
                    ZB[:, t, 0:8, :].rearrange("p (j k) d -> p k j d", k=2),
                    pb[:, :].rearrange("p (k j d) -> p k j d", k=2, j=4), ACT.Copy), ("bp", t, 0))
            for t in range(NT):
                pb = take(act, ("bp", t, 1))
                own.done(nc.scalar.activation(ZB[:, t, 8:10, :], pb[:, 0:128].rearrange("p (h d) -> p h d", h=2), ACT.Copy))
                own.done(nc.scalar.activation(VB[:, t, :], pb[:, 128:256], ACT.Copy), zb_act)
                give(own, nc.scalar.activation(
                    ZB[:, t, 12:16, :], pb[:, 256:512].rearrange("p (h d) -> p h d", h=4), ACT.Copy), ("bp", t, 1))
            act.wait_ge(zb_dve, NT)
            own.done(nc.scalar.activation(SQB, ZB[:, :, 0:12, :].rearrange("p t h d -> p t (h d)"), ACT.Square), qk_sq)
            act.wait_ge(qk_sum, 1)
            QKS = SMALL[:, 32:68]
            own.done(nc.scalar.activation(QKS, QKS, ACT.Sqrt, bias=EPS, scale=1.0 / HD), qk_std)
            for t in range(NT):
                copy_out(("vp", t), AIV[:, t, :])
            for h in range(AH):
                copy_out(("fp", h), FG[:, h, :], lambda pb: pb[:, 0:TOK], func=ACT.Sigmoid)
            act.wait_ge(bd_zero, 3)
            for t in range(NT):
                for kind, plain, diag in (("tq", QTP, QBD), ("ti", IQTP, IQBD)):
                    pb = take(act, (kind, t))
                    src = pb[:, :].rearrange("p (j n) -> p j n", j=4)
                    if t < 2:
                        give(own, nc.scalar.activation(plain[:, :, t * P:(t + 1) * P], src, ACT.Copy), (kind, t))
                    else:
                        for k in range(2):
                            rows = slice(k * HD, (k + 1) * HD)
                            ins = nc.scalar.activation(
                                diag[rows, :, k * HD:(k + 1) * HD].rearrange("p b (j t) -> p j b t", j=4),
                                src[rows].rearrange("p j (b t) -> p j b t", b=BD_), ACT.Copy)
                            if k:
                                give(own, ins, (kind, t))
                            else:
                                own.done(ins)
                pb = take(act, ("tk", t))
                if t < 2:
                    own.done(nc.scalar.activation(KTP[:, t * P:(t + 1) * P], pb[:, 0:P], ACT.Copy))
                    give(own, nc.scalar.activation(IKTP[:, t * P:(t + 1) * P], pb[:, P:2 * P], ACT.Copy), ("tk", t))
                else:
                    own.done(nc.scalar.activation(KTS[:, :, PAST:KS], pb[:, 0:P].rearrange("p (b t) -> p b t", b=BD_), ACT.Copy))
                    give(own, nc.scalar.activation(
                        IKTS[:, :, PAST:KS], pb[:, P:2 * P].rearrange("p (b t) -> p b t", b=BD_), ACT.Copy), ("tk", t))
            for kind, dst in (("kc", KTS), ("ic", IKTS)):
                for g in range(4):
                    pb = take(act, (kind, g))
                    give(own, nc.scalar.activation(
                        dst[:, 2 * g:2 * g + 2, 0:PAST], pb[:, :].rearrange("p (b n) -> p b n", b=2), ACT.Copy), (kind, g))
            for par in range(2):
                pb = take(act, ("dt", 0, par, 0))
                give(own, nc.scalar.activation(
                    RP[0].rearrange("p (i k) n -> p k i n", k=2)[:, par], pb[:, :].rearrange("p (i n) -> p i n", i=4),
                    ACT.Relu), ("dt", 0, par, 0))
            for par in range(2):
                for g in range(2):
                    pb = take(act, ("dt", 1, par, g))
                    give(own, nc.scalar.activation(
                        RP[1].rearrange("p (i k) n -> p k i n", k=2)[:, par, 2 * g:2 * g + 2],
                        pb[:, :].rearrange("p (i n) -> p i n", i=2), ACT.Relu), ("dt", 1, par, g))
            act.wait_ge(newkv_out, 16 * 9)
            for b in range(BD_):
                copy_out(("ds", b), RS_[:, b, :], lambda pb: pb[:, 0:KS], func=ACT.Relu)
            for h in range(AH):
                copy_out(("qp", h), SQ[:, h, :], lambda pb: pb[:, 0:TOK], func=ACT.Silu)
            for h in range(AH):
                copy_out(("gp", h), SG[:, h, :], lambda pb: pb[:, 0:TOK], func=ACT.Silu)

            NM, SUM = SMALL[:, 96:120], SMALL[:, 120:144]
            steps = 0
            for t in range(2):
                nk, per = (t + 1) * P, 4 // (t + 1)
                for kv in range(2):
                    for g in range(t + 1):
                        steps += 1
                        pb = take(act, ("lg", t, kv, g))
                        act.wait_ge(nmax, steps)
                        for i in range(per):
                            head = kv * 4 + g * per + i
                            ins = nc.scalar.activation(
                                PP[t][:, head, :], pb[:, i * nk:(i + 1) * nk], ACT.Exp,
                                bias=NM[:, t * 8 + head:t * 8 + head + 1], scale=HD ** -0.5,
                                accum_out=SUM[:, t * 8 + head:t * 8 + head + 1])
                            if i == per - 1:
                                give(own, ins, ("lg", t, kv, g))
                            else:
                                own.done(ins)
                for kv in range(2):
                    for g in range(t + 1):
                        at = (kv * 4 + g * per) * (t + 1)
                        pb = take(act, ("pt", t, kv, g))
                        give(own, nc.scalar.activation(PTP[t][:, at:at + 4, :], pb[:, :].rearrange("p (i n) -> p i n", i=4),
                                                       ACT.Copy), ("pt", t, kv, g))
                pb = take(act, ("pv", t))
                give(own, nc.scalar.activation(MIXB[:, :, t * P:(t + 1) * P], pb[:, :].rearrange("p (j n) -> p j n", j=4),
                                               ACT.Copy), ("pv", t))
            for b in range(BD_):
                steps += 1
                pb = take(act, ("lgs", b))
                act.wait_ge(nmax, steps)
                give(own, nc.scalar.activation(PS_[:, b, :], pb[:, 0:KS], ACT.Exp, bias=NM[:, 16 + b:17 + b],
                                               scale=HD ** -0.5, accum_out=SUM[:, 16 + b:17 + b]), ("lgs", b))
            for b in range(BD_):
                pb = take(act, ("pts", b))
                own.done(nc.scalar.activation(PTS[:, b, 0:2, :], pb[:, 0:2 * P].rearrange("p (s n) -> p s n", s=2), ACT.Copy))
                give(own, nc.scalar.activation(PTS[0:TS, b, 2, :], pb[0:TS, 2 * P:3 * P], ACT.Copy), ("pts", b))
            pb = take(act, ("pvs",))
            give(own, nc.scalar.activation(
                MIXB[:, :, 2 * P:TOK].rearrange("p j (b t) -> p b j t", b=BD_),
                pb[:, :].rearrange("p (b j t) -> p b j t", b=BD_, j=4), ACT.Copy), ("pvs",))

            act.wait_ge(f_done, 1)
            own.done(nc.scalar.activation(LF, FG, ACT.Ln), logf)
            act.wait_ge(cum_done, 1)
            own.done(nc.scalar.activation(EB, CUM, ACT.Exp), e_pos)
            own.done(nc.scalar.activation(KT, CUM, ACT.Exp, scale=-1.0), e_neg)
            act.wait_ge(gap_done, 1)
            own.done(nc.scalar.activation(LF, LF, ACT.Exp), e_gap)
            act.wait_ge(key_done, 1)
            for t in range(NT):
                pb = take(act, ("ot", t))
                own.done(nc.scalar.activation(OSQ[:, t, :], pb[:, :], ACT.Square), osq_ready)
                if t:
                    act.wait_ge(mixa_ready, t)
                copy_out(("ss", t), RSTD, func=ACT.Sqrt, bias=EPS, scale=1.0 / P)

            SS2, STD2 = SMALL[:, 6:9], SMALL[:, 9:12]
            for t in range(NT):
                stored(act, ("wo", t, 1))
                own.done(nc.scalar.activation(JUNK, X[:, t, :], ACT.Square, accum_out=SS2[:, t:t + 1]))
            own.done(nc.scalar.activation(STD2, SS2, ACT.Sqrt, bias=EPS, scale=1.0 / D), std2)
            for t in range(NT):
                for g in range(2):
                    pb = take(act, ("x2", t, g))
                    give(own, nc.scalar.activation(
                        XNT[:, 4 * g:4 * g + 4, t * P:(t + 1) * P], pb[:, :].rearrange("p (c n) -> p c n", c=4), ACT.Copy),
                        ("x2", t, g))
            for g in range(2):
                copy_out(("sk", g), SKT[:, 4 * g:4 * g + 4, :], lambda pb: pb[:, :].rearrange("p (h n) -> p h n", h=4))
            for h in range(PH):
                copy_out(("qq", h), QP[:, h, :], lambda pb: pb[:, 0:TOK])
            for t in range(NT):
                if t == 2:
                    act.wait_ge(ss_read, 1)
                for c in range(2):
                    for g in range(2):
                        copy_out(("se", t, c, g), SS[t % 2][:, c, 4 * g:4 * g + 4, :],
                                 lambda pb: pb[:, :].rearrange("p (h n) -> p h n", h=4))
            for t in range(NT):
                act.wait_ge(top_ready, t + 1)
                own.done(nc.scalar.activation(EXF, EXF, ACT.Exp), gate_exp)

            def weigh(i):
                act.wait_ge(dots_done, i + 1)
                nc.scalar.activation(GELU[:, :], DOTS[:, :], ACT.Gelu).then_inc(gelu_done, 1)
                act.wait_ge(wgt_done, i + 1)
                for s in range(PK):
                    if s == 0:
                        act.wait_ge(v_free, i * PK + RV)
                    nc.scalar.activation(DIAG[:, s, :], IDENT, ACT.Copy, scale=WGT[:, s:s + 1]).then_inc(diag_ready, 1)

            act.wait_ge(chosen, NT)
            with act.Fori(0, HEADS) as i:
                weigh(i)

        @block.vector
        def _(dve):
            own = Turns(dve, dve_step)
            v = nc.vector
            dve.wait_ge(std1, 1)
            dve.wait_ge(n1_in, 16)
            STD1 = SMALL[:, 3:6]
            own.done(v.reciprocal(STD1, STD1))
            for t in range(NT):
                own.done(v.scalar_tensor_tensor(out=XN[:, t, :], in0=X[:, t, :], scalar=STD1[:, t:t + 1], in1=NB[:, :],
                                                op0=ALU.mult, op1=ALU.mult), xn_ready)
            pb = take(dve, ("lb",))
            LBE, LBM, LB, OML = SMALL[:, 16:24], SMALL[:, 24:28], SMALL[:, 28:32], SMALL[:, 12:16]
            own.done(v.tensor_copy(LBE, pb[:, 0:8]))
            own.done(v.tensor_tensor(LBM, LBE[:, 0:4], LBE[:, 4:8], ALU.max))
            give(own, v.tensor_tensor(LBE[:, 0:4], LBE[:, 0:4], LBM, ALU.subtract), ("lb",))
            own.done(v.tensor_tensor(LBE[:, 4:8], LBE[:, 4:8], LBM, ALU.subtract), lb_shift)
            dve.wait_ge(lb_exp, 1)
            own.done(v.tensor_tensor(LBM, LBE[:, 0:4], LBE[:, 4:8], ALU.add))
            own.done(v.reciprocal(LBM, LBM))
            own.done(v.tensor_tensor(LB, LBE[:, 0:4], LBM, ALU.mult))
            own.done(v.tensor_scalar(OML, LB, -1.0, 1.0, ALU.mult, ALU.add))
            for t in range(NT):
                pb = take(dve, ("bp", t, 2))
                own.done(v.tensor_copy(ZB[:, t, 16:20, :], pb[:, 0:256].rearrange("p (h d) -> p h d", h=4)))
                own.done(v.tensor_copy(ZB[:, t, 10:12, :], wide(pb[:, 256:320], 1, 2)), zb_dve)
                give(own, v.tensor_scalar(IW[:, t, :], pb[:, 320:328], IH ** -0.5, HD ** -0.5, ALU.mult, ALU.mult),
                     ("bp", t, 2))
            dve.wait_ge(qk_sq, 1)
            QKS = SMALL[:, 32:68]
            own.done(v.tensor_reduce(QKS.rearrange("p (t h) -> p t h", t=NT), SQB.rearrange("p t (h d) -> p t h d", d=HD),
                                     axis=AX, op=ALU.add), qk_sum)
            dve.wait_ge(qk_std, 1)
            dve.wait_ge(gain_in, 16 * 12)
            own.done(v.reciprocal(QKS, QKS))
            ZN = ZB[:, :, 0:12, :]
            own.done(v.tensor_tensor(ZN, ZN, wide(QKS.rearrange("p (t h) -> p t h", t=NT), 3, HD), ALU.mult))
            ZF = ZN.rearrange("p t h d -> p t (h d)")
            own.done(v.tensor_tensor(ZF, ZF, wide(GAIN, 1, NT), ALU.mult))
            X1, X2 = ZB[:, :, :, 0:8], ZB[:, :, :, 8:16]
            cosw, sinw = wide(COS, 2, NZ), wide(SIN, 2, NZ)
            R = [view(HOLD, 6144 + k * 480, NT, NZ, 8) for k in range(4)]
            own.done(v.tensor_tensor(R[0], X1, cosw, ALU.mult))
            own.done(v.tensor_tensor(R[1], X2, sinw, ALU.mult))
            own.done(v.tensor_tensor(R[2], X2, cosw, ALU.mult))
            own.done(v.tensor_tensor(R[3], X1, sinw, ALU.mult))
            own.done(v.tensor_tensor(X1, R[0], R[1], ALU.subtract))
            own.done(v.tensor_tensor(X2, R[2], R[3], ALU.add), rope_done)
            own.done(v.tensor_copy(WREP.rearrange("p (k i t) -> p k i t", k=2, i=4),
                                   wide(IW[:, 2, :].rearrange("p (i k) -> p k i", k=2), 3, TS)), wrep_done)

            stored(dve, ("dt", 1, 1, 1))
            for t in range(2):
                nk = (t + 1) * P
                sc = SCORE[:, 0:nk]
                own.done(v.tensor_scalar(sc, RP[t][:, 0, :], IW[:, t, 0:1], None, ALU.mult))
                for h in range(1, IH):
                    own.done(v.scalar_tensor_tensor(out=sc, in0=RP[t][:, h, :], scalar=IW[:, t, h:h + 1], in1=sc,
                                                    op0=ALU.mult, op1=ALU.add))
                own.done(v.memset(SCORE[0:HD, nk - HD:nk], MASKED))
                pick(own, v, sc, TOP8[:, :], TOP_P // 8)
                own.done(v.tensor_scalar(PEN[t][:, :], sc, PICKED, DROP, ALU.not_equal, ALU.mult), pen_ready)
            pb = take(dve, ("wt",))
            give(own, v.tensor_tensor(
                REG[:, 12800:12800 + BD_ * (P + TS)].rearrange("p (b c) -> p b c", b=BD_)[:, :, 0:TS], pb[:, 0:P].rearrange("p (b t) -> p b t", b=BD_), TTM.rearrange("p (b t) -> p b t", b=BD_),
                ALU.mult), ("wt",))
            own.done(v.memset(SCORE[:, KS:KS + SPARE], DUMMY), wz_ready)
            pb = take(dve, ("sc",))
            give(own, v.tensor_copy(SCORE[:, 0:KS], pb[:, 0:KS]), ("sc",))
            pick(own, v, SCORE[:, :], TOP8[:, :], (TOP_S + SPARE) // 8)
            own.done(v.tensor_scalar(PEN[2][:, :], SCORE[:, 0:KS], PICKED, DROP, ALU.not_equal, ALU.mult), pen_ready)

            NM, SUM = SMALL[:, 96:120], SMALL[:, 120:144]

            def negmax(cols, src):
                own.done(v.tensor_reduce(NM[:, cols], src, axis=AX, op=ALU.max))
                own.done(v.tensor_scalar(NM[:, cols], NM[:, cols], -(HD ** -0.5), None, ALU.mult), nmax)

            for t in range(2):
                per = 4 // (t + 1)
                for kv in range(2):
                    for g in range(t + 1):
                        pb = take(dve, ("lg", t, kv, g))
                        c0 = t * 8 + kv * 4 + g * per
                        negmax(slice(c0, c0 + per), pb[:, :].rearrange("p (i n) -> p i n", i=per))
                stored(dve, ("lg", t, 1, t))
                cols = slice(t * 8, t * 8 + 8)
                own.done(v.reciprocal(SUM[:, cols], SUM[:, cols]))
                own.done(v.tensor_tensor(PP[t], PP[t], wide(SUM[:, cols], 2, (t + 1) * P), ALU.mult), pnorm)
            for b in range(BD_):
                pb = take(dve, ("lgs", b))
                negmax(slice(16 + b, 17 + b), pb[:, 0:KS])
            stored(dve, ("lgs", BD_ - 1))
            own.done(v.reciprocal(SUM[:, 16:24], SUM[:, 16:24]))
            own.done(v.tensor_tensor(PS_, PS_, wide(SUM[:, 16:24], 2, KS), ALU.mult), pnorm)

            for h in range(AH):
                own.done(v.tensor_scalar(FG[:, h, :], FG[:, h, :], OML[:, h:h + 1], LB[:, h:h + 1], ALU.mult, ALU.add),
                         None if h < AH - 1 else f_done)
            dve.wait_ge(logf, 1)
            own.done(v.tensor_scalar(FG, FG, -1.0, 1.0, ALU.mult, ALU.add))
            for h in range(AH):
                own.done(v.tensor_tensor_scan(out=CUM[:, h, :], data0=SCAN, data1=LF[:, h, :], initial=0.0,
                                              op0=ALU.mult, op1=ALU.add), None if h < AH - 1 else cum_done)
            blocks = "p h (b t) -> p (h b) t"
            cumb = CUM.rearrange(blocks, t=BLK)
            ends = cumb[:, :, BLK - 1:BLK].to_broadcast([P, AH * TOK // BLK, BLK])
            own.done(v.tensor_tensor(LF.rearrange(blocks, t=BLK), ends, cumb, ALU.subtract), gap_done)
            stored(dve, ("gp", AH - 1))
            dve.wait_ge(e_pos, 1)
            own.done(v.tensor_tensor(SQ, SQ, EB, ALU.mult))
            dve.wait_ge(e_neg, 1)
            own.done(v.tensor_tensor(KT, KT, FG, ALU.mult))
            dve.wait_ge(e_gap, 1)
            own.done(v.tensor_tensor(LF, LF, FG, ALU.mult), key_done)
            dve.wait_ge(rep_in, 32)
            dve.wait_ge(att_zero, 2)
            dve.wait_ge(st_in, 16)
            dve.wait_ge(gn_in, 16)
            for t in range(NT):
                pb = take(dve, ("ke", t))
                own.done(v.tensor_scalar(KE[:, 0, t, :], pb[:, :], CST[:, C_EVEN:C_EVEN + 1], None, ALU.mult))
                give(own, v.tensor_scalar(KE[:, 1, t, :], pb[:, :], CST[:, C_ODD:C_ODD + 1], None, ALU.mult), ("ke", t))
                pb = take(dve, ("at", t))
                give(own, v.copy_predicated(ATT[:, t, :, :], wide(BMASK[:, :], 1, AH),
                                            pb[:, :].rearrange("p (h n) -> p h n", h=AH)), ("at", t))
                for b in range(8):
                    pb = take(dve, ("u", t, b))
                    new = S[:, 8 if (t, b) == (1, 7) else (b + 1) % 8 if t < 2 else b]
                    if (t, b) in ((1, 0), (2, 0)):
                        take(dve, ("ot", t - 1))
                    if (t, b) == (0, 0):
                        give(own, v.tensor_copy(new, pb[:, :].rearrange("p (h n) -> p h n", h=AH)), ("u", t, b))
                        continue
                    for h in range(AH):
                        old = S[:, b % 8, h, :] if t < 2 else ST[:, b, h, :]
                        at = t * P + b * BLK + BLK - 1
                        ins = v.scalar_tensor_tensor(out=new[:, h, :], in0=old, scalar=EB[:, h, at:at + 1],
                                                     in1=pb[:, h * P:(h + 1) * P], op0=ALU.mult, op1=ALU.add)
                        if h == AH - 1:
                            give(own, ins, ("u", t, b))
                        else:
                            own.done(ins)
                stored(dve, ("ss", t))
                own.done(v.reciprocal(RSTD, RSTD))
                pb = take(dve, ("ot", t))
                give(own, v.scalar_tensor_tensor(out=NORMED, in0=pb[:, :], scalar=GNORM[:, 0:1], in1=RSTD,
                                                 op0=ALU.mult, op1=ALU.mult), ("ot", t))
                own.done(v.tensor_tensor(MIXA[:, :, t * P:(t + 1) * P], NORMED.rearrange("p (h n) -> p h n", h=AH),
                                         SG[:, :, t * P:(t + 1) * P], ALU.mult), mixa_ready)

            dve.wait_ge(h_in, 32)
            for n in range(2):
                for t in range(NT):
                    pb = take(dve, ("wo", t, n))
                    half = X[:, t, n * 512:(n + 1) * 512]
                    give(own, v.tensor_tensor(half, pb[:, :], half, ALU.add), ("wo", t, n))
            dve.wait_ge(std2, 1)
            dve.wait_ge(n2_in, 16)
            STD2 = SMALL[:, 9:12]
            own.done(v.reciprocal(STD2, STD2))
            for t in range(NT):
                own.done(v.scalar_tensor_tensor(out=XN[:, t, :], in0=X[:, t, :], scalar=STD2[:, t:t + 1], in1=NB[:, :],
                                                op0=ALU.mult, op1=ALU.mult), xn2_ready)
            dve.wait_ge(st_out, 32)
            for t in range(NT):
                stored(dve, ("se", t, 1, 1))
                s_ = SS[t % 2]
                for c in range(2):
                    for h in range(PH):
                        row = s_[:, c, h, :]
                        top16(own, v, row, SV[:, c, h, :], SIU[:, c, h, :].bitcast(U32))
                own.done(v.tensor_copy(SIF, SIU.bitcast(U32)), ss_read)
                own.done(v.tensor_tensor(CAND, wide(SV[:, 0], 3, PK), wide(SV[:, 1], 2, PK), ALU.add))
                for h in range(PH):
                    top16(own, v, CAND[:, h].rearrange("p i j -> p (i j)"), FV[:, h, :], FI[:, h, :].bitcast(U32))
                own.done(v.tensor_tensor(EXF, FV, FV[:, :, 0:1].to_broadcast([P, PH, PK]), ALU.subtract), top_ready)
                fiu = FI.bitcast(U32).rearrange("p h k -> p (h k)")
                for c in range(2):
                    if c == 0:
                        own.done(v.tensor_scalar(FPART.bitcast(U32), fiu, 4, None, ALU.logical_shift_right))
                    else:
                        own.done(v.tensor_scalar(FPART.bitcast(U32), fiu, PK - 1, None, ALU.bitwise_and))
                    own.done(v.tensor_copy(FPF, FPART.bitcast(U32)))
                    own.done(v.tensor_tensor(OH1, wide(FPF, 2, PK), wide(IOTA, 1, P), ALU.is_equal))
                    own.done(v.tensor_tensor(OH2.rearrange("p (h k) i -> p h k i", h=PH),
                                             OH1.rearrange("p (h k) i -> p h k i", h=PH), wide(SIF[:, c], 2, PK), ALU.mult))
                    own.done(v.tensor_reduce(EPART[:, c, :], OH2, axis=AX, op=ALU.add))
                own.done(v.scalar_tensor_tensor(out=EIDX[:, t * P:(t + 1) * P], in0=EPART[:, 0, :], scalar=float(NKEY),
                                                in1=EPART[:, 1, :], op0=ALU.mult, op1=ALU.add))
                dve.wait_ge(gate_exp, t + 1)
                own.done(v.tensor_reduce(GSUM, EXF, axis=AX, op=ALU.add))
                own.done(v.reciprocal(GSUM, GSUM))
                own.done(v.tensor_tensor(GATE[:, t * P:(t + 1) * P].rearrange("p (h k) -> p h k", h=PH), EXF,
                                         wide(GSUM, 2, PK), ALU.mult), chosen)

            def weights_of(i):
                dve.wait_ge(gelu_done, i + 1)
                v.tensor_tensor(WGT[:, :], GELU[:, :], GATE[:, bass.ds(i * PK, PK)], ALU.mult).then_inc(wgt_done, 1)

            def dots(i, t):
                for s in range(PK):
                    dve.wait_ge(u_got[s % RU], i * 32 + 16 * (s // RU + 1))
                    dve.wait_ge(u_free, i * PK + s + RU)
                    v.tensor_tensor_reduce(out=DJUNK, in0=UBUF[s % RU], in1=XN[:, t, :], scale=1.0, scalar=0.0,
                                           op0=ALU.mult, op1=ALU.add, accum_out=DOTS[:, s:s + 1]).then_inc(u_free, 1)
                dve.wait_ge(u_free, i * PK + PK + RU)
                v.memset(SMALL[:, 93:94], 0.0).then_inc(dots_done, 1)
                dve.wait_ge(dots_done, i + 1)
                weights_of(i)

            take(dve, ("se", 2, 1, 1))
            v.memset(SMALL[:, 94:95], 0.0).then_inc(u_free, RU)
            for t in range(NT):
                with dve.Fori(t * PH, (t + 1) * PH) as i:
                    dots(i, t)
            for t in range(NT):
                for n in range(2):
                    dve.wait_ge(y_full, 2 * t + n + 1)
                    own.done(v.tensor_copy(X[:, t, n * 512:(n + 1) * 512], bank[2 * t + n][:, :]), y_ready)

        @block.tensor
        def _(pe):
            mm = nc.tensor.matmul

            def start(name):
                b, turn = PLACE[name]
                if turn > 1:
                    pe.wait_ge(free[b], turn - 1)
                return bank[b]

            def end(ins, name):
                ins.then_inc(full[PLACE[name][0]], 1)

            def weights(chunk):
                s, count = landed[chunk]
                pe.wait_ge(w_in_slot[s], count)
                return W[s]

            def project_rows(name, w, t, n, lhs=XNT, cols=None):
                pb = start(name)
                for c in range(KC):
                    ins = mm(pb[:, 0:n], lhs[:, c, t * P:(t + 1) * P], w[:, c, 0:n], start=c == 0, stop=c == KC - 1)
                end(ins, name)

            def project_channels(name, w, h, lhs=XNT):
                pb = start(name)
                for c in range(KC):
                    ins = mm(pb[:, 0:TOK], w[:, c, h * P:(h + 1) * P], lhs[:, c, :], start=c == 0, stop=c == KC - 1)
                end(ins, name)

            def transposes(name, sources):
                pb = start(name)
                for i, src in enumerate(sources):
                    rows = src.shape[1]
                    ins = nc.tensor.transpose(pb[0:rows, i * P:(i + 1) * P], src, IDENT)
                end(ins, name)

            pe.wait_ge(cst_in, 16)
            for t in range(NT):
                pe.wait_ge(xn_ready, t + 1)
                for g in range(2):
                    transposes(("xt", t, g), [XN[:, t, (4 * g + c) * P:(4 * g + c + 1) * P] for c in range(4)])
            pe.wait_ge(lb_in, 16)
            pb = start(("lb",))
            end(nc.tensor.transpose(pb[:, 0:8], LBRAW[:, :], IDENT[0:8, 0:8]), ("lb",))
            for t in range(NT):
                for g in range(2):
                    stored(pe, ("xt", t, g))
            for c, (chunk, n) in enumerate((("B0", 512), ("B1", 512), ("B2", 328))):
                w = weights(chunk)
                for t in range(NT):
                    project_rows(("bp", t, c), w, t, n)
            w = weights("AI")
            for t in range(NT):
                project_rows(("vp", t), w, t, 512)
            w = weights("AF")
            for h in range(AH):
                project_channels(("fp", h), w, h)
            pe.wait_ge(rope_done, 1)
            for t in range(NT):
                flat = ZB[:, t, :, :].rearrange("p h d -> p (h d)")
                transposes(("tq", t), [flat[:, i * P:(i + 1) * P] for i in range(4)])
                transposes(("ti", t), [flat[:, (6 + i) * P:(7 + i) * P] for i in range(4)])
                transposes(("tk", t), [flat[:, i * P:(i + 1) * P] for i in (4, 5)])
            pe.wait_ge(kc_in, 16)
            for g in range(4):
                transposes(("kc", g), [KCN[:, 2 * g + i // 2, i % 2, :] for i in range(4)])
            pe.wait_ge(ic_in, 16)
            for g in range(4):
                pb = start(("ic", g))
                for i in range(4):
                    src = ICN[:, 2 * g + i // 2, i % 2, :]
                    for k in range(2):
                        ins = mm(pb[k * HD:(k + 1) * HD, i * P:(i + 1) * P], src, IDENT, start=True, stop=True)
                end(ins, ("ic", g))
            stored(pe, ("ic", 3))
            for t in range(2):
                nk, per = (t + 1) * P, 4 // (t + 1)
                for par in range(2):
                    rows = slice(par * HD, (par + 1) * HD)
                    for g in range(t + 1):
                        pb = start(("dt", t, par, g))
                        for i in range(per):
                            ins = mm(pb[:, i * nk:(i + 1) * nk], IQTP[rows, g * per + i, t * P:(t + 1) * P],
                                     IKTP[rows, 0:nk], start=True, stop=True)
                        end(ins, ("dt", t, par, g))
            pe.wait_ge(wrep_done, 1)
            pb = start(("wt",))
            end(nc.tensor.transpose(pb[:, 0:P], WREP, IDENT), ("wt",))
            for b in range(BD_):
                pb = start(("ds", b))
                end(mm(pb[:, 0:KS], IQBD[:, b, :], IKTS[:, b, :], start=True, stop=True), ("ds", b))
            w = weights("AQ")
            for h in range(AH):
                project_channels(("qp", h), w, h)
            w = weights("AG")
            for h in range(AH):
                project_channels(("gp", h), w, h)
            stored(pe, ("ds", BD_ - 1))
            pe.wait_ge(wz_ready, 1)
            pb = start(("sc",))
            for b in range(BD_):
                ins = mm(pb[:, 0:KS], WZ[:, b, :], RS_[:, b, :], start=b == 0, stop=b == BD_ - 1)
            end(ins, ("sc",))
            for t in range(2):
                nk, per = (t + 1) * P, 4 // (t + 1)
                pe.wait_ge(pen_ready, t + 1)
                for kv in range(2):
                    rows = slice(kv * HD, (kv + 1) * HD)
                    for g in range(t + 1):
                        pb = start(("lg", t, kv, g))
                        mm(pb[:, :], IDENT, wide(PEN[t][:, :], 1, per), start=True, stop=False)
                        for i in range(per):
                            ins = mm(pb[:, i * nk:(i + 1) * nk], QTP[rows, g * per + i, t * P:(t + 1) * P], KTP[rows, 0:nk],
                                     start=False, stop=i == per - 1)
                        end(ins, ("lg", t, kv, g))
                pe.wait_ge(pnorm, t + 1)
                if t == 0:
                    stored(pe, ("sc",))
                for kv in range(2):
                    for g in range(t + 1):
                        transposes(("pt", t, kv, g),
                                   [PP[t][:, kv * 4 + (g * 4 + i) // (t + 1), (i % (t + 1)) * P:(i % (t + 1) + 1) * P]
                                    for i in range(4)])
                stored(pe, ("pt", t, 1, t))
                pb = start(("pv", t))
                for kv in range(2):
                    for j in range(4):
                        for s in range(t + 1):
                            ins = mm(pb[kv * HD:(kv + 1) * HD, j * P:(j + 1) * P], VB[:, s, kv * HD:(kv + 1) * HD],
                                     PTP[t][:, (kv * 4 + j) * (t + 1) + s, :], start=s == 0, stop=s == t)
                end(ins, ("pv", t))
            pe.wait_ge(pen_ready, 3)
            pe.wait_ge(rep_in, 32)
            for b in range(BD_):
                pb = start(("lgs", b))
                mm(pb[:, 0:KS], REP[:, b, :], PEN[2][:, :], start=True, stop=False)
                end(mm(pb[:, 0:KS], QBD[:, b, :], KTS[:, b, :], start=False, stop=True), ("lgs", b))
            pe.wait_ge(pnorm, 3)
            for b in range(BD_):
                transposes(("pts", b), [PS_[:, b, 0:P], PS_[:, b, P:2 * P], PS_[:, b, 2 * P:KS]])
            stored(pe, ("pts", BD_ - 1))
            pe.wait_ge(vc_in, 16)
            pe.wait_ge(vn_in, 16 * BD_)
            pb = start(("pvs",))
            for b in range(BD_):
                for kv in range(2):
                    cols = slice(kv * HD, (kv + 1) * HD)
                    dst = pb[cols, b * HD:(b + 1) * HD]
                    for s in range(2):
                        mm(dst, VC[:, b, s, cols], PTS[:, b, s, cols], start=s == 0, stop=False)
                    ins = mm(dst, VN[0:TS, b, cols], PTS[0:TS, b, 2, cols], start=False, stop=True)
            end(ins, ("pvs",))
            pe.wait_ge(key_done, 1)
            for t in range(NT):
                toks = slice(t * P, (t + 1) * P)
                transposes(("ke", t), [LF[:, h, toks] for h in range(AH)])
                pb = start(("at", t))
                for h in range(AH):
                    ins = mm(pb[:, h * P:(h + 1) * P], KT[:, h, toks], SQ[:, h, toks], start=True, stop=True)
                end(ins, ("at", t))
                stored(pe, ("ke", t))
                for b in range(8):
                    pb = start(("u", t, b))
                    rows = slice(32 * (b // 2), 32 * (b // 2) + 32)
                    for h in range(AH):
                        cols = slice(h * P, (h + 1) * P)
                        ins = mm(pb[:, cols], KE[rows, b % 2, t, cols], AIV[rows, t, cols], start=True, stop=True)
                    end(ins, ("u", t, b))
                stored(pe, ("at", t))
                if t < 2:
                    stored(pe, ("u", t, 6))
                pb = start(("ot", t))
                for h in range(AH):
                    cols = slice(h * P, (h + 1) * P)
                    mm(pb[:, cols], AIV[:, t, cols], ATT[:, t, h, :], start=True, stop=False)
                    for b in range(1 if t == 0 else 0, 8):
                        state = S[:, b, h, :] if t < 2 else ST[:, b, h, :]
                        ins = mm(pb[:, h * P + b * BLK:h * P + (b + 1) * BLK], state,
                                 SQ[:, h, t * P + b * BLK:t * P + (b + 1) * BLK], start=False, stop=b == 7)
                end(ins, ("ot", t))
                pe.wait_ge(osq_ready, t + 1)
                pb = start(("ss", t))
                end(mm(pb[:, :], ONES, OSQ[:, t, :], start=True, stop=True), ("ss", t))
            stored(pe, ("pvs",))
            pe.wait_ge(mixa_ready, NT)
            for n in range(2):
                w = weights(f"O{n}")
                for t in range(NT):
                    pb = start(("wo", t, n))
                    toks = slice(t * P, (t + 1) * P)
                    for c in range(KC):
                        ins = mm(pb[:, :], (MIXA if c < 4 else MIXB)[:, c % 4, toks], w[:, c, :],
                                 start=c == 0, stop=c == KC - 1)
                    end(ins, ("wo", t, n))
            for t in range(NT):
                pe.wait_ge(xn2_ready, t + 1)
                for g in range(2):
                    transposes(("x2", t, g), [XN[:, t, (4 * g + c) * P:(4 * g + c + 1) * P] for c in range(4)])
            pe.wait_ge(sk_in, 32)
            for g in range(2):
                pb = start(("sk", g))
                for i in range(4):
                    for c in range(2):
                        ins = mm(pb[c * HD:(c + 1) * HD, i * P:(i + 1) * P], SKN[:, c, 4 * g + i, :], IDENT,
                                 start=True, stop=True)
                end(ins, ("sk", g))
            for t in range(NT):
                for g in range(2):
                    stored(pe, ("x2", t, g))
            for n in range(2):
                w = weights(f"P{n}")
                for h in range(4):
                    project_channels(("qq", 4 * n + h), w, h)
            for g in range(2):
                stored(pe, ("sk", g))
            for h in range(PH):
                stored(pe, ("qq", h))
            for t in range(NT):
                for c in range(2):
                    rows = slice(c * HD, (c + 1) * HD)
                    for g in range(2):
                        pb = start(("se", t, c, g))
                        for i in range(4):
                            ins = mm(pb[:, i * P:(i + 1) * P], QP[rows, 4 * g + i, t * P:(t + 1) * P],
                                     SKT[rows, 4 * g + i, :], start=True, stop=True)
                        end(ins, ("se", t, c, g))
            for b in range(8):
                last = max(n for n, name in enumerate(ORDER) if n % 8 == b)
                stored(pe, ORDER[last])
            pe.wait_ge(att_zero, 2)
            for t in range(NT):
                acc = [bank[2 * t], bank[2 * t + 1]]
                for n in range(2):
                    ins = mm(acc[n][:, :], IDENT, X[:, t, n * 512:(n + 1) * 512], start=True, stop=False)
                if t == 0:
                    ins.then_inc(v_free, RV)
                with pe.Fori(t * PH, (t + 1) * PH) as i:
                    for s in range(PK):
                        pe.wait_ge(v_got[s % RV], i * 32 + 16 * (s // RV + 1))
                        pe.wait_ge(diag_ready, i * PK + s + 1)
                        mm(acc[0][:, :], DIAG[:, s, :], VBUF[s % RV][:, 0:512], start=False, stop=False)
                        mm(acc[1][:, :], DIAG[:, s, :], VBUF[s % RV][:, 512:1024], start=False, stop=False).then_inc(v_free, 1)
                for n in range(2):
                    mm(acc[n][:, :], ZERO, X[:, t, n * 512:(n + 1) * 512], start=False, stop=True).then_inc(y_full, 1)



def constants():
    p, c = np.arange(P)[:, None], np.arange(P)[None, :]
    pos = np.stack([np.arange(P), P + np.arange(P), PAST + np.arange(P) % TS], 1).astype(np.float32)
    inv = (np.float32(500000.0) ** (-(np.arange(8, dtype=np.float32) * np.float32(2.0) / np.float32(16.0)))).astype(np.float32)
    ang = (pos[:, :, None] * inv).reshape(P, NT * 8)
    cst = np.zeros((P, C_END), np.float32)
    cst[:, C_ID:C_ID + P] = p == c
    cst[:, C_TT:C_TT + P] = p % TS == c % TS
    cst[:, C_ONE:C_ONE + P] = 1.0
    cst[:, C_SCAN:C_SCAN + TOK] = np.arange(TOK) % BLK != 0
    cst[:, C_COS:C_COS + NT * 8] = np.cos(ang)
    cst[:, C_SIN:C_SIN + NT * 8] = np.sin(ang)
    cst[:, C_IOTA:C_IOTA + PK] = np.arange(PK)
    cst[:, C_EVEN] = np.arange(P) // BLK % 2 == 0
    cst[:, C_ODD] = np.arange(P) // BLK % 2 == 1
    same = (p[:, :, None] // TS == np.arange(BD_)[None, :, None]) & (p[:, :, None] % TS == c[:, None, :] % TS)
    bmask = (p // BLK == c // BLK) & (p <= c)
    return {"cst": cst, "rep": same.astype(np.float32).reshape(P, BD_ * P), "bmask": bmask.astype(np.int32)}


INPUTS = ["x_prompt", "x_sample", "cache_k", "cache_v", "cache_kidx", "state_hgrn", "norm1", "w_in", "a_lb_raw",
          "a_gnorm", "b_qnorm", "b_knorm", "idx_knorm", "w_o", "norm2", "p_wq", "p_subkeys", "p_u", "p_v"]
OUTPUTS = {"y": (TOK, D), "nk_p": (2 * P, KVH * HD), "nv_p": (2 * P, KVH * HD), "ni_p": (2 * P, HD),
           "ns_p": (AH, P, P), "nk_s": (P, KVH * HD), "nv_s": (P, KVH * HD), "ni_s": (P, HD),
           "ns_s": (BD_, AH, P, P)}


def kernel(**inputs):
    import concourse.bacc as bacc
    from concourse.bass_utils import run_bass_kernel_spmd

    nc = bacc.Bacc("TRN2", target_bir_lowering=False, num_devices=1)
    arrays = {f"in_{n}": np.ascontiguousarray(inputs[n]) for n in INPUTS}
    arrays |= {f"in_{n}": v for n, v in constants().items()}
    a = {n[3:]: nc.dram_tensor(n, v.shape, mybir.dt.from_np(v.dtype), kind="ExternalInput").ap() for n, v in arrays.items()}
    a |= {n: nc.dram_tensor(f"out_{n}", shape, F32, kind="ExternalOutput").ap() for n, shape in OUTPUTS.items()}
    a["p_u"] = a["p_u"].rearrange("o e d -> (o e) d")
    a["p_v"] = a["p_v"].rearrange("o e d -> (o e) d")
    trunk_kernel(nc, a)
    r = run_bass_kernel_spmd(nc, [arrays], core_ids=[0]).results[0]
    o = {n: r[f"out_{n}"] for n in OUTPUTS}
    return (o["y"][0:2 * P].reshape(1, 2 * P, D), o["y"][2 * P:].reshape(BD_, TS, D),
            o["nk_p"].reshape(1, 1, 2 * P, KVH, HD), o["nv_p"].reshape(1, 1, 2 * P, KVH, HD),
            o["ni_p"].reshape(1, 1, 2 * P, HD), o["ns_p"].reshape(1, 1, AH, P, P),
            o["nk_s"].reshape(1, BD_, TS, KVH, HD), o["nv_s"].reshape(1, BD_, TS, KVH, HD),
            o["ni_s"].reshape(1, BD_, TS, HD), o["ns_s"].reshape(1, BD_, AH, P, P))
```

```python
from contextlib import ExitStack

import numpy as np

import concourse.bass as bass
from concourse import mybir

F32 = mybir.dt.float32
U32 = mybir.dt.uint32
I32 = mybir.dt.int32
ALU = mybir.AluOpType
ACT = mybir.ActivationFunctionType
AX = mybir.AxisListType.X

P = 128
D = 1024
KC = D // P
NT = 3
TOK = NT * P
N_IN = 3400
EPS = 1e-6
AH = 4
AW = AH * P
BLK = 16
HD = 64
QH, KVH, IH = 8, 2, 8
NZ = 20
BD_, TS = 8, 16
PAST = 256
KS = PAST + TS
TOP_P, TOP_S = 64, 68
SPARE = 4
PH, PK, NKEY = 8, 16, 128
HEADS = NT * PH
RU = RV = 8
ND = 8
SLOTS = PH * PK
ALL = 1 << 30

MASKED, PICKED, DUMMY, DROP = -3.0e38, -3.3e38, 3.0e38, -1.0e30

W_AQ, W_AF, W_AI, W_AG = (0, 512), (512, 512), (1024, 512), (1536, 512)
W_B0, W_B1, W_B2 = (2048, 512), (2560, 512), (3072, 328)
CHUNKS = ["B0", "B1", "B2", "AI", "AF", "AQ", "AG", "O0", "O1", "P0", "P1"]
WSLOTS = 3
C_ID, C_TT, C_ONE, C_SCAN, C_COS, C_SIN, C_IOTA, C_EVEN, C_ODD, C_END = (
    0, 128, 256, 384, 768, 792, 816, 832, 833, 834)


def product_order():
    o = [("xt", t, g) for t in range(NT) for g in range(2)] + [("lb",)]
    o += [("bp", t, c) for c in range(3) for t in range(NT)]
    o += [("vp", t) for t in range(NT)] + [("fp", h) for h in range(AH)]
    o += [(k, t) for t in range(NT) for k in ("tq", "ti", "tk")]
    o += [("kc", g) for g in range(4)] + [("ic", g) for g in range(4)]
    o += [("dt", 0, par, 0) for par in range(2)] + [("dt", 1, par, g) for par in range(2) for g in range(2)]
    o += [("wt",)] + [("ds", b) for b in range(BD_)]
    o += [("qp", h) for h in range(AH)] + [("gp", h) for h in range(AH)] + [("sc",)]
    o += [("lg", 0, kv, 0) for kv in range(2)] + [("pt", 0, kv, 0) for kv in range(2)] + [("pv", 0)]
    o += [("lg", 1, kv, g) for kv in range(2) for g in range(2)]
    o += [("pt", 1, kv, g) for kv in range(2) for g in range(2)] + [("pv", 1)]
    o += [("lgs", b) for b in range(BD_)] + [("pts", b) for b in range(BD_)] + [("pvs",)]
    loop_starts = 0
    for t in range(NT):
        if t == 1:
            loop_starts = len(o)
        us, ot = [("u", t, b) for b in range(8)], [("ot", t), ("ss", t)]
        o += [("ke", t), ("at", t)] + (us + ot if t < 2 else ot + us)
        o += [("wo", t, n) for n in range(KC)] + [("x2", t, g) for g in range(2)]
        if t == 0:
            o += [("sk", g) for g in range(2)]
        o += [("qq", t, h) for h in range(PH)] + [("se", t, c, g) for c in range(2) for g in range(2)]
    return o, loop_starts


def places():
    place, turns = {}, [0] * 8
    for n, name in enumerate(ORDER):
        b = n % 8 if n < LOOP_STARTS else (n - LOOP_STARTS) % 6
        turns[b] += 1
        place[name] = (b, turns[b])
    return place


ORDER, LOOP_STARTS = product_order()
PLACE = places()
LAST_OF_CHUNK = {"B0": ("bp", 2, 0), "B1": ("bp", 2, 1), "B2": ("bp", 2, 2), "AI": ("vp", 2), "AF": ("fp", 3),
                 "AQ": ("qp", 3), "AG": ("gp", 3), "O0": ("wo", 0, 3), "O1": ("wo", 0, 7)}


class Turns:

    def __init__(self, eng, step):
        self.eng, self.step, self.count = eng, step, {}

    def done(self, ins, sem=None, by=1):
        sem = self.step if sem is None else sem
        key = sem.name
        self.count[key] = self.count.get(key, 0) + by
        ins.then_inc(sem, by)
        self.eng.wait_ge(sem, self.count[key])

    def mark(self, ins):
        self.count[self.step.name] = self.count.get(self.step.name, 0) + 1
        ins.then_inc(self.step, 1)

    def caught_up(self, behind=0):
        self.eng.wait_ge(self.step, self.count[self.step.name] - behind)


def in_slots(front):
    due = next(front)

    def upto(slot):
        nonlocal due
        while due <= slot:
            due = next(front, ALL + 1)
    return upto


def pick(own, v, scores, top8, rounds):
    for _ in range(rounds):
        own.done(v.max(top8, scores))
        own.done(v.match_replace(out=scores, in_to_replace=top8, in_values=scores, imm_value=PICKED))


def top16(own, v, rows, slot):
    for step in range(5):
        yield slot + step
        for row, values, places in rows:
            own.caught_up(len(rows) - 1)
            lo, hi = slice(0, 8), slice(8, 16)
            if step == 0:
                ins = v.max(values[:, lo], row)
            elif step == 1:
                ins = v.max_index(places[:, lo], values[:, lo], row)
            elif step == 2:
                ins = v.match_replace(out=row, in_to_replace=values[:, lo], in_values=row, imm_value=PICKED)
            elif step == 3:
                ins = v.max(values[:, hi], row)
            else:
                ins = v.max_index(places[:, hi], values[:, hi], row)
            own.mark(ins)


def trunk_kernel(nc, a):
    ctx = ExitStack()
    with ctx:
        def sb(name, cols, dt=F32, rows=P):
            return ctx.enter_context(nc.sbuf_tensor(name, [rows, cols], dt))

        def sem(name):
            return ctx.enter_context(nc.semaphore(name))

        def view(t, at, *dims):
            n = int(np.prod(dims))
            v = t[:, at:at + n]
            names = "abcd"[:len(dims)]
            if len(dims) == 1:
                return v
            return v.rearrange(f"p ({' '.join(names)}) -> p {' '.join(names)}",
                               **{k: d for k, d in zip(names, dims)})

        def wide(ap, axis, n):
            v = ap.unsqueeze(axis)
            shape = list(v.shape)
            shape[axis] = n
            return v.to_broadcast(shape)

        CST = sb("CST", C_END)
        IDENT, TTM, ONES = CST[:, C_ID:C_ID + P], CST[:, C_TT:C_TT + P], CST[:, C_ONE:C_ONE + P]
        SCAN = CST[:, C_SCAN:C_SCAN + TOK]
        COS, SIN = view(CST, C_COS, NT, 8), view(CST, C_SIN, NT, 8)
        IOTA = CST[:, C_IOTA:C_IOTA + PK]
        BMASK = sb("BMASK", P, I32)
        REP_ = sb("REP", BD_ * P)
        REP = view(REP_, 0, BD_, P)
        GNORM = sb("GNORM", 1)
        LBRAW = sb("LBRAW", P, rows=8)
        SMALL = sb("SMALL", 512)
        VB = view(sb("VB", NT * P), 0, NT, P)
        IW = view(sb("IW", NT * IH), 0, NT, IH)
        PEN = [sb("PEN0", P), sb("PEN1", 2 * P), sb("PEN2", KS)]
        SCORE = sb("SCORE", KS + SPARE)
        TOP8 = sb("TOP8", 8)
        XNT_ = sb("XNT", KC * TOK)
        XNT = view(XNT_, 0, KC, TOK)
        X_ = sb("X", NT * D)
        X = view(X_, 0, NT, D)
        XN_ = sb("XN", NT * D)
        XN = view(XN_, 0, NT, D)
        NB = sb("NB", D)
        WR = sb("WR", WSLOTS * KC * 512)
        W = [view(WR, s * KC * 512, KC, 512) for s in range(WSLOTS)]
        HOLD = sb("HOLD", 7 * NT * AW - NT * AW)
        AIV = view(HOLD, 0, NT, AW)
        FG = view(HOLD, 1536, AH, TOK)
        SQ = view(HOLD, 3072, AH, TOK)
        SG = view(HOLD, 4608, AH, TOK)
        MIXA = view(HOLD, 6144, AH, TOK)
        MIXB = view(HOLD, 7680, AH, TOK)
        REG = sb("REG", 17152)

        ZB = view(REG, 0, NT, NZ, HD)
        KTS, IKTS = view(REG, 3840, BD_, KS), view(REG, 6016, BD_, KS)
        QBD, IQBD = view(REG, 8192, BD_, P), view(REG, 9216, BD_, P)
        QTP, IQTP = view(REG, 10240, 4, 2 * P), view(REG, 11264, 4, 2 * P)
        KTP, IKTP = view(REG, 12288, 2 * P), view(REG, 12544, 2 * P)
        WZ = view(REG, 12800, BD_, P)
        VN = view(REG, 13824, BD_, P)
        VC = view(REG, 14848, BD_, 2, P)
        WREP = view(REG, 16896, P)
        RS_ = view(REG, 0, BD_, KS)
        PTP = [view(REG, 0, 8, P), view(REG, 1024, 16, P)]
        RP = [view(X_, 0, 8, P), view(X_, 1024, 8, 2 * P)]
        PP = RP
        PS_ = view(XN_, 0, BD_, KS)
        PTS = view(X_, 0, BD_, 3, P)
        KCN, ICN = view(XN_, 0, BD_, 2, P), view(XN_, 2048, BD_, 2, HD)
        SQB = view(HOLD, 6144, NT, 12 * HD)
        GAIN = view(HOLD, 8448, 12 * HD)

        KT = view(REG, 0, AH, TOK)
        LF = view(REG, 1536, AH, TOK)
        EB = view(REG, 3072, AH, TOK)
        CUM = view(REG, 4608, AH, TOK)
        S = view(REG, 3072, 9, AH, P)
        ATT = view(REG, 7680, AH, P)
        KE = view(REG, 8192, 2, AW)
        JUNK = view(REG, 8192, D)
        EBE = view(SMALL, 144, AH, TOK // BLK)
        OSQ = view(HOLD, 1536, AW)
        RSTD = view(HOLD, 2048, AW)
        NORMED = view(HOLD, 2560, AW)

        XN2 = view(XN_, 0, 2, D)
        XNT2 = view(XNT_, 0, KC, P)
        QP = view(XNT_, KC * P, PH, P)
        SKT = view(XNT_, 2 * KC * P, PH, P)
        WQ = [view(REP_, 0, KC, P), view(REG, 15752, KC, P)]
        SKN = view(REG, 15752, 2, PH, HD)

        SS = view(REG, 3584, 2, PH, NKEY)
        CAND = view(REG, 3584, PH, PK, PK)
        OH = view(XNT_, 0, PH * PK, PK)
        SEL = REG[:, 13312:14984]
        SV, SIU, SIF = view(SEL, 0, 2, PH, PK), view(SEL, 256, 2, PH, PK), view(SEL, 512, 2, PH, PK)
        FV, FI = view(SEL, 768, PH, PK), view(SEL, 896, PH, PK)
        FPART, FPF, EPART = view(SEL, 1024, P), view(SEL, 1152, P), view(SEL, 1280, 2, P)
        EXF = view(SEL, 1536, PH, PK)
        GSUM = view(SEL, 1664, PH)
        EIDX = REG[:, 14984:14984 + HEADS * PK].bitcast(U32)
        GATE = REG[:, 15368:15368 + HEADS * PK]

        UBUF = [WR[:, s * D:(s + 1) * D] for s in range(RU)]
        VBUF = [WR[:, (RU + s) * D:(RU + s + 1) * D] for s in range(4)] + [
            REG[:, 9216 + s * D:9216 + (s + 1) * D] for s in range(4)]
        DIAG = view(XN_, 2 * D, ND, P)
        STU, STV = sb("STU", 2 * PK, U32), sb("STV", 2 * PK, U32)
        DOTS, GELU, WGT = sb("DOTS", PK), sb("GELU", PK), sb("WGT", PK)
        ZERO = SMALL[:, 256:384]

        bank = [ctx.enter_context(nc.psum_tensor(f"bank{b}", [P, 512], F32)) for b in range(8)]
        full = [sem(f"full{b}") for b in range(8)]
        free = [sem(f"free{b}") for b in range(8)]

        cst_in, x_in, n1_in, lb_in, gain_in, kc_in, ic_in, vc_in, rep_in, st_in = [
            sem(n) for n in ("cst_in", "x_in", "n1_in", "lb_in", "gain_in", "kc_in", "ic_in", "vc_in", "rep_in", "st_in")]
        h_in, n2_in, sk_in, gn_in = [sem(n) for n in ("h_in", "n2_in", "sk_in", "gn_in")]
        w_in_slot = [sem(f"w_slot{s}") for s in range(WSLOTS)]
        dve_step, act_step, pool_step = sem("dve_step"), sem("act_step"), sem("pool_step")
        std1, xn_ready = sem("std1"), sem("xn_ready")
        lb_shift, lb_exp = sem("lb_shift"), sem("lb_exp")
        zb_act, zb_dve, qk_sq, qk_sum, qk_std, rope_done, wrep_done = [
            sem(n) for n in ("zb_act", "zb_dve", "qk_sq", "qk_sum", "qk_std", "rope_done", "wrep_done")]
        bd_zero, wz_ready, pen_ready = [
            sem(n) for n in ("bd_zero", "wz_ready", "pen_ready")]
        nmax, pnorm, vn_in, newkv_out = [
            sem(n) for n in ("nmax", "pnorm", "vn_in", "newkv_out")]
        mixb_ready = [sem(n) for n in ("mixb_ready")]
        f_done, logf, cum_done, e_pos, e_neg, gap_done, e_gap, key_done = [
            sem(n) for n in ("f_done", "logf", "cum_done", "e_pos", "e_neg", "gap_done", "e_gap", "key_done")]
        att_zero, osq_ready, mixa_ready, st_out = [
            sem(n) for n in ("att_zero", "osq_ready", "mixa_ready", "st_out")]
        std2, xn2_ready = [sem(n) for n in ("std2", "xn2_ready")]
        wq_in = [sem(f"wq_in{s}") for s in range(2)]
        top_ready, gate_exp, heads_chosen = sem("top_ready"), sem("gate_exp"), sem("heads_chosen")
        u_got = [sem(f"u_got{s}") for s in range(RU)]
        v_got = [sem(f"v_got{s}") for s in range(RV)]
        u_free, v_free, staged, go, dots_done, gelu_done, wgt_done, diag_ready = [
            sem(n) for n in ("u_free", "v_free", "staged", "go", "dots_done", "gelu_done", "wgt_done", "diag_ready")]
        y_full, y_ready, y_out = sem("y_full"), sem("y_ready"), sem("y_out")

        def take(eng, name):
            b, turn = PLACE[name]
            eng.wait_ge(full[b], turn)
            return bank[b]

        def stored(eng, name):
            b, turn = PLACE[name]
            eng.wait_ge(free[b], turn)

        def give(own, ins, name):
            b, turn = PLACE[name]
            ins.then_inc(free[b], 1)
            own.eng.wait_ge(free[b], turn)

        block = ctx.enter_context(nc.Block())

        def weight_source(chunk):
            if chunk[0] == "O":
                n = int(chunk[1]) * 512
                wa = a["w_o"][0, 0:AW, n:n + 512].rearrange("(c p) n -> p c n", p=P)
                wb = [a["w_o"][0, AW + kv * 256:AW + (kv + 1) * 256, n:n + 512].rearrange("(j d) n -> d j n", d=HD)
                      for kv in range(2)]
                return wa, wb
            if chunk[0] == "P":
                n = int(chunk[1]) * 512
                return a["p_wq"][0, :, n:n + 512].rearrange("(c p) n -> p c n", p=P), None
            at, n = {"B0": W_B0, "B1": W_B1, "B2": W_B2, "AI": W_AI, "AF": W_AF, "AQ": W_AQ, "AG": W_AG}[chunk]
            return a["w_in"][0, :, at:at + n].rearrange("(c p) n -> p c n", p=P), None

        landed, slot_count = {}, [0] * WSLOTS
        for n, chunk in enumerate(CHUNKS):
            slot_count[n % WSLOTS] += 48 if chunk[0] == "O" else 16
            landed[chunk] = (n % WSLOTS, slot_count[n % WSLOTS])

        small, small_count = [], [0, 0]
        for t in (1, 2):
            for kind in ("wo", "qq"):
                for n in range(KC):
                    s = len(small) % 2
                    small_count[s] += 48 if kind == "wo" else 16
                    small.append(((kind, t, n), s, small_count[s]))
        small_landed = {name: (s, count) for name, s, count in small}

        @block.sync
        def _(sp):
            def load_weights(chunk):
                n = CHUNKS.index(chunk)
                s = n % WSLOTS
                if n >= WSLOTS:
                    take(sp, LAST_OF_CHUNK[CHUNKS[n - WSLOTS]])
                src, halves = weight_source(chunk)
                if halves is None:
                    sp.dma_start(W[s][:, :, 0:src.shape[2]], src).then_inc(w_in_slot[s], 16)
                else:
                    sp.dma_start(W[s][:, 0:4, :], src).then_inc(w_in_slot[s], 16)
                    for kv in range(2):
                        sp.dma_start(W[s][kv * HD:(kv + 1) * HD, 4:8, :], halves[kv]).then_inc(w_in_slot[s], 16)

            sp.dma_start(X[:, 0:2, :], a["x_prompt"][0].rearrange("(t p) d -> p t d", p=P)).then_inc(x_in, 16)
            sp.dma_start(X[:, 2, :], a["x_sample"].rearrange("b t d -> (b t) d")).then_inc(x_in, 16)
            sp.dma_start(CST[:, :], a["cst"]).then_inc(cst_in, 16)
            sp.dma_start(NB[:, :], a["norm1"].partition_broadcast(P).rearrange("p o d -> p (o d)")).then_inc(n1_in, 16)
            sp.dma_start(LBRAW[:, :], a["a_lb_raw"].rearrange("r (h p) -> (r h) p", p=P)).then_inc(lb_in, 16)
            load_weights("B0")
            load_weights("B1")
            load_weights("B2")
            for s, (src, n) in enumerate(((a["b_qnorm"], 8), (a["b_knorm"], 2), (a["idx_knorm"], 2))):
                at = {0: 0, 1: 8, 2: 10}[s]
                for i in range(n):
                    sp.dma_start(GAIN[:, (at + i) * HD:(at + i + 1) * HD],
                                 src.partition_broadcast(P).rearrange("p o d -> p (o d)")).then_inc(gain_in, 16)
            sp.dma_start(GNORM[:, :], a["a_gnorm"].rearrange("o p -> p o")).then_inc(gn_in, 16)
            sp.dma_start(VC, a["cache_v"][0].rearrange("b (s p) k d -> p b s (k d)", p=P)).then_inc(vc_in, 16)
            sp.dma_start(REP, a["rep"].rearrange("p (b c) -> p b c", c=P)).then_inc(rep_in, 16)
            sp.dma_start(BMASK[:, :], a["bmask"]).then_inc(rep_in, 16)
            take(sp, ("xt", 2, 1))
            take(sp, ("xt", 2, 0))
            sp.dma_start(KCN, a["cache_k"][0].rearrange("b (s p) k d -> p b s (k d)", p=P)).then_inc(kc_in, 16)
            sp.dma_start(ICN, a["cache_kidx"][0].rearrange("b (s p) d -> p b s d", p=P)).then_inc(ic_in, 16)
            sp.wait_ge(xn_ready, NT)
            sp.dma_start(NB[:, :], a["norm2"].partition_broadcast(P).rearrange("p o d -> p (o d)")).then_inc(n2_in, 16)
            for chunk in ("AI", "AF", "AQ", "AG", "O0", "O1"):
                load_weights(chunk)
            take(sp, ("pvs",))
            sp.dma_start(X[:, 0:2, :], a["x_prompt"][0].rearrange("(t p) d -> p t d", p=P)).then_inc(h_in, 16)
            sp.dma_start(X[:, 2, :], a["x_sample"].rearrange("b t d -> (b t) d")).then_inc(h_in, 16)
            load_weights("P0")
            load_weights("P1")
            for c in range(2):
                sp.dma_start(SKN[:, c, :, :], a["p_subkeys"][0, :, c].rearrange("h k d -> k h d")).then_inc(sk_in, 16)

            def load_small(k):
                (kind, _, n), s, _ = small[k]
                if k == 1:
                    take(sp, ("sk", 1))
                if k >= 2:
                    take(sp, small[k - 2][0])
                cols = slice(n * P, (n + 1) * P)
                if kind == "wo":
                    sp.dma_start(WQ[s][:, 0:4, :], a["w_o"][0, 0:AW, cols].rearrange("(c p) n -> p c n", p=P)).then_inc(wq_in[s], 16)
                    for kv in range(2):
                        first = AW + kv * 256
                        sp.dma_start(WQ[s][kv * HD:(kv + 1) * HD, 4:8, :],
                                     a["w_o"][0, first:first + 256, cols].rearrange("(j d) n -> d j n", d=HD)).then_inc(wq_in[s], 16)
                else:
                    sp.dma_start(WQ[s], a["p_wq"][0, :, cols].rearrange("(c p) n -> p c n", p=P)).then_inc(wq_in[s], 16)

            def store_y(t):
                sp.wait_ge(y_ready, 2 * t + 2)
                sp.dma_start(a["y"][t * P:(t + 1) * P, :], X[:, t, :]).then_inc(y_out, 16)

            load_small(0)
            load_small(1)
            stored(sp, ("u", 1, 7))
            sp.dma_start(a["ns_p"].rearrange("h d v -> d h v"), S[:, 8, :, :]).then_inc(st_out, 16)
            for k in range(2, 18):
                load_small(k)
            sp.wait_ge(heads_chosen, 2 * PH)
            sp.dma_start(S[:, 0:8, :, :], a["state_hgrn"][0].rearrange("b h d v -> d b h v")).then_inc(st_in, 16)
            store_y(0)
            stored(sp, ("u", 2, 7))
            sp.dma_start(a["ns_s"].rearrange("b h d v -> d b h v"), S[:, 0:8, :, :]).then_inc(st_out, 16)
            for k in range(18, 32):
                load_small(k)
            store_y(1)
            store_y(2)
            sp.wait_ge(st_out, 32)
            sp.wait_ge(y_out, 16 * NT)

        @block.gpsimd
        def _(pool):
            own = Turns(pool, pool_step)
            own.done(nc.gpsimd.memset(QBD, 0.0), bd_zero)
            own.done(nc.gpsimd.memset(IQBD, 0.0), bd_zero)
            own.done(nc.gpsimd.memset(WZ, 0.0), bd_zero)
            pool.wait_ge(rope_done, 1)
            pool.wait_ge(zb_act, NT)
            for t in range(2):
                rows = slice(t * P, (t + 1) * P)
                pool.dma_start(a["nk_p"][rows], ZB[:, t, 8:10, :]).then_inc(newkv_out, 16)
                pool.dma_start(a["nv_p"][rows], VB[:, t, :]).then_inc(newkv_out, 16)
                pool.dma_start(a["ni_p"][rows], ZB[:, t, 10, :]).then_inc(newkv_out, 16)
            pool.dma_start(a["nk_s"], ZB[:, 2, 8:10, :]).then_inc(newkv_out, 16)
            pool.dma_start(a["nv_s"], VB[:, 2, :]).then_inc(newkv_out, 16)
            pool.dma_start(a["ni_s"], ZB[:, 2, 10, :]).then_inc(newkv_out, 16)
            for b in range(BD_):
                pool.dma_start(VN[0:TS, b, :], VB[b * TS:(b + 1) * TS, 2, :]).then_inc(vn_in, 16)
            take(pool, ("pvs",))
            own.done(nc.gpsimd.memset(ATT, 0.0), att_zero)
            own.done(nc.gpsimd.memset(ZERO, 0.0), att_zero)

            pool.wait_ge(heads_chosen, PH)
            take(pool, ("se", 0, 1, 1))

            def stage(buf, i, par):
                nc.gpsimd.tensor_copy(buf[:, par * PK:(par + 1) * PK], EIDX[:, bass.ds(i * PK, PK)]).then_inc(staged, 1)

            def gather_u(i, par, s):
                pool.wait_ge(u_free, i * PK + s + 1)
                pool.sem_inc(go, 1)
                nc.gpsimd.indirect_dma_start(
                    UBUF[s % RU], None, a["p_u"], bass.IndirectOffsetOnAxis(STU[:, par * PK + s:par * PK + s + 1], 0)
                ).then_inc(u_got[s % RU], 16)

            def gather_v(i, par, s):
                pool.wait_ge(v_free, i * PK + s + 1)
                pool.sem_inc(go, 1)
                nc.gpsimd.indirect_dma_start(
                    VBUF[s % RV], None, a["p_v"], bass.IndirectOffsetOnAxis(STV[:, par * PK + s:par * PK + s + 1], 0)
                ).then_inc(v_got[s % RV], 16)

            def gather_both(i, par, nth):
                pool.wait_ge(heads_chosen, i + 2)
                stage(STU, i + 1, 1 - par)
                stage(STV, i, par)
                pool.wait_ge(staged, nth)
                for s in range(PK):
                    gather_u(i + 1, 1 - par, s)
                    gather_v(i, par, s)

            stage(STU, 0, 0)
            pool.wait_ge(staged, 1)
            for s in range(PK):
                gather_u(0, 0, s)
            with pool.Fori(0, HEADS // 2 - 1) as j:
                gather_both(2 * j, 0, 4 * j + 3)
                gather_both(2 * j + 1, 1, 4 * j + 5)
            gather_both(HEADS - 2, 0, 2 * HEADS - 1)
            stage(STV, HEADS - 1, 1)
            pool.wait_ge(staged, 2 * HEADS)
            for s in range(PK):
                gather_v(HEADS - 1, 1, s)
            pool.wait_ge(newkv_out, 16 * 9)

        @block.scalar
        def _(act):
            own = Turns(act, act_step)

            def copy_out(name, out, in_=None, sem_=None, func=ACT.Copy, **kw):
                pb = take(act, name)
                give(own, nc.scalar.activation(out, pb[:, :] if in_ is None else in_(pb), func, **kw), name)

            act.wait_ge(x_in, 32)
            SS1, STD1 = SMALL[:, 0:3], SMALL[:, 3:6]
            for t in range(NT):
                own.done(nc.scalar.activation(view(XNT_, 0, D), X[:, t, :], ACT.Square, accum_out=SS1[:, t:t + 1]))
            own.done(nc.scalar.activation(STD1, SS1, ACT.Sqrt, bias=EPS, scale=1.0 / D), std1)
            for t in range(NT):
                for g in range(2):
                    pb = take(act, ("xt", t, g))
                    give(own, nc.scalar.activation(
                        XNT[:, 4 * g:4 * g + 4, t * P:(t + 1) * P], pb[:, :].rearrange("p (c n) -> p c n", c=4), ACT.Copy),
                        ("xt", t, g))
            act.wait_ge(lb_shift, 1)
            own.done(nc.scalar.activation(SMALL[:, 16:24], SMALL[:, 16:24], ACT.Exp), lb_exp)
            for t in range(NT):
                pb = take(act, ("bp", t, 0))
                give(own, nc.scalar.activation(
                    ZB[:, t, 0:8, :].rearrange("p (j k) d -> p k j d", k=2),
                    pb[:, :].rearrange("p (k j d) -> p k j d", k=2, j=4), ACT.Copy), ("bp", t, 0))
            for t in range(NT):
                pb = take(act, ("bp", t, 1))
                own.done(nc.scalar.activation(ZB[:, t, 8:10, :], pb[:, 0:128].rearrange("p (h d) -> p h d", h=2), ACT.Copy))
                own.done(nc.scalar.activation(VB[:, t, :], pb[:, 128:256], ACT.Copy), zb_act)
                give(own, nc.scalar.activation(
                    ZB[:, t, 12:16, :], pb[:, 256:512].rearrange("p (h d) -> p h d", h=4), ACT.Copy), ("bp", t, 1))
            act.wait_ge(zb_dve, NT)
            own.done(nc.scalar.activation(SQB, ZB[:, :, 0:12, :].rearrange("p t h d -> p t (h d)"), ACT.Square), qk_sq)
            act.wait_ge(qk_sum, 1)
            QKS = SMALL[:, 32:68]
            own.done(nc.scalar.activation(QKS, QKS, ACT.Sqrt, bias=EPS, scale=1.0 / HD), qk_std)
            for t in range(NT):
                copy_out(("vp", t), AIV[:, t, :])
            for h in range(AH):
                copy_out(("fp", h), FG[:, h, :], lambda pb: pb[:, 0:TOK], func=ACT.Sigmoid)
            act.wait_ge(bd_zero, 3)
            for t in range(NT):
                for kind, plain, diag in (("tq", QTP, QBD), ("ti", IQTP, IQBD)):
                    pb = take(act, (kind, t))
                    src = pb[:, :].rearrange("p (j n) -> p j n", j=4)
                    if t < 2:
                        give(own, nc.scalar.activation(plain[:, :, t * P:(t + 1) * P], src, ACT.Copy), (kind, t))
                    else:
                        for k in range(2):
                            rows = slice(k * HD, (k + 1) * HD)
                            ins = nc.scalar.activation(
                                diag[rows, :, k * HD:(k + 1) * HD].rearrange("p b (j t) -> p j b t", j=4),
                                src[rows].rearrange("p j (b t) -> p j b t", b=BD_), ACT.Copy)
                            if k:
                                give(own, ins, (kind, t))
                            else:
                                own.done(ins)
                pb = take(act, ("tk", t))
                if t < 2:
                    own.done(nc.scalar.activation(KTP[:, t * P:(t + 1) * P], pb[:, 0:P], ACT.Copy))
                    give(own, nc.scalar.activation(IKTP[:, t * P:(t + 1) * P], pb[:, P:2 * P], ACT.Copy), ("tk", t))
                else:
                    own.done(nc.scalar.activation(KTS[:, :, PAST:KS], pb[:, 0:P].rearrange("p (b t) -> p b t", b=BD_), ACT.Copy))
                    give(own, nc.scalar.activation(
                        IKTS[:, :, PAST:KS], pb[:, P:2 * P].rearrange("p (b t) -> p b t", b=BD_), ACT.Copy), ("tk", t))
            for kind, dst in (("kc", KTS), ("ic", IKTS)):
                for g in range(4):
                    pb = take(act, (kind, g))
                    give(own, nc.scalar.activation(
                        dst[:, 2 * g:2 * g + 2, 0:PAST], pb[:, :].rearrange("p (b n) -> p b n", b=2), ACT.Copy), (kind, g))
            for par in range(2):
                pb = take(act, ("dt", 0, par, 0))
                give(own, nc.scalar.activation(
                    RP[0].rearrange("p (i k) n -> p k i n", k=2)[:, par], pb[:, :].rearrange("p (i n) -> p i n", i=4),
                    ACT.Relu), ("dt", 0, par, 0))
            for par in range(2):
                for g in range(2):
                    pb = take(act, ("dt", 1, par, g))
                    give(own, nc.scalar.activation(
                        RP[1].rearrange("p (i k) n -> p k i n", k=2)[:, par, 2 * g:2 * g + 2],
                        pb[:, :].rearrange("p (i n) -> p i n", i=2), ACT.Relu), ("dt", 1, par, g))
            act.wait_ge(newkv_out, 16 * 9)
            for b in range(BD_):
                copy_out(("ds", b), RS_[:, b, :], lambda pb: pb[:, 0:KS], func=ACT.Relu)
            for h in range(AH):
                copy_out(("qp", h), SQ[:, h, :], lambda pb: pb[:, 0:TOK], func=ACT.Silu)
            for h in range(AH):
                copy_out(("gp", h), SG[:, h, :], lambda pb: pb[:, 0:TOK], func=ACT.Silu)

            NM, SUM = SMALL[:, 96:120], SMALL[:, 120:144]
            steps = 0
            for t in range(2):
                nk, per = (t + 1) * P, 4 // (t + 1)
                for kv in range(2):
                    for g in range(t + 1):
                        steps += 1
                        pb = take(act, ("lg", t, kv, g))
                        act.wait_ge(nmax, steps)
                        for i in range(per):
                            head = kv * 4 + g * per + i
                            ins = nc.scalar.activation(
                                PP[t][:, head, :], pb[:, i * nk:(i + 1) * nk], ACT.Exp,
                                bias=NM[:, t * 8 + head:t * 8 + head + 1], scale=HD ** -0.5,
                                accum_out=SUM[:, t * 8 + head:t * 8 + head + 1])
                            if i == per - 1:
                                give(own, ins, ("lg", t, kv, g))
                            else:
                                own.done(ins)
                for kv in range(2):
                    for g in range(t + 1):
                        at = (kv * 4 + g * per) * (t + 1)
                        pb = take(act, ("pt", t, kv, g))
                        give(own, nc.scalar.activation(PTP[t][:, at:at + 4, :], pb[:, :].rearrange("p (i n) -> p i n", i=4),
                                                       ACT.Copy), ("pt", t, kv, g))
                pb = take(act, ("pv", t))
                give(own, nc.scalar.activation(MIXB[:, :, t * P:(t + 1) * P], pb[:, :].rearrange("p (j n) -> p j n", j=4),
                                               ACT.Copy), ("pv", t))
            for b in range(BD_):
                steps += 1
                pb = take(act, ("lgs", b))
                act.wait_ge(nmax, steps)
                give(own, nc.scalar.activation(PS_[:, b, :], pb[:, 0:KS], ACT.Exp, bias=NM[:, 16 + b:17 + b],
                                               scale=HD ** -0.5, accum_out=SUM[:, 16 + b:17 + b]), ("lgs", b))
            for b in range(BD_):
                pb = take(act, ("pts", b))
                own.done(nc.scalar.activation(PTS[:, b, 0:2, :], pb[:, 0:2 * P].rearrange("p (s n) -> p s n", s=2), ACT.Copy))
                give(own, nc.scalar.activation(PTS[0:TS, b, 2, :], pb[0:TS, 2 * P:3 * P], ACT.Copy), ("pts", b))
            pb = take(act, ("pvs",))
            give(own, nc.scalar.activation(
                MIXB[:, :, 2 * P:TOK].rearrange("p j (b t) -> p b j t", b=BD_),
                pb[:, :].rearrange("p (b j t) -> p b j t", b=BD_, j=4), ACT.Copy), ("pvs",))

            act.wait_ge(f_done, 1)
            own.done(nc.scalar.activation(LF, FG, ACT.Ln), logf)
            act.wait_ge(cum_done, 1)
            own.done(nc.scalar.activation(EB, CUM, ACT.Exp), e_pos)
            own.done(nc.scalar.activation(KT, CUM, ACT.Exp, scale=-1.0), e_neg)
            act.wait_ge(gap_done, 1)
            own.done(nc.scalar.activation(LF, LF, ACT.Exp), e_gap)
            act.wait_ge(key_done, 1)

            def front(t):
                yield 24 if t < 2 else 17
                pb = take(act, ("ot", t))
                own.done(nc.scalar.activation(OSQ, pb[:, :], ACT.Square), osq_ready)
                yield 26 if t < 2 else 19
                if t:
                    act.wait_ge(mixa_ready, t)
                copy_out(("ss", t), RSTD, func=ACT.Sqrt, bias=EPS, scale=1.0 / P)
                SS2, STD2 = SMALL[:, 6 + t:7 + t], SMALL[:, 9 + t:10 + t]
                yield 46
                stored(act, ("wo", t, KC - 1))
                own.done(nc.scalar.activation(JUNK, X[:, t, :], ACT.Square, accum_out=SS2))
                own.done(nc.scalar.activation(STD2, SS2, ACT.Sqrt, bias=EPS, scale=1.0 / D), std2)
                if t:
                    act.wait_ge(heads_chosen, PH * t)
                for g in range(2):
                    yield 50 + g
                    pb = take(act, ("x2", t, g))
                    give(own, nc.scalar.activation(XNT2[:, 4 * g:4 * g + 4, :], pb[:, :].rearrange("p (c n) -> p c n", c=4),
                                                   ACT.Copy), ("x2", t, g))
                if t == 0:
                    for g in range(2):
                        copy_out(("sk", g), SKT[:, 4 * g:4 * g + 4, :], lambda pb: pb[:, :].rearrange("p (h n) -> p h n", h=4))
                for h in range(PH):
                    yield 53 + h
                    copy_out(("qq", t, h), QP[:, h, :], lambda pb: pb[:, 0:P])
                if t == 2:
                    act.wait_ge(st_out, 32)
                for c in range(2):
                    for g in range(2):
                        yield 62 + 2 * c + g
                        copy_out(("se", t, c, g), SS[:, c, 4 * g:4 * g + 4, :],
                                 lambda pb: pb[:, :].rearrange("p (h n) -> p h n", h=4))
                yield 102
                act.wait_ge(top_ready, t + 1)
                own.done(nc.scalar.activation(EXF, EXF, ACT.Exp), gate_exp)

            in_slots(front(0))(ALL)
            front1, front2 = in_slots(front(1)), in_slots(front(2))

            def fronts(slot):
                front1(slot)
                front2(slot - SLOTS)

            def weigh(i):
                act.wait_ge(dots_done, i + 1)
                nc.scalar.activation(GELU[:, :], DOTS[:, :], ACT.Gelu).then_inc(gelu_done, 1)
                act.wait_ge(wgt_done, i + 1)
                straight = isinstance(i, int)
                for s in range(PK):
                    act.wait_ge(v_free, i * PK + s + 1)
                    nc.scalar.activation(DIAG[:, s % ND, :], IDENT, ACT.Copy, scale=WGT[:, s:s + 1]).then_inc(diag_ready, 1)
                    if straight and s == ND - 1 and i and i % PH == 0:
                        read_y(i // PH - 1)
                    if straight and s >= ND:
                        fronts((i + 1) * PK + s - ND)
                if straight:
                    fronts((i + 1) * PK + PK - 1)

            def read_y(t):
                for n in range(2):
                    act.wait_ge(y_full, 2 * t + n + 1)
                    own.done(nc.scalar.activation(X[:, t, n * 512:(n + 1) * 512], bank[6 + n][:, :], ACT.Copy), y_ready)

            fronts(PK - 1)
            for i in range(2 * PH + 1):
                weigh(i)
            with act.Fori(2 * PH + 1, HEADS) as i:
                weigh(i)
            read_y(2)

        @block.vector
        def _(dve):
            own = Turns(dve, dve_step)
            v = nc.vector
            dve.wait_ge(std1, 1)
            dve.wait_ge(n1_in, 16)
            STD1 = SMALL[:, 3:6]
            own.done(v.reciprocal(STD1, STD1))
            for t in range(NT):
                own.done(v.scalar_tensor_tensor(out=XN[:, t, :], in0=X[:, t, :], scalar=STD1[:, t:t + 1], in1=NB[:, :],
                                                op0=ALU.mult, op1=ALU.mult), xn_ready)
            pb = take(dve, ("lb",))
            LBE, LBM, LB, OML = SMALL[:, 16:24], SMALL[:, 24:28], SMALL[:, 28:32], SMALL[:, 12:16]
            own.done(v.tensor_copy(LBE, pb[:, 0:8]))
            own.done(v.tensor_tensor(LBM, LBE[:, 0:4], LBE[:, 4:8], ALU.max))
            give(own, v.tensor_tensor(LBE[:, 0:4], LBE[:, 0:4], LBM, ALU.subtract), ("lb",))
            own.done(v.tensor_tensor(LBE[:, 4:8], LBE[:, 4:8], LBM, ALU.subtract), lb_shift)
            dve.wait_ge(lb_exp, 1)
            own.done(v.tensor_tensor(LBM, LBE[:, 0:4], LBE[:, 4:8], ALU.add))
            own.done(v.reciprocal(LBM, LBM))
            own.done(v.tensor_tensor(LB, LBE[:, 0:4], LBM, ALU.mult))
            own.done(v.tensor_scalar(OML, LB, -1.0, 1.0, ALU.mult, ALU.add))
            for t in range(NT):
                pb = take(dve, ("bp", t, 2))
                own.done(v.tensor_copy(ZB[:, t, 16:20, :], pb[:, 0:256].rearrange("p (h d) -> p h d", h=4)))
                own.done(v.tensor_copy(ZB[:, t, 10:12, :], wide(pb[:, 256:320], 1, 2)), zb_dve)
                give(own, v.tensor_scalar(IW[:, t, :], pb[:, 320:328], IH ** -0.5, HD ** -0.5, ALU.mult, ALU.mult),
                     ("bp", t, 2))
            dve.wait_ge(qk_sq, 1)
            QKS = SMALL[:, 32:68]
            own.done(v.tensor_reduce(QKS.rearrange("p (t h) -> p t h", t=NT), SQB.rearrange("p t (h d) -> p t h d", d=HD),
                                     axis=AX, op=ALU.add), qk_sum)
            dve.wait_ge(qk_std, 1)
            dve.wait_ge(gain_in, 16 * 12)
            own.done(v.reciprocal(QKS, QKS))
            ZN = ZB[:, :, 0:12, :]
            own.done(v.tensor_tensor(ZN, ZN, wide(QKS.rearrange("p (t h) -> p t h", t=NT), 3, HD), ALU.mult))
            ZF = ZN.rearrange("p t h d -> p t (h d)")
            own.done(v.tensor_tensor(ZF, ZF, wide(GAIN, 1, NT), ALU.mult))
            X1, X2 = ZB[:, :, :, 0:8], ZB[:, :, :, 8:16]
            cosw, sinw = wide(COS, 2, NZ), wide(SIN, 2, NZ)
            R = [view(HOLD, 6144 + k * 480, NT, NZ, 8) for k in range(4)]
            own.done(v.tensor_tensor(R[0], X1, cosw, ALU.mult))
            own.done(v.tensor_tensor(R[1], X2, sinw, ALU.mult))
            own.done(v.tensor_tensor(R[2], X2, cosw, ALU.mult))
            own.done(v.tensor_tensor(R[3], X1, sinw, ALU.mult))
            own.done(v.tensor_tensor(X1, R[0], R[1], ALU.subtract))
            own.done(v.tensor_tensor(X2, R[2], R[3], ALU.add), rope_done)
            own.done(v.tensor_copy(WREP.rearrange("p (k i t) -> p k i t", k=2, i=4),
                                   wide(IW[:, 2, :].rearrange("p (i k) -> p k i", k=2), 3, TS)), wrep_done)

            stored(dve, ("dt", 1, 1, 1))
            for t in range(2):
                nk = (t + 1) * P
                sc = SCORE[:, 0:nk]
                own.done(v.tensor_scalar(sc, RP[t][:, 0, :], IW[:, t, 0:1], None, ALU.mult))
                for h in range(1, IH):
                    own.done(v.scalar_tensor_tensor(out=sc, in0=RP[t][:, h, :], scalar=IW[:, t, h:h + 1], in1=sc,
                                                    op0=ALU.mult, op1=ALU.add))
                own.done(v.memset(SCORE[0:HD, nk - HD:nk], MASKED))
                pick(own, v, sc, TOP8[:, :], TOP_P // 8)
                own.done(v.tensor_scalar(PEN[t][:, :], sc, PICKED, DROP, ALU.not_equal, ALU.mult), pen_ready)
            pb = take(dve, ("wt",))
            give(own, v.tensor_tensor(
                REG[:, 12800:12800 + BD_ * (P + TS)].rearrange("p (b c) -> p b c", b=BD_)[:, :, 0:TS], pb[:, 0:P].rearrange("p (b t) -> p b t", b=BD_), TTM.rearrange("p (b t) -> p b t", b=BD_),
                ALU.mult), ("wt",))
            own.done(v.memset(SCORE[:, KS:KS + SPARE], DUMMY), wz_ready)
            pb = take(dve, ("sc",))
            give(own, v.tensor_copy(SCORE[:, 0:KS], pb[:, 0:KS]), ("sc",))
            pick(own, v, SCORE[:, :], TOP8[:, :], (TOP_S + SPARE) // 8)
            own.done(v.tensor_scalar(PEN[2][:, :], SCORE[:, 0:KS], PICKED, DROP, ALU.not_equal, ALU.mult), pen_ready)

            NM, SUM = SMALL[:, 96:120], SMALL[:, 120:144]

            def negmax(cols, src):
                own.done(v.tensor_reduce(NM[:, cols], src, axis=AX, op=ALU.max))
                own.done(v.tensor_scalar(NM[:, cols], NM[:, cols], -(HD ** -0.5), None, ALU.mult), nmax)

            for t in range(2):
                per = 4 // (t + 1)
                for kv in range(2):
                    for g in range(t + 1):
                        pb = take(dve, ("lg", t, kv, g))
                        c0 = t * 8 + kv * 4 + g * per
                        negmax(slice(c0, c0 + per), pb[:, :].rearrange("p (i n) -> p i n", i=per))
                stored(dve, ("lg", t, 1, t))
                cols = slice(t * 8, t * 8 + 8)
                own.done(v.reciprocal(SUM[:, cols], SUM[:, cols]))
                own.done(v.tensor_tensor(PP[t], PP[t], wide(SUM[:, cols], 2, (t + 1) * P), ALU.mult), pnorm)
            for b in range(BD_):
                pb = take(dve, ("lgs", b))
                negmax(slice(16 + b, 17 + b), pb[:, 0:KS])
            stored(dve, ("lgs", BD_ - 1))
            own.done(v.reciprocal(SUM[:, 16:24], SUM[:, 16:24]))
            own.done(v.tensor_tensor(PS_, PS_, wide(SUM[:, 16:24], 2, KS), ALU.mult), pnorm)

            for h in range(AH):
                own.done(v.tensor_scalar(FG[:, h, :], FG[:, h, :], OML[:, h:h + 1], LB[:, h:h + 1], ALU.mult, ALU.add),
                         None if h < AH - 1 else f_done)
            dve.wait_ge(logf, 1)
            own.done(v.tensor_scalar(FG, FG, -1.0, 1.0, ALU.mult, ALU.add))
            for h in range(AH):
                own.done(v.tensor_tensor_scan(out=CUM[:, h, :], data0=SCAN, data1=LF[:, h, :], initial=0.0,
                                              op0=ALU.mult, op1=ALU.add), None if h < AH - 1 else cum_done)
            blocks = "p h (b t) -> p (h b) t"
            cumb = CUM.rearrange(blocks, t=BLK)
            ends = cumb[:, :, BLK - 1:BLK].to_broadcast([P, AH * TOK // BLK, BLK])
            own.done(v.tensor_tensor(LF.rearrange(blocks, t=BLK), ends, cumb, ALU.subtract), gap_done)
            stored(dve, ("gp", AH - 1))
            dve.wait_ge(e_pos, 1)
            own.done(v.tensor_tensor(SQ, SQ, EB, ALU.mult))
            own.done(v.tensor_copy(EBE.rearrange("p h b -> p (h b)"), EB.rearrange(blocks, t=BLK)[:, :, BLK - 1]))
            dve.wait_ge(e_neg, 1)
            own.done(v.tensor_tensor(KT, KT, FG, ALU.mult))
            dve.wait_ge(e_gap, 1)
            own.done(v.tensor_tensor(LF, LF, FG, ALU.mult), key_done)
            dve.wait_ge(rep_in, 32)
            dve.wait_ge(att_zero, 2)
            dve.wait_ge(gn_in, 16)
            dve.wait_ge(n2_in, 16)
            dve.wait_ge(h_in, 32)

            def update(t, b):
                pb = take(dve, ("u", t, b))
                if t < 2:
                    old, new = S[:, b], S[:, 8 if (t, b) == (1, 7) else (b + 1) % 8]
                else:
                    old = new = S[:, b]
                if (t, b) == (0, 0):
                    give(own, v.tensor_copy(new, pb[:, :].rearrange("p (h n) -> p h n", h=AH)), ("u", t, b))
                    return
                for h in range(AH):
                    ins = v.scalar_tensor_tensor(out=new[:, h, :], in0=old[:, h, :], scalar=EBE[:, h, t * 8 + b:t * 8 + b + 1],
                                                 in1=pb[:, h * P:(h + 1) * P], op0=ALU.mult, op1=ALU.add)
                    if h < AH - 1:
                        own.mark(ins)
                own.caught_up()
                give(own, ins, ("u", t, b))

            def front(t):
                yield 2
                pb = take(dve, ("ke", t))
                if t:
                    take(dve, ("u", t - 1, 7))
                own.done(v.tensor_scalar(KE[:, 0, :], pb[:, :], CST[:, C_EVEN:C_EVEN + 1], None, ALU.mult))
                give(own, v.tensor_scalar(KE[:, 1, :], pb[:, :], CST[:, C_ODD:C_ODD + 1], None, ALU.mult), ("ke", t))
                yield 3
                pb = take(dve, ("at", t))
                if t:
                    take(dve, ("ot", t - 1))
                give(own, v.copy_predicated(ATT, wide(BMASK[:, :], 1, AH), pb[:, :].rearrange("p (h n) -> p h n", h=AH)),
                     ("at", t))
                if t < 2:
                    for b in range(8):
                        yield 5 + b
                        update(t, b)
                yield 28 if t < 2 else 20
                stored(dve, ("ss", t))
                own.done(v.reciprocal(RSTD, RSTD))
                pb = take(dve, ("ot", t))
                give(own, v.scalar_tensor_tensor(out=NORMED, in0=pb[:, :], scalar=GNORM[:, 0:1], in1=RSTD,
                                                 op0=ALU.mult, op1=ALU.mult), ("ot", t))
                own.done(v.tensor_tensor(MIXA[:, :, t * P:(t + 1) * P], NORMED.rearrange("p (h n) -> p h n", h=AH),
                                         SG[:, :, t * P:(t + 1) * P], ALU.mult), mixa_ready)
                if t == 2:
                    for b in range(8):
                        yield 21 + b
                        update(t, b)
                for n in range(KC):
                    yield 31 + 2 * n
                    pb = take(dve, ("wo", t, n))
                    part = X[:, t, n * P:(n + 1) * P]
                    give(own, v.tensor_tensor(part, pb[:, 0:P], part, ALU.add), ("wo", t, n))
                yield 47
                dve.wait_ge(std2, t + 1)
                STD2 = SMALL[:, 9 + t:10 + t]
                own.done(v.reciprocal(STD2, STD2))
                if t == 2:
                    dve.wait_ge(u_free, PH * PK + RU)
                own.done(v.scalar_tensor_tensor(out=XN2[:, t % 2, :], in0=X[:, t, :], scalar=STD2, in1=NB[:, :],
                                                op0=ALU.mult, op1=ALU.mult), xn2_ready)
                for n in range(4):
                    yield 65 + 5 * n
                    if n % 2 == 0:
                        stored(dve, ("se", t, n // 2, 1))
                    rows = [(n // 2, 4 * (n % 2) + i) for i in range(4)]
                    yield from top16(own, v, [(SS[:, c, h, :], SV[:, c, h, :], SIU[:, c, h, :].bitcast(U32)) for c, h in rows],
                                     65 + 5 * n)
                yield 85
                own.caught_up()
                own.done(v.tensor_copy(SIF, SIU.bitcast(U32)))
                yield 86
                own.done(v.tensor_tensor(CAND, wide(SV[:, 0], 3, PK), wide(SV[:, 1], 2, PK), ALU.add))
                for n in range(2):
                    yield from top16(own, v, [(CAND[:, h].rearrange("p i j -> p (i j)"), FV[:, h, :],
                                               FI[:, h, :].bitcast(U32)) for h in range(4 * n, 4 * n + 4)], 88 + 6 * n)
                yield 101
                own.caught_up()
                own.done(v.tensor_tensor(EXF, FV, FV[:, :, 0:1].to_broadcast([P, PH, PK]), ALU.subtract), top_ready)
                fiu = FI.bitcast(U32).rearrange("p h k -> p (h k)")
                for c in range(2):
                    yield 102 + 7 * c
                    if c == 0:
                        own.done(v.tensor_scalar(FPART.bitcast(U32), fiu, 4, None, ALU.logical_shift_right))
                    else:
                        own.done(v.tensor_scalar(FPART.bitcast(U32), fiu, PK - 1, None, ALU.bitwise_and))
                    own.done(v.tensor_copy(FPF, FPART.bitcast(U32)))
                    own.done(v.tensor_tensor(OH, wide(FPF, 2, PK), wide(IOTA, 1, P), ALU.is_equal))
                    yield 104 + 7 * c
                    OHH = OH.rearrange("p (h k) i -> p h k i", h=PH)
                    own.done(v.tensor_tensor(OHH, OHH, wide(SIF[:, c], 2, PK), ALU.mult))
                    yield 106 + 7 * c
                    own.done(v.tensor_reduce(EPART[:, c, :], OH, axis=AX, op=ALU.add))
                yield 115
                own.done(v.scalar_tensor_tensor(out=EIDX[:, t * P:(t + 1) * P], in0=EPART[:, 0, :], scalar=float(NKEY),
                                                in1=EPART[:, 1, :], op0=ALU.mult, op1=ALU.add))
                dve.wait_ge(gate_exp, t + 1)
                own.done(v.tensor_reduce(GSUM, EXF, axis=AX, op=ALU.add))
                own.done(v.reciprocal(GSUM, GSUM))
                own.done(v.tensor_tensor(GATE[:, t * P:(t + 1) * P].rearrange("p (h k) -> p h k", h=PH), EXF,
                                         wide(GSUM, 2, PK), ALU.mult), heads_chosen, PH)

            in_slots(front(0))(ALL)
            front1, front2 = in_slots(front(1)), in_slots(front(2))

            def weights_of(i):
                dve.wait_ge(gelu_done, i + 1)
                v.tensor_tensor(WGT[:, :], GELU[:, :], GATE[:, bass.ds(i * PK, PK)], ALU.mult).then_inc(wgt_done, 1)

            def dots(i, t):
                for s in range(PK):
                    row = UBUF[s % RU]
                    dve.wait_ge(u_got[s % RU], i * 32 + 16 * (s // RU + 1))
                    dve.wait_ge(u_free, i * PK + s + RU)
                    v.tensor_tensor_reduce(out=row, in0=row, in1=XN2[:, t % 2, :], scale=1.0, scalar=0.0,
                                           op0=ALU.mult, op1=ALU.add, accum_out=DOTS[:, s:s + 1]).then_inc(u_free, 1)
                    if s == PK - 1:
                        dve.wait_ge(u_free, i * PK + PK + RU)
                        v.memset(SMALL[:, 93:94], 0.0).then_inc(dots_done, 1)
                    if isinstance(i, int):
                        front1(i * PK + s)
                        front2(i * PK + s - SLOTS)
                dve.wait_ge(dots_done, i + 1)
                weights_of(i)

            take(dve, ("se", 0, 1, 1))
            v.memset(SMALL[:, 94:95], 0.0).then_inc(u_free, RU)
            for i in range(2 * PH):
                dots(i, i // PH)
            with dve.Fori(2 * PH, HEADS) as i:
                dots(i, 2)

        @block.tensor
        def _(pe):
            mm = nc.tensor.matmul

            def start(name):
                b, turn = PLACE[name]
                if turn > 1:
                    pe.wait_ge(free[b], turn - 1)
                return bank[b]

            def end(ins, name):
                ins.then_inc(full[PLACE[name][0]], 1)

            def weights(chunk):
                s, count = landed[chunk]
                pe.wait_ge(w_in_slot[s], count)
                return W[s]

            def project_rows(name, w, t, n, lhs=XNT, cols=None):
                pb = start(name)
                for c in range(KC):
                    ins = mm(pb[:, 0:n], lhs[:, c, t * P:(t + 1) * P], w[:, c, 0:n], start=c == 0, stop=c == KC - 1)
                end(ins, name)

            def project_channels(name, w, h, lhs=XNT):
                pb = start(name)
                for c in range(KC):
                    ins = mm(pb[:, 0:TOK], w[:, c, h * P:(h + 1) * P], lhs[:, c, :], start=c == 0, stop=c == KC - 1)
                end(ins, name)

            def transposes(name, sources):
                pb = start(name)
                for i, src in enumerate(sources):
                    rows = src.shape[1]
                    ins = nc.tensor.transpose(pb[0:rows, i * P:(i + 1) * P], src, IDENT)
                end(ins, name)

            pe.wait_ge(cst_in, 16)
            for t in range(NT):
                pe.wait_ge(xn_ready, t + 1)
                for g in range(2):
                    transposes(("xt", t, g), [XN[:, t, (4 * g + c) * P:(4 * g + c + 1) * P] for c in range(4)])
            pe.wait_ge(lb_in, 16)
            pb = start(("lb",))
            end(nc.tensor.transpose(pb[:, 0:8], LBRAW[:, :], IDENT[0:8, 0:8]), ("lb",))
            for t in range(NT):
                for g in range(2):
                    stored(pe, ("xt", t, g))
            for c, (chunk, n) in enumerate((("B0", 512), ("B1", 512), ("B2", 328))):
                w = weights(chunk)
                for t in range(NT):
                    project_rows(("bp", t, c), w, t, n)
            w = weights("AI")
            for t in range(NT):
                project_rows(("vp", t), w, t, 512)
            w = weights("AF")
            for h in range(AH):
                project_channels(("fp", h), w, h)
            pe.wait_ge(rope_done, 1)
            for t in range(NT):
                flat = ZB[:, t, :, :].rearrange("p h d -> p (h d)")
                transposes(("tq", t), [flat[:, i * P:(i + 1) * P] for i in range(4)])
                transposes(("ti", t), [flat[:, (6 + i) * P:(7 + i) * P] for i in range(4)])
                transposes(("tk", t), [flat[:, i * P:(i + 1) * P] for i in (4, 5)])
            pe.wait_ge(kc_in, 16)
            for g in range(4):
                transposes(("kc", g), [KCN[:, 2 * g + i // 2, i % 2, :] for i in range(4)])
            pe.wait_ge(ic_in, 16)
            for g in range(4):
                pb = start(("ic", g))
                for i in range(4):
                    src = ICN[:, 2 * g + i // 2, i % 2, :]
                    for k in range(2):
                        ins = mm(pb[k * HD:(k + 1) * HD, i * P:(i + 1) * P], src, IDENT, start=True, stop=True)
                end(ins, ("ic", g))
            stored(pe, ("ic", 3))
            for t in range(2):
                nk, per = (t + 1) * P, 4 // (t + 1)
                for par in range(2):
                    rows = slice(par * HD, (par + 1) * HD)
                    for g in range(t + 1):
                        pb = start(("dt", t, par, g))
                        for i in range(per):
                            ins = mm(pb[:, i * nk:(i + 1) * nk], IQTP[rows, g * per + i, t * P:(t + 1) * P],
                                     IKTP[rows, 0:nk], start=True, stop=True)
                        end(ins, ("dt", t, par, g))
            pe.wait_ge(wrep_done, 1)
            pb = start(("wt",))
            end(nc.tensor.transpose(pb[:, 0:P], WREP, IDENT), ("wt",))
            for b in range(BD_):
                pb = start(("ds", b))
                end(mm(pb[:, 0:KS], IQBD[:, b, :], IKTS[:, b, :], start=True, stop=True), ("ds", b))
            w = weights("AQ")
            for h in range(AH):
                project_channels(("qp", h), w, h)
            w = weights("AG")
            for h in range(AH):
                project_channels(("gp", h), w, h)
            stored(pe, ("ds", BD_ - 1))
            pe.wait_ge(wz_ready, 1)
            pb = start(("sc",))
            for b in range(BD_):
                ins = mm(pb[:, 0:KS], WZ[:, b, :], RS_[:, b, :], start=b == 0, stop=b == BD_ - 1)
            end(ins, ("sc",))
            for t in range(2):
                nk, per = (t + 1) * P, 4 // (t + 1)
                pe.wait_ge(pen_ready, t + 1)
                for kv in range(2):
                    rows = slice(kv * HD, (kv + 1) * HD)
                    for g in range(t + 1):
                        pb = start(("lg", t, kv, g))
                        mm(pb[:, :], IDENT, wide(PEN[t][:, :], 1, per), start=True, stop=False)
                        for i in range(per):
                            ins = mm(pb[:, i * nk:(i + 1) * nk], QTP[rows, g * per + i, t * P:(t + 1) * P], KTP[rows, 0:nk],
                                     start=False, stop=i == per - 1)
                        end(ins, ("lg", t, kv, g))
                pe.wait_ge(pnorm, t + 1)
                if t == 0:
                    stored(pe, ("sc",))
                for kv in range(2):
                    for g in range(t + 1):
                        transposes(("pt", t, kv, g),
                                   [PP[t][:, kv * 4 + (g * 4 + i) // (t + 1), (i % (t + 1)) * P:(i % (t + 1) + 1) * P]
                                    for i in range(4)])
                stored(pe, ("pt", t, 1, t))
                pb = start(("pv", t))
                for kv in range(2):
                    for j in range(4):
                        for s in range(t + 1):
                            ins = mm(pb[kv * HD:(kv + 1) * HD, j * P:(j + 1) * P], VB[:, s, kv * HD:(kv + 1) * HD],
                                     PTP[t][:, (kv * 4 + j) * (t + 1) + s, :], start=s == 0, stop=s == t)
                end(ins, ("pv", t))
            pe.wait_ge(pen_ready, 3)
            pe.wait_ge(rep_in, 32)
            for b in range(BD_):
                pb = start(("lgs", b))
                mm(pb[:, 0:KS], REP[:, b, :], PEN[2][:, :], start=True, stop=False)
                end(mm(pb[:, 0:KS], QBD[:, b, :], KTS[:, b, :], start=False, stop=True), ("lgs", b))
            pe.wait_ge(pnorm, 3)
            for b in range(BD_):
                transposes(("pts", b), [PS_[:, b, 0:P], PS_[:, b, P:2 * P], PS_[:, b, 2 * P:KS]])
            stored(pe, ("pts", BD_ - 1))
            pe.wait_ge(vc_in, 16)
            pe.wait_ge(vn_in, 16 * BD_)
            pb = start(("pvs",))
            for b in range(BD_):
                for kv in range(2):
                    cols = slice(kv * HD, (kv + 1) * HD)
                    dst = pb[cols, b * HD:(b + 1) * HD]
                    for s in range(2):
                        mm(dst, VC[:, b, s, cols], PTS[:, b, s, cols], start=s == 0, stop=False)
                    ins = mm(dst, VN[0:TS, b, cols], PTS[0:TS, b, 2, cols], start=False, stop=True)
            end(ins, ("pvs",))
            pe.wait_ge(key_done, 1)

            def small_weights(kind, t, n):
                if t == 0:
                    return weights(f"{'O' if kind == 'wo' else 'P'}{n // 4}")[:, :, n % 4 * P:(n % 4 + 1) * P]
                s, count = small_landed[(kind, t, n)]
                pe.wait_ge(wq_in[s], count)
                return WQ[s]

            def outer_products(t, slot):
                for b in range(8):
                    yield slot + b
                    if b == 0:
                        stored(pe, ("ke", t))
                    pb = start(("u", t, b))
                    rows = slice(32 * (b // 2), 32 * (b // 2) + 32)
                    for h in range(AH):
                        cols = slice(h * P, (h + 1) * P)
                        ins = mm(pb[:, cols], KE[rows, b % 2, cols], AIV[rows, t, cols], start=True, stop=True)
                    end(ins, ("u", t, b))

            def front(t):
                toks = slice(t * P, (t + 1) * P)
                yield 0
                transposes(("ke", t), [LF[:, h, toks] for h in range(AH)])
                pb = start(("at", t))
                for h in range(AH):
                    ins = mm(pb[:, h * P:(h + 1) * P], KT[:, h, toks], SQ[:, h, toks], start=True, stop=True)
                end(ins, ("at", t))
                if t < 2:
                    yield from outer_products(t, 4)
                for h in range(AH):
                    yield (13 if t < 2 else 6) + 3 * h
                    if h == 0:
                        stored(pe, ("at", t))
                        if t < 2:
                            stored(pe, ("u", t, 6))
                        else:
                            pe.wait_ge(st_in, 16)
                        pb = start(("ot", t))
                    mm(pb[:, h * P:(h + 1) * P], AIV[:, t, h * P:(h + 1) * P], ATT[:, h, :], start=True, stop=False)
                    for b in range(1 if t == 0 else 0, 8):
                        ins = mm(pb[:, h * P + b * BLK:h * P + (b + 1) * BLK], S[:, b, h, :],
                                 SQ[:, h, t * P + b * BLK:t * P + (b + 1) * BLK], start=False, stop=b == 7)
                end(ins, ("ot", t))
                yield 25 if t < 2 else 18
                pe.wait_ge(osq_ready, t + 1)
                pb = start(("ss", t))
                end(mm(pb[:, :], ONES, OSQ, start=True, stop=True), ("ss", t))
                if t == 2:
                    yield from outer_products(t, 19)
                for n in range(KC):
                    yield 30 + 2 * n
                    if n == 0:
                        stored(pe, ("pvs",))
                        pe.wait_ge(mixa_ready, t + 1)
                    w = small_weights("wo", t, n)
                    pb = start(("wo", t, n))
                    for c in range(KC):
                        ins = mm(pb[:, 0:P], (MIXA if c < 4 else MIXB)[:, c % 4, toks], w[:, c, :],
                                 start=c == 0, stop=c == KC - 1)
                    end(ins, ("wo", t, n))
                for g in range(2):
                    yield 49 + g
                    if g == 0:
                        pe.wait_ge(xn2_ready, t + 1)
                    transposes(("x2", t, g), [XN2[:, t % 2, (4 * g + c) * P:(4 * g + c + 1) * P] for c in range(4)])
                if t == 0:
                    pe.wait_ge(sk_in, 32)
                    for g in range(2):
                        pb = start(("sk", g))
                        for i in range(4):
                            for c in range(2):
                                ins = mm(pb[c * HD:(c + 1) * HD, i * P:(i + 1) * P], SKN[:, c, 4 * g + i, :], IDENT,
                                         start=True, stop=True)
                        end(ins, ("sk", g))
                for h in range(PH):
                    yield 52 + h
                    if h == 0:
                        stored(pe, ("x2", t, 0))
                        stored(pe, ("x2", t, 1))
                    w = small_weights("qq", t, h)
                    pb = start(("qq", t, h))
                    for c in range(KC):
                        ins = mm(pb[:, 0:P], w[:, c, :], XNT2[:, c, :], start=c == 0, stop=c == KC - 1)
                    end(ins, ("qq", t, h))
                for c in range(2):
                    rows = slice(c * HD, (c + 1) * HD)
                    for g in range(2):
                        yield 61 + 2 * c + g
                        if (c, g) == (0, 0):
                            stored(pe, ("sk", 1))
                            for h in range(PH):
                                stored(pe, ("qq", t, h))
                        pb = start(("se", t, c, g))
                        for i in range(4):
                            ins = mm(pb[:, i * P:(i + 1) * P], QP[rows, 4 * g + i, :], SKT[rows, 4 * g + i, :],
                                     start=True, stop=True)
                        end(ins, ("se", t, c, g))

            in_slots(front(0))(ALL)
            front1, front2 = in_slots(front(1)), in_slots(front(2))

            def fronts(slot):
                front1(slot)
                front2(slot - SLOTS)

            for b in (6, 7):
                last = [name for n, name in enumerate(ORDER) if n < LOOP_STARTS and PLACE[name][0] == b][-1]
                stored(pe, last)
            pe.wait_ge(att_zero, 2)
            fronts(PK - 1)

            def accumulate(i):
                for s in range(PK):
                    pe.wait_ge(v_got[s % RV], i * 32 + 16 * (s // RV + 1))
                    pe.wait_ge(diag_ready, i * PK + s + 1)
                    for n in range(2):
                        ins = mm(bank[6 + n][:, :], DIAG[:, s % ND, :], VBUF[s % RV][:, n * 512:(n + 1) * 512],
                                 start=False, stop=False)
                    ins.then_inc(v_free, 1)
                    if isinstance(i, int):
                        fronts((i + 1) * PK + s)

            for t in range(NT):
                if t:
                    pe.wait_ge(y_ready, 2 * t)
                for n in range(2):
                    ins = mm(bank[6 + n][:, :], IDENT, X[:, t, n * 512:(n + 1) * 512], start=True, stop=False)
                if t == 0:
                    ins.then_inc(v_free, RV)
                if t < 2:
                    for i in range(t * PH, (t + 1) * PH):
                        accumulate(i)
                else:
                    with pe.Fori(2 * PH, HEADS) as i:
                        accumulate(i)
                for n in range(2):
                    mm(bank[6 + n][:, :], ZERO, X[:, t, n * 512:(n + 1) * 512], start=False, stop=True).then_inc(y_full, 1)


def constants():
    p, c = np.arange(P)[:, None], np.arange(P)[None, :]
    pos = np.stack([np.arange(P), P + np.arange(P), PAST + np.arange(P) % TS], 1).astype(np.float32)
    inv = (np.float32(500000.0) ** (-(np.arange(8, dtype=np.float32) * np.float32(2.0) / np.float32(16.0)))).astype(np.float32)
    ang = (pos[:, :, None] * inv).reshape(P, NT * 8)
    cst = np.zeros((P, C_END), np.float32)
    cst[:, C_ID:C_ID + P] = p == c
    cst[:, C_TT:C_TT + P] = p % TS == c % TS
    cst[:, C_ONE:C_ONE + P] = 1.0
    cst[:, C_SCAN:C_SCAN + TOK] = np.arange(TOK) % BLK != 0
    cst[:, C_COS:C_COS + NT * 8] = np.cos(ang)
    cst[:, C_SIN:C_SIN + NT * 8] = np.sin(ang)
    cst[:, C_IOTA:C_IOTA + PK] = np.arange(PK)
    cst[:, C_EVEN] = np.arange(P) // BLK % 2 == 0
    cst[:, C_ODD] = np.arange(P) // BLK % 2 == 1
    same = (p[:, :, None] // TS == np.arange(BD_)[None, :, None]) & (p[:, :, None] % TS == c[:, None, :] % TS)
    bmask = (p // BLK == c // BLK) & (p <= c)
    return {"cst": cst, "rep": same.astype(np.float32).reshape(P, BD_ * P), "bmask": bmask.astype(np.int32)}


INPUTS = ["x_prompt", "x_sample", "cache_k", "cache_v", "cache_kidx", "state_hgrn", "norm1", "w_in", "a_lb_raw",
          "a_gnorm", "b_qnorm", "b_knorm", "idx_knorm", "w_o", "norm2", "p_wq", "p_subkeys", "p_u", "p_v"]
OUTPUTS = {"y": (TOK, D), "nk_p": (2 * P, KVH * HD), "nv_p": (2 * P, KVH * HD), "ni_p": (2 * P, HD),
           "ns_p": (AH, P, P), "nk_s": (P, KVH * HD), "nv_s": (P, KVH * HD), "ni_s": (P, HD),
           "ns_s": (BD_, AH, P, P)}


def kernel(**inputs):
    import concourse.bacc as bacc
    from concourse.bass_utils import run_bass_kernel_spmd

    nc = bacc.Bacc("TRN2", target_bir_lowering=False, num_devices=1)
    arrays = {f"in_{n}": np.ascontiguousarray(inputs[n]) for n in INPUTS}
    arrays |= {f"in_{n}": v for n, v in constants().items()}
    a = {n[3:]: nc.dram_tensor(n, v.shape, mybir.dt.from_np(v.dtype), kind="ExternalInput").ap() for n, v in arrays.items()}
    a |= {n: nc.dram_tensor(f"out_{n}", shape, F32, kind="ExternalOutput").ap() for n, shape in OUTPUTS.items()}
    a["p_u"] = a["p_u"].rearrange("o e d -> (o e) d")
    a["p_v"] = a["p_v"].rearrange("o e d -> (o e) d")
    trunk_kernel(nc, a)
    r = run_bass_kernel_spmd(nc, [arrays], core_ids=[0]).results[0]
    o = {n: r[f"out_{n}"] for n in OUTPUTS}
    return (o["y"][0:2 * P].reshape(1, 2 * P, D), o["y"][2 * P:].reshape(BD_, TS, D),
            o["nk_p"].reshape(1, 1, 2 * P, KVH, HD), o["nv_p"].reshape(1, 1, 2 * P, KVH, HD),
            o["ni_p"].reshape(1, 1, 2 * P, HD), o["ns_p"].reshape(1, 1, AH, P, P),
            o["nk_s"].reshape(1, BD_, TS, KVH, HD), o["nv_s"].reshape(1, BD_, TS, KVH, HD),
            o["ni_s"].reshape(1, BD_, TS, HD), o["ns_s"].reshape(1, BD_, AH, P, P))
```

```python
from contextlib import ExitStack

import numpy as np

import concourse.bass as bass
from concourse import mybir

F32 = mybir.dt.float32
BF16 = mybir.dt.bfloat16
U32 = mybir.dt.uint32
I32 = mybir.dt.int32
F32R = mybir.dt.float32r
ALU = mybir.AluOpType
ACT = mybir.ActivationFunctionType
AX = mybir.AxisListType.X

P = 128
D = 1024
KC = D // P
NT = 3
TOK = NT * P
N_IN = 3400
EPS = 1e-6
AH = 4
AW = AH * P
BLK = 16
HD = 64
QH, KVH, IH = 8, 2, 8
NZ = 20
BD_, TS = 8, 16
PAST = 256
KS = PAST + TS
TOP_P, TOP_S = 64, 68
SPARE = 4
PH, PK, NKEY = 8, 16, 128
HEADS = NT * PH
RU = RV = 8
ND = 8
SLOTS = PH * PK
START = {1: 41, 2: SLOTS + 18}
ALL = 1 << 30

MASKED, PICKED, DUMMY, DROP = -3.0e38, -3.3e38, 3.0e38, -1.0e30

W_AQ, W_AF, W_AI, W_AG = (0, 512), (512, 512), (1024, 512), (1536, 512)
W_B0, W_B1, W_B2 = (2048, 512), (2560, 512), (3072, 328)
CHUNKS = ["B0", "B1", "B2", "AI", "AF", "AQ", "AG", "O0", "O1", "P0", "P1"]
WSLOTS = 3
SPLIT = ["B1", "B2", "AI", "AF"]
UPPER = 0xFFFFF000
C_ID, C_TT, C_ONE, C_SCAN, C_COS, C_SIN, C_IOTA, C_EVEN, C_ODD, C_END = (
    0, 128, 256, 384, 768, 792, 816, 832, 833, 834)


FIRST_BLOCKS = (0, 2, 4, 6, 1, 3, 5, 7)


def product_order():
    o = [("xt", t, g) for t in range(NT) for g in range(2)] + [("lb",)]
    o += [("bp", t, c) for c in range(3) for t in range(NT)]
    o += [("vp", t) for t in range(NT)] + [("fp", h) for h in range(AH)]
    o += [(k, t) for t in range(NT) for k in ("tq", "ti", "tk")]
    o += [("kc", g) for g in range(4)]
    o += [("dt", 0, par, 0) for par in range(2)] + [("dt", 1, par, g) for par in range(2) for g in range(2)]
    o += [("ic", g) for g in range(4)]
    o += [("qp", h) for h in range(AH)] + [("wt",)] + [("ds", b) for b in range(BD_)]
    o += [("lg", 0, kv, 0) for kv in range(2)] + [("sc",)]
    o += [("lg", 1, kv, g) for kv in range(2) for g in range(2)] + [("gp", h) for h in range(AH)]
    for t in range(2):
        o += [("pt", t, kv, g) for kv in range(2) for g in range(t + 1)] + [("pv", t)]
    o += [("lgs", b) for b in range(BD_)] + [("ke", 0), ("at", 0)] + [("pts", b) for b in range(BD_)]
    loop_starts = 0
    for t in range(NT):
        if t == 1:
            loop_starts = len(o)
        us, ot = [("u", t, b) for b in (FIRST_BLOCKS if t == 0 else range(8))], [("ot", t), ("ss", t)]
        if t:
            o += [("ke", t), ("at", t)]
        o += (us + ot if t < 2 else ot + us) + ([("pvs",)] if t == 0 else [])
        o += [("wo", t, n) for n in range(KC)]
        o += [("x2", t, g) for g in range(2)]
        if t == 0:
            o += [("sk", g) for g in range(2)]
        for h in range(PH):
            o += [("qq", t, h + 1)] if 0 < h < PH - 1 else []
            o += [("qq", t, 0)] if h == 0 else []
            o += [("se", t, h, 0), ("se", t, h, 1)] + ([("qq", t, 1)] if h == 0 else [])
    return o, loop_starts


def places():
    place, turns = {}, [0] * 8
    for n, name in enumerate(ORDER):
        b = n % 8 if n < LOOP_STARTS else (n - LOOP_STARTS) % 6
        turns[b] += 1
        place[name] = (b, turns[b])
    return place


ORDER, LOOP_STARTS = product_order()
PLACE = places()
LAST_OF_CHUNK = {"B0": ("bp", 2, 0), "B1": ("bp", 2, 1), "B2": ("bp", 2, 2), "AI": ("vp", 2), "AF": ("fp", 3),
                 "AQ": ("qp", 3), "AG": ("gp", 3), "O0": ("wo", 0, 3), "O1": ("wo", 0, 7)}


class Turns:

    def __init__(self, eng, step):
        self.eng, self.step, self.count = eng, step, {}

    def done(self, ins, sem=None, by=1):
        sem = self.step if sem is None else sem
        key = sem.name
        self.count[key] = self.count.get(key, 0) + by
        ins.then_inc(sem, by)
        self.eng.wait_ge(sem, self.count[key])

    def mark(self, ins):
        self.count[self.step.name] = self.count.get(self.step.name, 0) + 1
        ins.then_inc(self.step, 1)

    def caught_up(self, behind=0):
        self.eng.wait_ge(self.step, self.count[self.step.name] - behind)


def in_slots(front):
    due = next(front)

    def upto(slot):
        nonlocal due
        while due <= slot:
            due = next(front, ALL + 1)
    return upto


def pick(own, v, scores, top8, rounds):
    for _ in range(rounds):
        own.done(v.max(top8, scores))
        own.done(v.match_replace(out=scores, in_to_replace=top8, in_values=scores, imm_value=PICKED))


def choice_slot(t, h):
    return (5 * (h - 1) if h < 2 else 5 * h + 6) if t == 0 else 63 + 5 * h


def query_slot(h):
    return (47, 50)[h] if h < 2 else 47 + 2 * h


def score_slot(h):
    return 49 if h == 0 else 50 + 2 * h


def top16(own, v, rows, slot, pace):
    for step in range(5):
        yield slot + step // pace
        for row, values, places in rows:
            own.caught_up(len(rows) - 1)
            lo, hi = slice(0, 8), slice(8, 16)
            if step == 0:
                ins = v.max(values[:, lo], row)
            elif step == 1:
                ins = v.max_index(places[:, lo], values[:, lo], row)
            elif step == 2:
                ins = v.match_replace(out=row, in_to_replace=values[:, lo], in_values=row, imm_value=PICKED)
            elif step == 3:
                ins = v.max(values[:, hi], row)
            else:
                ins = v.max_index(places[:, hi], values[:, hi], row)
            own.mark(ins)


def trunk_kernel(nc, a):
    ctx = ExitStack()
    with ctx:
        def sb(name, cols, dt=F32, rows=P):
            return ctx.enter_context(nc.sbuf_tensor(name, [rows, cols], dt))

        def sem(name):
            return ctx.enter_context(nc.semaphore(name))

        def view(t, at, *dims):
            n = int(np.prod(dims))
            v = t[:, at:at + n]
            names = "abcd"[:len(dims)]
            if len(dims) == 1:
                return v
            return v.rearrange(f"p ({' '.join(names)}) -> p {' '.join(names)}",
                               **{k: d for k, d in zip(names, dims)})

        def wide(ap, axis, n):
            v = ap.unsqueeze(axis)
            shape = list(v.shape)
            shape[axis] = n
            return v.to_broadcast(shape)

        CST = sb("CST", C_END)
        IDENT, TTM, ONES = CST[:, C_ID:C_ID + P], CST[:, C_TT:C_TT + P], CST[:, C_ONE:C_ONE + P]
        SCAN = CST[:, C_SCAN:C_SCAN + TOK]
        COS, SIN = view(CST, C_COS, NT, 8), view(CST, C_SIN, NT, 8)
        IOTA = CST[:, C_IOTA:C_IOTA + PK]
        BMASK = sb("BMASK", P, I32)
        REP_ = sb("REP", BD_ * P)
        REP = view(REP_, 0, BD_, P)
        GNORM = sb("GNORM", 1)
        LBRAW = sb("LBRAW", P, rows=8)
        SMALL = sb("SMALL", 512)
        VB = view(sb("VB", NT * P), 0, NT, P)
        IW = view(sb("IW", NT * IH), 0, NT, IH)
        PEN = [sb(f"PEN{t}", n, BF16) for t, n in enumerate((P, 2 * P, KS))]
        SCORE = sb("SCORE", KS + SPARE)
        TOP8 = sb("TOP8", 8)
        XNT_ = sb("XNT", KC * TOK)
        XNT = view(XNT_, 0, KC, TOK)
        XN_ = sb("XN", NT * D)
        XN = view(XN_, 0, NT, D)
        NB = sb("NB", D)
        with nc.sbuf_tensor("PARTS", [P, WSLOTS * KC * 512 + 17152 + NT * D], F32R) as parts_:
            PARTS = parts_
        WR = sb("WR", WSLOTS * KC * 512)
        REG = sb("REG", 17152)
        X_ = sb("X", NT * D)
        X = view(X_, 0, NT, D)
        IN_REG, IN_X = WSLOTS * KC * 512, WSLOTS * KC * 512 + 17152
        WL = [view(PARTS, s * KC * 512, KC, 512) for s in range(WSLOTS)]
        WU = [view(PARTS, IN_REG + 3840 + k * KC * 512, KC, 512) for k in range(2)]
        WU_SAME = [view(REG, 3840 + k * KC * 512, KC, 512) for k in range(2)]
        XNTU, XNTL = view(PARTS, IN_X, KC, TOK), view(PARTS, IN_REG + 12032, KC, TOK)
        W = [view(WR, s * KC * 512, KC, 512) for s in range(WSLOTS)]
        HOLD = sb("HOLD", 6 * NT * AW)
        AIV = view(HOLD, 0, NT, AW)
        FG = view(HOLD, 1536, AH, TOK)
        SQ = view(HOLD, 3072, AH, TOK)
        SG = view(HOLD, 4608, AH, TOK)
        MIXA = view(HOLD, 6144, AH, TOK)
        MIXB = view(HOLD, 7680, AH, TOK)

        ZB = view(REG, 0, NT, NZ, HD)
        KTS, IKTS = view(REG, 3840, BD_, KS), view(REG, 6016, BD_, KS)
        QBD, IQBD = view(REG, 8192, BD_, P), view(REG, 9216, BD_, P)
        QTP, IQTP = view(REG, 10240, 4, 2 * P), view(REG, 11264, 4, 2 * P)
        KTP, IKTP = view(REG, 12288, 2 * P), view(REG, 12544, 2 * P)
        WZ = view(REG, 12800, BD_, P)
        VN = view(REG, 13824, BD_, P)
        VC = view(REG, 14848, BD_, 2, P)
        WREP = view(XN_, 2944, P)
        RS_ = view(XN_, 0, BD_, KS)
        REPB = view(XN_[:, 2176:2176 + BD_ * P // 2].bitcast(BF16), 0, BD_, P)
        IDENTB = XN_[:, 2688:2688 + P // 2].bitcast(BF16)
        PTP = [view(XNT_, 0, 8, P), view(XNT_, 1024, 16, P)]
        RP = [view(X_, 0, 8, P), view(X_, 1024, 8, 2 * P)]
        PP = RP
        PS_ = view(XN_, 0, BD_, KS)
        PTS = view(X_, 0, BD_, 3, P)
        KCN, ICN = view(XN_, 0, BD_, 2, P), view(REG, 15104, BD_, 2, P)
        SQB = view(HOLD, 6144, NT, 12 * HD)
        GAIN = view(HOLD, 8448, 12 * HD)

        KT = view(REG, 0, AH, TOK)
        LF = view(REG, 1536, AH, TOK)
        CUM = view(HOLD, 6144, AH, TOK)
        EB = CUM
        S = view(REG, 3072, 9, AH, P)
        ATT = view(REG, 7680, AH, P)
        KE = view(REG, 8192, 2, AW)
        JUNK = view(REG, 8192, D)
        EBE = view(SMALL, 144, AH, TOK // BLK)
        OSQ = view(HOLD, 1536, AW)
        RSTD = view(HOLD, 2048, AW)
        NORMED = view(HOLD, 2560, AW)

        XN2 = view(XN_, 0, 2, D)
        XNT2 = view(XNT_, 0, KC, P)
        QP = view(XNT_, KC * P, PH, P)
        SKT = view(XNT_, 2 * KC * P, PH, P)
        WQ = [view(REP_, 0, KC, P), view(REG, 15752, KC, P)]
        SKN = view(REG, 15752, PH, P)

        SS = view(REG, 3584, PH, 2, NKEY)
        CAND = view(REG, 3584, PH, PK, PK)
        SEL = REG[:, 13312:14984]
        SV, SIU, SIF = view(SEL, 0, 2, PK), view(SEL, 32, 2, PK), view(SEL, 64, 2, PK)
        FV, FI, EXF = view(SEL, 96, PK), view(SEL, 112, PK), view(SEL, 128, PK)
        FPART, FPF, EPART = view(SEL, 144, 2, PK), view(SEL, 176, 2, PK), view(SEL, 208, 2, PK)
        GSUM = view(SEL, 240, 1)
        OH = view(SEL, 256, 2, PK, PK)
        EIDX = REG[:, 14984:14984 + HEADS * PK].bitcast(U32)
        GATE = REG[:, 15368:15368 + HEADS * PK]

        UBUF = [WR[:, s * D:(s + 1) * D] for s in range(RU)]
        VBUF = [WR[:, (RU + s) * D:(RU + s + 1) * D] for s in range(4)] + [
            REG[:, 9216 + s * D:9216 + (s + 1) * D] for s in range(4)]
        DIAG = view(XN_, 2 * D, ND, P)
        STU, STV = sb("STU", 2 * PK, U32), sb("STV", 2 * PK, U32)
        DOTS, GELU, WGT = sb("DOTS", PK), sb("GELU", PK), sb("WGT", PK)
        ZERO = SMALL[:, 256:320].bitcast(BF16)

        bank = [ctx.enter_context(nc.psum_tensor(f"bank{b}", [P, 512], F32)) for b in range(8)]
        full = [sem(f"full{b}") for b in range(8)]
        free = [sem(f"free{b}") for b in range(8)]

        x_in = [sem(f"x_in{t}") for t in range(NT)]
        cst_in, n1_in, lb_in, gain_in, kc_in, ic_in, vc_in, rep_in, st_in = [
            sem(n) for n in ("cst_in", "n1_in", "lb_in", "gain_in", "kc_in", "ic_in", "vc_in", "rep_in", "st_in")]
        h_in, n2_in, sk_in, gn_in = [sem(n) for n in ("h_in", "n2_in", "sk_in", "gn_in")]
        w_in_slot = [sem(f"w_slot{s}") for s in range(WSLOTS)]
        dve_step, act_step, pool_step = sem("dve_step"), sem("act_step"), sem("pool_step")
        bf_ready = sem("bf_ready")
        split_done = sem("split_done")
        std1, xn_ready = sem("std1"), sem("xn_ready")
        lb_shift, lb_exp = sem("lb_shift"), sem("lb_exp")
        zb_act, zb_dve, qk_sq, qk_sum, qk_std, rope_done, wrep_done = [
            sem(n) for n in ("zb_act", "zb_dve", "qk_sq", "qk_sum", "qk_std", "rope_done", "wrep_done")]
        bd_zero, wz_ready, pen_ready = [
            sem(n) for n in ("bd_zero", "wz_ready", "pen_ready")]
        nmax, pnorm, vn_in, newkv_out = [
            sem(n) for n in ("nmax", "pnorm", "vn_in", "newkv_out")]
        f_done, logf, cum_done, e_pos, e_neg, gap_done, e_gap, key_done = [
            sem(n) for n in ("f_done", "logf", "cum_done", "e_pos", "e_neg", "gap_done", "e_gap", "key_done")]
        att_zero, osq_ready, mixa_ready, st_out = [
            sem(n) for n in ("att_zero", "osq_ready", "mixa_ready", "st_out")]
        std2, xn2_ready = [sem(n) for n in ("std2", "xn2_ready")]
        wq_in = [sem(f"wq_in{s}") for s in range(2)]
        top_ready, gate_exp, heads_chosen = sem("top_ready"), sem("gate_exp"), sem("heads_chosen")
        u_got = [sem(f"u_got{s}") for s in range(RU)]
        v_got = [sem(f"v_got{s}") for s in range(RV)]
        u_free, v_free, staged, go, dots_done, gelu_done, wgt_done, diag_ready = [
            sem(n) for n in ("u_free", "v_free", "staged", "go", "dots_done", "gelu_done", "wgt_done", "diag_ready")]
        y_full, y_ready, y_out = sem("y_full"), sem("y_ready"), sem("y_out")

        def take(eng, name):
            b, turn = PLACE[name]
            eng.wait_ge(full[b], turn)
            return bank[b]

        def stored(eng, name):
            b, turn = PLACE[name]
            eng.wait_ge(free[b], turn)

        def give(own, ins, name):
            b, turn = PLACE[name]
            ins.then_inc(free[b], 1)
            own.eng.wait_ge(free[b], turn)

        block = ctx.enter_context(nc.Block())

        def weight_source(chunk):
            if chunk[0] == "O":
                n = int(chunk[1]) * 512
                wa = a["w_o"][0, 0:AW, n:n + 512].rearrange("(c p) n -> p c n", p=P)
                wb = [a["w_o"][0, AW + kv * 256:AW + (kv + 1) * 256, n:n + 512].rearrange("(j d) n -> d j n", d=HD)
                      for kv in range(2)]
                return wa, wb
            if chunk[0] == "P":
                n = int(chunk[1]) * 512
                return a["p_wq"][0, :, n:n + 512].rearrange("(c p) n -> p c n", p=P), None
            at, n = {"B0": W_B0, "B1": W_B1, "B2": W_B2, "AI": W_AI, "AF": W_AF, "AQ": W_AQ, "AG": W_AG}[chunk]
            return a["w_in"][0, :, at:at + n].rearrange("(c p) n -> p c n", p=P), None

        landed, slot_count = {}, [0] * WSLOTS
        for n, chunk in enumerate(CHUNKS):
            slot_count[n % WSLOTS] += 48 if chunk[0] == "O" else 16
            landed[chunk] = (n % WSLOTS, slot_count[n % WSLOTS])

        small, small_count = [], [0, 0]
        for t in (1, 2):
            for kind in ("wo", "qq"):
                for n in range(KC):
                    s = len(small) % 2
                    small_count[s] += 48 if kind == "wo" else 16
                    small.append(((kind, t, n), s, small_count[s]))
        small_landed = {name: (s, count) for name, s, count in small}

        @block.sync
        def _(sp):
            def load_weights(chunk):
                n = CHUNKS.index(chunk)
                s = n % WSLOTS
                if n >= WSLOTS:
                    take(sp, LAST_OF_CHUNK[CHUNKS[n - WSLOTS]])
                src, halves = weight_source(chunk)
                if halves is None:
                    sp.dma_start(W[s][:, :, 0:src.shape[2]], src).then_inc(w_in_slot[s], 16)
                else:
                    sp.dma_start(W[s][:, 0:4, :], src).then_inc(w_in_slot[s], 16)
                    for kv in range(2):
                        sp.dma_start(W[s][kv * HD:(kv + 1) * HD, 4:8, :], halves[kv]).then_inc(w_in_slot[s], 16)

            for t in range(NT):
                src = a["x_prompt"][0, t * P:(t + 1) * P] if t < 2 else a["x_sample"].rearrange("b t d -> (b t) d")
                sp.dma_start(X[:, t, :], src).then_inc(x_in[t], 16)
                if t == 0:
                    sp.dma_start(NB[:, :], a["norm1"].partition_broadcast(P).rearrange("p o d -> p (o d)")).then_inc(n1_in, 16)
                    sp.dma_start(CST[:, :], a["cst"]).then_inc(cst_in, 16)
            sp.dma_start(LBRAW[:, :], a["a_lb_raw"].rearrange("r (h p) -> (r h) p", p=P)).then_inc(lb_in, 16)
            load_weights("B0")
            load_weights("B1")
            load_weights("B2")
            for s, (src, n) in enumerate(((a["b_qnorm"], 8), (a["b_knorm"], 2), (a["idx_knorm"], 2))):
                at = {0: 0, 1: 8, 2: 10}[s]
                for i in range(n):
                    sp.dma_start(GAIN[:, (at + i) * HD:(at + i + 1) * HD],
                                 src.partition_broadcast(P).rearrange("p o d -> p (o d)")).then_inc(gain_in, 16)
            sp.dma_start(GNORM[:, :], a["a_gnorm"].rearrange("o p -> p o")).then_inc(gn_in, 16)
            sp.dma_start(REP, a["rep"].rearrange("p (b c) -> p b c", c=P)).then_inc(rep_in, 16)
            sp.dma_start(BMASK[:, :], a["bmask"]).then_inc(rep_in, 16)
            take(sp, ("xt", 2, 1))
            take(sp, ("xt", 2, 0))
            sp.dma_start(KCN, a["cache_k"][0].rearrange("b (s p) k d -> p b s (k d)", p=P)).then_inc(kc_in, 16)
            for k in range(2):
                sp.dma_start(ICN[:, :, :, k * HD:(k + 1) * HD],
                             a["cache_kidx"][0].rearrange("b (s p) d -> p b s d", p=P)).then_inc(ic_in, 16)
            sp.wait_ge(xn_ready, NT)
            sp.dma_start(NB[:, :], a["norm2"].partition_broadcast(P).rearrange("p o d -> p (o d)")).then_inc(n2_in, 16)
            for chunk in ("AI", "AF", "AQ", "AG", "O0", "O1", "P0"):
                load_weights(chunk)
            take(sp, ("ic", 3))
            sp.dma_start(VC, a["cache_v"][0].rearrange("b (s p) k d -> p b s (k d)", p=P)).then_inc(vc_in, 16)
            take(sp, ("pvs",))
            sp.dma_start(X[:, 0:2, :], a["x_prompt"][0].rearrange("(t p) d -> p t d", p=P)).then_inc(h_in, 16)
            sp.dma_start(X[:, 2, :], a["x_sample"].rearrange("b t d -> (b t) d")).then_inc(h_in, 16)
            load_weights("P1")
            for c in range(2):
                sp.dma_start(SKN[:, :, c * HD:(c + 1) * HD], a["p_subkeys"][0, :, c].rearrange("h k d -> k h d")).then_inc(sk_in, 16)

            def load_small(k):
                (kind, _, n), s, _ = small[k]
                if k == 1:
                    take(sp, ("sk", 1))
                if k >= 2:
                    take(sp, small[k - 2][0])
                cols = slice(n * P, (n + 1) * P)
                if kind == "wo":
                    sp.dma_start(WQ[s][:, 0:4, :], a["w_o"][0, 0:AW, cols].rearrange("(c p) n -> p c n", p=P)).then_inc(wq_in[s], 16)
                    for kv in range(2):
                        first = AW + kv * 256
                        sp.dma_start(WQ[s][kv * HD:(kv + 1) * HD, 4:8, :],
                                     a["w_o"][0, first:first + 256, cols].rearrange("(j d) n -> d j n", d=HD)).then_inc(wq_in[s], 16)
                else:
                    sp.dma_start(WQ[s], a["p_wq"][0, :, cols].rearrange("(c p) n -> p c n", p=P)).then_inc(wq_in[s], 16)

            def store_y(t):
                for n in range(2):
                    cols = slice(n * 512, (n + 1) * 512)
                    sp.wait_ge(y_ready, 2 * t + n + 1)
                    sp.dma_start(a["y"][t * P:(t + 1) * P, cols], X[:, t, cols]).then_inc(y_out, 16)

            load_small(0)
            load_small(1)
            stored(sp, ("u", 1, 7))
            sp.dma_start(a["ns_p"].rearrange("h d v -> d h v"), S[:, 8, :, :]).then_inc(st_out, 16)
            for k in range(2, 18):
                load_small(k)
            sp.wait_ge(heads_chosen, 2 * PH)
            sp.dma_start(S[:, 0:8, :, :], a["state_hgrn"][0].rearrange("b h d v -> d b h v")).then_inc(st_in, 16)
            store_y(0)
            stored(sp, ("u", 2, 7))
            sp.dma_start(a["ns_s"].rearrange("b h d v -> d b h v"), S[:, 0:8, :, :]).then_inc(st_out, 16)
            for k in range(18, 32):
                load_small(k)
            store_y(1)
            store_y(2)
            sp.wait_ge(st_out, 32)
            sp.wait_ge(y_out, 32 * NT)

        @block.gpsimd
        def _(pool):
            own = Turns(pool, pool_step)
            take(pool, ("fp", AH - 1))
            own.done(nc.gpsimd.memset(QBD, 0.0), bd_zero)
            own.done(nc.gpsimd.memset(IQBD, 0.0), bd_zero)
            own.done(nc.gpsimd.memset(WZ, 0.0), bd_zero)
            take(pool, ("xt", 2, 1))
            pool.wait_ge(rep_in, 32)
            own.done(nc.gpsimd.tensor_copy(REPB, REP), bf_ready)
            own.done(nc.gpsimd.tensor_copy(IDENTB, IDENT), bf_ready)
            pool.wait_ge(rope_done, 1)
            pool.wait_ge(zb_act, NT)
            for t in range(2):
                rows = slice(t * P, (t + 1) * P)
                pool.dma_start(a["nk_p"][rows], ZB[:, t, 8:10, :]).then_inc(newkv_out, 16)
                pool.dma_start(a["nv_p"][rows], VB[:, t, :]).then_inc(newkv_out, 16)
                pool.dma_start(a["ni_p"][rows], ZB[:, t, 10, :]).then_inc(newkv_out, 16)
            pool.dma_start(a["nk_s"], ZB[:, 2, 8:10, :]).then_inc(newkv_out, 16)
            pool.dma_start(a["nv_s"], VB[:, 2, :]).then_inc(newkv_out, 16)
            pool.dma_start(a["ni_s"], ZB[:, 2, 10, :]).then_inc(newkv_out, 16)
            for b in range(BD_):
                pool.dma_start(VN[0:TS, b, :], VB[b * TS:(b + 1) * TS, 2, :]).then_inc(vn_in, 16)
            take(pool, ("ds", BD_ - 1))
            own.done(nc.gpsimd.memset(ATT, 0.0), att_zero)
            own.done(nc.gpsimd.memset(ZERO, 0.0), att_zero)

            pool.wait_ge(heads_chosen, 1)

            def stage(buf, i, par):
                nc.gpsimd.tensor_copy(buf[:, par * PK:(par + 1) * PK], EIDX[:, bass.ds(i * PK, PK)]).then_inc(staged, 1)

            def gather_u(i, par, s):
                pool.wait_ge(u_free, i * PK + s + 1)
                pool.sem_inc(go, 1)
                nc.gpsimd.indirect_dma_start(
                    UBUF[s % RU], None, a["p_u"], bass.IndirectOffsetOnAxis(STU[:, par * PK + s:par * PK + s + 1], 0)
                ).then_inc(u_got[s % RU], 16)

            def gather_v(i, par, s):
                pool.wait_ge(v_free, i * PK + s + 1)
                pool.sem_inc(go, 1)
                nc.gpsimd.indirect_dma_start(
                    VBUF[s % RV], None, a["p_v"], bass.IndirectOffsetOnAxis(STV[:, par * PK + s:par * PK + s + 1], 0)
                ).then_inc(v_got[s % RV], 16)

            def gather_both(i, par, nth):
                pool.wait_ge(heads_chosen, i + 2)
                stage(STU, i + 1, 1 - par)
                stage(STV, i, par)
                pool.wait_ge(staged, nth)
                for s in range(PK):
                    gather_u(i + 1, 1 - par, s)
                    gather_v(i, par, s)

            stage(STU, 0, 0)
            pool.wait_ge(staged, 1)
            for s in range(PK):
                if s % 4 == 0 and s < RU:
                    take(pool, ("qq", 0, s + 3))
                gather_u(0, 0, s)
            with pool.Fori(0, HEADS // 2 - 1) as j:
                gather_both(2 * j, 0, 4 * j + 3)
                gather_both(2 * j + 1, 1, 4 * j + 5)
            gather_both(HEADS - 2, 0, 2 * HEADS - 1)
            stage(STV, HEADS - 1, 1)
            pool.wait_ge(staged, 2 * HEADS)
            for s in range(PK):
                gather_v(HEADS - 1, 1, s)
            pool.wait_ge(newkv_out, 16 * 9)

        @block.scalar
        def _(act):
            own = Turns(act, act_step)

            def copy_out(name, out, in_=None, sem_=None, func=ACT.Copy, **kw):
                pb = take(act, name)
                give(own, nc.scalar.activation(out, pb[:, :] if in_ is None else in_(pb), func, **kw), name)

            SS1, STD1 = SMALL[:, 0:3], SMALL[:, 3:6]
            for t in range(NT):
                act.wait_ge(x_in[t], 16)
                own.done(nc.scalar.activation(view(REG, 4096, D), X[:, t, :], ACT.Square, accum_out=SS1[:, t:t + 1]))
                own.done(nc.scalar.activation(STD1[:, t:t + 1], SS1[:, t:t + 1], ACT.Sqrt, bias=EPS, scale=1.0 / D), std1)
            for t in range(NT):
                for g in range(2):
                    pb = take(act, ("xt", t, g))
                    give(own, nc.scalar.activation(
                        XNT[:, 4 * g:4 * g + 4, t * P:(t + 1) * P], pb[:, :].rearrange("p (c n) -> p c n", c=4), ACT.Copy),
                        ("xt", t, g))
            act.wait_ge(lb_shift, 1)
            own.done(nc.scalar.activation(SMALL[:, 16:24], SMALL[:, 16:24], ACT.Exp), lb_exp)
            for t in range(NT):
                pb = take(act, ("bp", t, 0))
                give(own, nc.scalar.activation(
                    ZB[:, t, 0:8, :].rearrange("p (j k) d -> p k j d", k=2),
                    pb[:, :].rearrange("p (k j d) -> p k j d", k=2, j=4), ACT.Copy), ("bp", t, 0))
            for t in range(NT):
                pb = take(act, ("bp", t, 1))
                own.done(nc.scalar.activation(ZB[:, t, 8:10, :], pb[:, 0:128].rearrange("p (h d) -> p h d", h=2), ACT.Copy))
                own.done(nc.scalar.activation(VB[:, t, :], pb[:, 128:256], ACT.Copy), zb_act)
                give(own, nc.scalar.activation(
                    ZB[:, t, 12:16, :], pb[:, 256:512].rearrange("p (h d) -> p h d", h=4), ACT.Copy), ("bp", t, 1))
            act.wait_ge(zb_dve, NT)
            own.done(nc.scalar.activation(SQB, ZB[:, :, 0:12, :].rearrange("p t h d -> p t (h d)"), ACT.Square), qk_sq)
            act.wait_ge(qk_sum, 1)
            QKS = SMALL[:, 32:68]
            own.done(nc.scalar.activation(QKS, QKS, ACT.Sqrt, bias=EPS, scale=1.0 / HD), qk_std)
            for t in range(NT):
                copy_out(("vp", t), AIV[:, t, :])
            for h in range(AH):
                copy_out(("fp", h), FG[:, h, :], lambda pb: pb[:, 0:TOK], func=ACT.Sigmoid)
            act.wait_ge(bd_zero, 3)
            for t in range(NT):
                for kind, plain, diag in (("tq", QTP, QBD), ("ti", IQTP, IQBD)):
                    pb = take(act, (kind, t))
                    src = pb[:, :].rearrange("p (j n) -> p j n", j=4)
                    if t < 2:
                        give(own, nc.scalar.activation(plain[:, :, t * P:(t + 1) * P], src, ACT.Copy), (kind, t))
                    else:
                        for k in range(2):
                            rows = slice(k * HD, (k + 1) * HD)
                            ins = nc.scalar.activation(
                                diag[rows, :, k * HD:(k + 1) * HD].rearrange("p b (j t) -> p j b t", j=4),
                                src[rows].rearrange("p j (b t) -> p j b t", b=BD_), ACT.Copy)
                            if k:
                                give(own, ins, (kind, t))
                            else:
                                own.done(ins)
                pb = take(act, ("tk", t))
                if t < 2:
                    own.done(nc.scalar.activation(KTP[:, t * P:(t + 1) * P], pb[:, 0:P], ACT.Copy))
                    give(own, nc.scalar.activation(IKTP[:, t * P:(t + 1) * P], pb[:, P:2 * P], ACT.Copy), ("tk", t))
                else:
                    own.done(nc.scalar.activation(KTS[:, :, PAST:KS], pb[:, 0:P].rearrange("p (b t) -> p b t", b=BD_), ACT.Copy))
                    give(own, nc.scalar.activation(
                        IKTS[:, :, PAST:KS], pb[:, P:2 * P].rearrange("p (b t) -> p b t", b=BD_), ACT.Copy), ("tk", t))
            def cached(kind, dst):
                for g in range(4):
                    pb = take(act, (kind, g))
                    give(own, nc.scalar.activation(
                        dst[:, 2 * g:2 * g + 2, 0:PAST], pb[:, :].rearrange("p (b n) -> p b n", b=2), ACT.Copy), (kind, g))

            cached("kc", KTS)
            for par in range(2):
                pb = take(act, ("dt", 0, par, 0))
                give(own, nc.scalar.activation(
                    RP[0].rearrange("p (i k) n -> p k i n", k=2)[:, par], pb[:, :].rearrange("p (i n) -> p i n", i=4),
                    ACT.Relu), ("dt", 0, par, 0))
            for par in range(2):
                for g in range(2):
                    pb = take(act, ("dt", 1, par, g))
                    give(own, nc.scalar.activation(
                        RP[1].rearrange("p (i k) n -> p k i n", k=2)[:, par, 2 * g:2 * g + 2],
                        pb[:, :].rearrange("p (i n) -> p i n", i=2), ACT.Relu), ("dt", 1, par, g))
            cached("ic", IKTS)
            for h in range(AH):
                copy_out(("qp", h), SQ[:, h, :], lambda pb: pb[:, 0:TOK], func=ACT.Silu)
            for b in range(BD_):
                copy_out(("ds", b), RS_[:, b, :], lambda pb: pb[:, 0:KS], func=ACT.Relu)
            act.wait_ge(newkv_out, 16 * 9)
            act.wait_ge(f_done, 1)
            own.done(nc.scalar.activation(LF, FG, ACT.Ln), logf)
            act.wait_ge(cum_done, 1)
            own.done(nc.scalar.activation(KT, CUM, ACT.Exp, scale=-1.0), e_neg)
            act.wait_ge(gap_done, 1)
            own.done(nc.scalar.activation(LF, LF, ACT.Exp), e_gap)
            own.done(nc.scalar.activation(EB, CUM, ACT.Exp), e_pos)

            NM, SUM = SMALL[:, 96:120], SMALL[:, 120:144]
            steps = 0

            def numerators(t):
                nonlocal steps
                nk, per = (t + 1) * P, 4 // (t + 1)
                for kv in range(2):
                    for g in range(t + 1):
                        steps += 1
                        pb = take(act, ("lg", t, kv, g))
                        act.wait_ge(nmax, steps)
                        for i in range(per):
                            head = kv * 4 + g * per + i
                            ins = nc.scalar.activation(
                                PP[t][:, head, :], pb[:, i * nk:(i + 1) * nk], ACT.Exp,
                                bias=NM[:, t * 8 + head:t * 8 + head + 1], scale=HD ** -0.5,
                                accum_out=SUM[:, t * 8 + head:t * 8 + head + 1])
                            if i == per - 1:
                                give(own, ins, ("lg", t, kv, g))
                            else:
                                own.done(ins)

            numerators(0)
            numerators(1)
            for h in range(AH):
                copy_out(("gp", h), SG[:, h, :], lambda pb: pb[:, 0:TOK], func=ACT.Silu)
            for t in range(2):
                for kv in range(2):
                    for g in range(t + 1):
                        at = (kv * 4 + g * 4 // (t + 1)) * (t + 1)
                        pb = take(act, ("pt", t, kv, g))
                        give(own, nc.scalar.activation(PTP[t][:, at:at + 4, :], pb[:, :].rearrange("p (i n) -> p i n", i=4),
                                                       ACT.Copy), ("pt", t, kv, g))
                pb = take(act, ("pv", t))
                give(own, nc.scalar.activation(MIXB[:, :, t * P:(t + 1) * P], pb[:, :].rearrange("p (j n) -> p j n", j=4),
                                               ACT.Copy), ("pv", t))
            for b in range(BD_):
                steps += 1
                pb = take(act, ("lgs", b))
                act.wait_ge(nmax, steps)
                give(own, nc.scalar.activation(PS_[:, b, :], pb[:, 0:KS], ACT.Exp, bias=NM[:, 16 + b:17 + b],
                                               scale=HD ** -0.5, accum_out=SUM[:, 16 + b:17 + b]), ("lgs", b))
            for b in range(BD_):
                pb = take(act, ("pts", b))
                own.done(nc.scalar.activation(PTS[:, b, 0:2, :], pb[:, 0:2 * P].rearrange("p (s n) -> p s n", s=2), ACT.Copy))
                give(own, nc.scalar.activation(PTS[0:TS, b, 2, :], pb[0:TS, 2 * P:3 * P], ACT.Copy), ("pts", b))

            act.wait_ge(key_done, 1)

            def front(t):
                early = 0 if t else -2 * SLOTS
                yield early + (24 if t < 2 else 17)
                pb = take(act, ("ot", t))
                own.done(nc.scalar.activation(OSQ, pb[:, :], ACT.Square), osq_ready)
                yield early + (26 if t < 2 else 19)
                if t:
                    act.wait_ge(mixa_ready, t)
                copy_out(("ss", t), RSTD, func=ACT.Sqrt, bias=EPS, scale=1.0 / P)
                if t == 0:
                    pb = take(act, ("pvs",))
                    give(own, nc.scalar.activation(
                        MIXB[:, :, 2 * P:TOK].rearrange("p j (b t) -> p b j t", b=BD_),
                        pb[:, :].rearrange("p (b j t) -> p b j t", b=BD_, j=4), ACT.Copy), ("pvs",))
                SS2, STD2 = SMALL[:, 6 + t:7 + t], SMALL[:, 9 + t:10 + t]
                yield early + 42
                stored(act, ("wo", t, KC - 1))
                own.done(nc.scalar.activation(JUNK, X[:, t, :], ACT.Square, accum_out=SS2))
                own.done(nc.scalar.activation(STD2, SS2, ACT.Sqrt, bias=EPS, scale=1.0 / D), std2)
                for g in range(2):
                    yield early + 45 + g
                    pb = take(act, ("x2", t, g))
                    give(own, nc.scalar.activation(XNT2[:, 4 * g:4 * g + 4, :], pb[:, :].rearrange("p (c n) -> p c n", c=4),
                                                   ACT.Copy), ("x2", t, g))
                if t == 0:
                    for g in range(2):
                        copy_out(("sk", g), SKT[:, 4 * g:4 * g + 4, :], lambda pb: pb[:, :].rearrange("p (h n) -> p h n", h=4))
                if t == 2:
                    act.wait_ge(st_out, 32)
                def queries(h):
                    copy_out(("qq", t, h), QP[:, h, :], lambda pb: pb[:, 0:P])

                for h in range(PH):
                    if h == 0:
                        yield early + query_slot(0) + 1
                        queries(0)
                    elif h < PH - 1:
                        yield early + query_slot(h + 1) + 1
                        queries(h + 1)
                    yield early + score_slot(h) + 1
                    if t and h == 0:
                        act.wait_ge(heads_chosen, PH * t)
                    for c in range(2):
                        copy_out(("se", t, h, c), SS[:, h, c, :], lambda pb: pb[:, 0:NKEY])
                    if h == 0:
                        yield early + query_slot(1) + 1
                        queries(1)
                for h in range(PH):
                    yield choice_slot(t, h) + 3
                    act.wait_ge(top_ready, t * PH + h + 1)
                    own.done(nc.scalar.activation(EXF, EXF, ACT.Exp), gate_exp)

            front0, front1, front2 = [in_slots(front(t)) for t in range(NT)]
            front0(-1)

            def fronts(slot):
                front0(slot)
                front1(slot - START[1])
                front2(slot - START[2])

            def weigh(i):
                act.wait_ge(dots_done, i + 1)
                nc.scalar.activation(GELU[:, :], DOTS[:, :], ACT.Gelu).then_inc(gelu_done, 1)
                act.wait_ge(wgt_done, i + 1)
                straight = isinstance(i, int)
                for s in range(PK):
                    act.wait_ge(v_free, i * PK + s + 1)
                    nc.scalar.activation(DIAG[:, s % ND, :], IDENT, ACT.Copy, scale=WGT[:, s:s + 1]).then_inc(diag_ready, 1)
                    if straight and s == ND - 1 and i and i % PH == 0:
                        read_y(i // PH - 1)
                    if straight and s >= ND:
                        fronts((i + 1) * PK + s - ND)
                if straight:
                    fronts((i + 1) * PK + PK - 1)

            def read_y(t):
                for n in range(2):
                    act.wait_ge(y_full, 2 * t + n + 1)
                    own.done(nc.scalar.activation(X[:, t, n * 512:(n + 1) * 512], bank[6 + n][:, :], ACT.Copy), y_ready)

            fronts(PK - 1)
            for i in range(2 * PH + 1):
                weigh(i)
            with act.Fori(2 * PH + 1, HEADS) as i:
                weigh(i)
            read_y(2)

        @block.vector
        def _(dve):
            own = Turns(dve, dve_step)
            v = nc.vector
            dve.wait_ge(n1_in, 16)
            STD1 = SMALL[:, 3:6]
            for t in range(NT):
                dve.wait_ge(std1, t + 1)
                own.done(v.reciprocal(STD1[:, t:t + 1], STD1[:, t:t + 1]))
                own.done(v.scalar_tensor_tensor(out=XN[:, t, :], in0=X[:, t, :], scalar=STD1[:, t:t + 1], in1=NB[:, :],
                                                op0=ALU.mult, op1=ALU.mult), xn_ready)
            pb = take(dve, ("lb",))
            LBE, LBM, LB, OML = SMALL[:, 16:24], SMALL[:, 24:28], SMALL[:, 28:32], SMALL[:, 12:16]
            own.done(v.tensor_copy(LBE, pb[:, 0:8]))
            own.done(v.tensor_tensor(LBM, LBE[:, 0:4], LBE[:, 4:8], ALU.max))
            give(own, v.tensor_tensor(LBE[:, 0:4], LBE[:, 0:4], LBM, ALU.subtract), ("lb",))
            own.done(v.tensor_tensor(LBE[:, 4:8], LBE[:, 4:8], LBM, ALU.subtract), lb_shift)
            dve.wait_ge(lb_exp, 1)
            own.done(v.tensor_tensor(LBM, LBE[:, 0:4], LBE[:, 4:8], ALU.add))
            own.done(v.reciprocal(LBM, LBM))
            own.done(v.tensor_tensor(LB, LBE[:, 0:4], LBM, ALU.mult))
            own.done(v.tensor_scalar(OML, LB, -1.0, 1.0, ALU.mult, ALU.add))
            def split(upper, same, lower, source):
                own.done(v.tensor_scalar(same.bitcast(U32), source.bitcast(U32), UPPER, None, ALU.bitwise_and))
                own.done(v.tensor_copy(upper, same))
                own.done(v.tensor_tensor(lower, source, upper.bitcast(F32), ALU.subtract), split_done)

            def split_weights(chunk, n):
                s, count = landed[chunk]
                dve.wait_ge(w_in_slot[s], count)
                k = SPLIT.index(chunk) % 2
                split(WU[k][:, :, 0:n], WU_SAME[k][:, :, 0:n], WL[s][:, :, 0:n], W[s][:, :, 0:n])

            for t in range(NT):
                for g in range(2):
                    stored(dve, ("xt", t, g))
            split(XNTU, view(X_, 0, KC, TOK), XNTL, XNT)
            split_weights("B1", 512)
            split_weights("B2", 328)
            take(dve, LAST_OF_CHUNK["B1"])
            split_weights("AI", 512)
            for t in range(NT):
                pb = take(dve, ("bp", t, 2))
                own.done(v.tensor_copy(ZB[:, t, 16:20, :], pb[:, 0:256].rearrange("p (h d) -> p h d", h=4)))
                own.done(v.tensor_copy(ZB[:, t, 10:12, :], wide(pb[:, 256:320], 1, 2)), zb_dve)
                give(own, v.tensor_scalar(IW[:, t, :], pb[:, 320:328], IH ** -0.5, HD ** -0.5, ALU.mult, ALU.mult),
                     ("bp", t, 2))
            take(dve, LAST_OF_CHUNK["B2"])
            split_weights("AF", 512)
            dve.wait_ge(qk_sq, 1)
            QKS = SMALL[:, 32:68]
            own.done(v.tensor_reduce(QKS.rearrange("p (t h) -> p t h", t=NT), SQB.rearrange("p t (h d) -> p t h d", d=HD),
                                     axis=AX, op=ALU.add), qk_sum)
            dve.wait_ge(qk_std, 1)
            dve.wait_ge(gain_in, 16 * 12)
            own.done(v.reciprocal(QKS, QKS))
            ZN = ZB[:, :, 0:12, :]
            own.done(v.tensor_tensor(ZN, ZN, wide(QKS.rearrange("p (t h) -> p t h", t=NT), 3, HD), ALU.mult))
            ZF = ZN.rearrange("p t h d -> p t (h d)")
            own.done(v.tensor_tensor(ZF, ZF, wide(GAIN, 1, NT), ALU.mult))
            X1, X2 = ZB[:, :, :, 0:8], ZB[:, :, :, 8:16]
            cosw, sinw = wide(COS, 2, NZ), wide(SIN, 2, NZ)
            R = [view(HOLD, 6144 + k * 480, NT, NZ, 8) for k in range(4)]
            own.done(v.tensor_tensor(R[0], X1, cosw, ALU.mult))
            own.done(v.tensor_tensor(R[1], X2, sinw, ALU.mult))
            own.done(v.tensor_tensor(R[2], X2, cosw, ALU.mult))
            own.done(v.tensor_tensor(R[3], X1, sinw, ALU.mult))
            own.done(v.tensor_tensor(X1, R[0], R[1], ALU.subtract))
            own.done(v.tensor_tensor(X2, R[2], R[3], ALU.add), rope_done)
            own.done(v.tensor_copy(WREP.rearrange("p (k i t) -> p k i t", k=2, i=4),
                                   wide(IW[:, 2, :].rearrange("p (i k) -> p k i", k=2), 3, TS)), wrep_done)

            stored(dve, ("fp", AH - 1))
            for h in range(AH):
                own.done(v.tensor_scalar(FG[:, h, :], FG[:, h, :], OML[:, h:h + 1], LB[:, h:h + 1], ALU.mult, ALU.add),
                         None if h < AH - 1 else f_done)

            stored(dve, ("dt", 1, 1, 1))
            for t in range(2):
                nk = (t + 1) * P
                sc = SCORE[:, 0:nk]
                own.done(v.tensor_scalar(sc, RP[t][:, 0, :], IW[:, t, 0:1], None, ALU.mult))
                for h in range(1, IH):
                    own.done(v.scalar_tensor_tensor(out=sc, in0=RP[t][:, h, :], scalar=IW[:, t, h:h + 1], in1=sc,
                                                    op0=ALU.mult, op1=ALU.add))
                own.done(v.memset(SCORE[0:HD, nk - HD:nk], MASKED))
                pick(own, v, sc, TOP8[:, :], TOP_P // 8)
                own.done(v.tensor_scalar(PEN[t][:, :], sc, PICKED, DROP, ALU.not_equal, ALU.mult), pen_ready)
            pb = take(dve, ("wt",))
            give(own, v.tensor_tensor(
                REG[:, 12800:12800 + BD_ * (P + TS)].rearrange("p (b c) -> p b c", b=BD_)[:, :, 0:TS],
                pb[:, 0:P].rearrange("p (b t) -> p b t", b=BD_), TTM.rearrange("p (b t) -> p b t", b=BD_), ALU.mult), ("wt",))
            own.done(v.memset(SCORE[:, KS:KS + SPARE], DUMMY), wz_ready)

            NM, SUM = SMALL[:, 96:120], SMALL[:, 120:144]

            def negmax(cols, src):
                own.done(v.tensor_reduce(NM[:, cols], src, axis=AX, op=ALU.max))
                own.done(v.tensor_scalar(NM[:, cols], NM[:, cols], -(HD ** -0.5), None, ALU.mult), nmax)

            def maxima(t):
                per = 4 // (t + 1)
                for kv in range(2):
                    for g in range(t + 1):
                        pb = take(dve, ("lg", t, kv, g))
                        c0 = t * 8 + kv * 4 + g * per
                        negmax(slice(c0, c0 + per), pb[:, :].rearrange("p (i n) -> p i n", i=per))

            def normalise(t):
                stored(dve, ("lg", t, 1, t))
                cols = slice(t * 8, t * 8 + 8)
                own.done(v.reciprocal(SUM[:, cols], SUM[:, cols]))
                own.done(v.tensor_tensor(PP[t], PP[t], wide(SUM[:, cols], 2, (t + 1) * P), ALU.mult), pnorm)

            maxima(0)
            dve.wait_ge(logf, 1)
            own.done(v.tensor_scalar(FG, FG, -1.0, 1.0, ALU.mult, ALU.add))
            for h in range(AH):
                own.done(v.tensor_tensor_scan(out=CUM[:, h, :], data0=SCAN, data1=LF[:, h, :], initial=0.0,
                                              op0=ALU.mult, op1=ALU.add), None if h < AH - 1 else cum_done)
            blocks = "p h (b t) -> p (h b) t"
            cumb = CUM.rearrange(blocks, t=BLK)
            ends = cumb[:, :, BLK - 1:BLK].to_broadcast([P, AH * TOK // BLK, BLK])
            own.done(v.tensor_tensor(LF.rearrange(blocks, t=BLK), ends, cumb, ALU.subtract), gap_done)
            dve.wait_ge(e_neg, 1)
            own.done(v.tensor_tensor(KT, KT, FG, ALU.mult))
            dve.wait_ge(e_gap, 1)
            own.done(v.tensor_tensor(LF, LF, FG, ALU.mult))
            stored(dve, ("qp", AH - 1))
            dve.wait_ge(e_pos, 1)
            own.done(v.tensor_copy(EBE.rearrange("p h b -> p (h b)"), EB.rearrange(blocks, t=BLK)[:, :, BLK - 1]))
            own.done(v.tensor_tensor(SQ, SQ, EB, ALU.mult), key_done)
            pb = take(dve, ("sc",))
            give(own, v.tensor_copy(SCORE[:, 0:KS], pb[:, 0:KS]), ("sc",))
            normalise(0)
            maxima(1)
            normalise(1)

            pick(own, v, SCORE[:, :], TOP8[:, :], (TOP_S + SPARE) // 8)
            own.done(v.tensor_scalar(PEN[2][:, :], SCORE[:, 0:KS], PICKED, DROP, ALU.not_equal, ALU.mult), pen_ready)
            for b in range(BD_):
                pb = take(dve, ("lgs", b))
                negmax(slice(16 + b, 17 + b), pb[:, 0:KS])
            stored(dve, ("lgs", BD_ - 1))
            own.done(v.reciprocal(SUM[:, 16:24], SUM[:, 16:24]))
            own.done(v.tensor_tensor(PS_, PS_, wide(SUM[:, 16:24], 2, KS), ALU.mult), pnorm)

            dve.wait_ge(rep_in, 32)
            dve.wait_ge(att_zero, 2)
            dve.wait_ge(gn_in, 16)
            dve.wait_ge(n2_in, 16)

            def update(t, b):
                pb = take(dve, ("u", t, b))
                if t < 2:
                    old, new = S[:, b], S[:, 8 if (t, b) == (1, 7) else (b + 1) % 8]
                else:
                    old = new = S[:, b]
                if (t, b) == (0, 0):
                    give(own, v.tensor_copy(new, pb[:, :].rearrange("p (h n) -> p h n", h=AH)), ("u", t, b))
                    return
                for h in range(AH):
                    ins = v.scalar_tensor_tensor(out=new[:, h, :], in0=old[:, h, :], scalar=EBE[:, h, t * 8 + b:t * 8 + b + 1],
                                                 in1=pb[:, h * P:(h + 1) * P], op0=ALU.mult, op1=ALU.add)
                    if h < AH - 1:
                        own.mark(ins)
                own.caught_up()
                give(own, ins, ("u", t, b))

            def front(t):
                early = 0 if t else -2 * SLOTS
                yield early + 2
                pb = take(dve, ("ke", t))
                if t:
                    take(dve, ("u", t - 1, 7))
                own.done(v.tensor_scalar(KE[:, 0, :], pb[:, :], CST[:, C_EVEN:C_EVEN + 1], None, ALU.mult))
                give(own, v.tensor_scalar(KE[:, 1, :], pb[:, :], CST[:, C_ODD:C_ODD + 1], None, ALU.mult), ("ke", t))
                yield early + 3
                pb = take(dve, ("at", t))
                if t:
                    take(dve, ("ot", t - 1))
                give(own, v.copy_predicated(ATT, wide(BMASK[:, :], 1, AH), pb[:, :].rearrange("p (h n) -> p h n", h=AH)),
                     ("at", t))
                if t < 2:
                    for b in range(8):
                        yield early + 5 + b
                        update(t, b)
                yield early + (28 if t < 2 else 20)
                stored(dve, ("ss", t))
                own.done(v.reciprocal(RSTD, RSTD))
                pb = take(dve, ("ot", t))
                give(own, v.scalar_tensor_tensor(out=NORMED, in0=pb[:, :], scalar=GNORM[:, 0:1], in1=RSTD,
                                                 op0=ALU.mult, op1=ALU.mult), ("ot", t))
                own.done(v.tensor_tensor(MIXA[:, :, t * P:(t + 1) * P], NORMED.rearrange("p (h n) -> p h n", h=AH),
                                         SG[:, :, t * P:(t + 1) * P], ALU.mult), mixa_ready)
                if t == 2:
                    for b in range(8):
                        yield 21 + b
                        update(t, b)
                for n in range(KC):
                    yield early + 30 + 3 * n // 2
                    pb = take(dve, ("wo", t, n))
                    if (t, n) == (0, 0):
                        dve.wait_ge(h_in, 32)
                    part = X[:, t, n * P:(n + 1) * P]
                    give(own, v.tensor_tensor(part, pb[:, 0:P], part, ALU.add), ("wo", t, n))
                yield early + 43
                dve.wait_ge(std2, t + 1)
                STD2 = SMALL[:, 9 + t:10 + t]
                own.done(v.reciprocal(STD2, STD2))
                if t == 2:
                    dve.wait_ge(u_free, PH * PK + RU)
                own.done(v.scalar_tensor_tensor(out=XN2[:, t % 2, :], in0=X[:, t, :], scalar=STD2, in1=NB[:, :],
                                                op0=ALU.mult, op1=ALU.mult), xn2_ready)
                for h in range(PH):
                    slot = choice_slot(t, h)
                    yield slot
                    stored(dve, ("se", t, h, 0))
                    stored(dve, ("se", t, h, 1))
                    yield from top16(own, v, [(SS[:, h, c, :], SV[:, c, :], SIU[:, c, :].bitcast(U32)) for c in range(2)],
                                     slot, 5)
                    yield slot + 1
                    own.caught_up()
                    own.mark(v.tensor_copy(SIF, SIU.bitcast(U32)))
                    own.done(v.tensor_tensor(CAND[:, h], wide(SV[:, 0], 2, PK), wide(SV[:, 1], 1, PK), ALU.add))
                    yield from top16(own, v, [(CAND[:, h].rearrange("p i j -> p (i j)"), FV, FI.bitcast(U32))], slot + 1, 5)
                    yield slot + 2
                    own.caught_up()
                    own.done(v.tensor_tensor(EXF, FV, FV[:, 0:1].to_broadcast([P, PK]), ALU.subtract), top_ready)
                    own.mark(v.tensor_scalar(FPART[:, 0, :].bitcast(U32), FI.bitcast(U32), 4, None, ALU.logical_shift_right))
                    own.mark(v.tensor_scalar(FPART[:, 1, :].bitcast(U32), FI.bitcast(U32), PK - 1, None, ALU.bitwise_and))
                    own.caught_up()
                    own.done(v.tensor_copy(FPF, FPART.bitcast(U32)))
                    own.done(v.tensor_tensor(OH.rearrange("p c k i -> p (c k) i"), wide(FPF.rearrange("p c k -> p (c k)"), 2, PK),
                                             wide(IOTA, 1, 2 * PK), ALU.is_equal))
                    yield slot + 3
                    own.done(v.tensor_tensor(OH, OH, wide(SIF, 2, PK), ALU.mult))
                    own.done(v.tensor_reduce(EPART, OH, axis=AX, op=ALU.add))
                    at = slice((t * PH + h) * PK, (t * PH + h + 1) * PK)
                    own.done(v.scalar_tensor_tensor(out=EIDX[:, at], in0=EPART[:, 0, :], scalar=float(NKEY),
                                                    in1=EPART[:, 1, :], op0=ALU.mult, op1=ALU.add), heads_chosen)
                    yield slot + 5
                    dve.wait_ge(gate_exp, t * PH + h + 1)
                    own.done(v.tensor_reduce(GSUM, EXF, axis=AX, op=ALU.add))
                    own.done(v.reciprocal(GSUM, GSUM))
                    own.done(v.tensor_scalar(GATE[:, at], EXF, GSUM, None, ALU.mult))

            v.memset(SMALL[:, 94:95], 0.0).then_inc(u_free, RU)
            front0, front1, front2 = [in_slots(front(t)) for t in range(NT)]
            front0(-1)

            def fronts(slot):
                front0(slot)
                front1(slot - START[1])
                front2(slot - START[2])


            def weights_of(i):
                dve.wait_ge(gelu_done, i + 1)
                v.tensor_tensor(WGT[:, :], GELU[:, :], GATE[:, bass.ds(i * PK, PK)], ALU.mult).then_inc(wgt_done, 1)

            def dots(i, t):
                for s in range(PK):
                    row = UBUF[s % RU]
                    dve.wait_ge(u_got[s % RU], i * 32 + 16 * (s // RU + 1))
                    dve.wait_ge(u_free, i * PK + s + RU)
                    v.tensor_tensor_reduce(out=row, in0=row, in1=XN2[:, t % 2, :], scale=1.0, scalar=0.0,
                                           op0=ALU.mult, op1=ALU.add, accum_out=DOTS[:, s:s + 1]).then_inc(u_free, 1)
                    if s == PK - 1:
                        dve.wait_ge(u_free, i * PK + PK + RU)
                        v.memset(SMALL[:, 93:94], 0.0).then_inc(dots_done, 1)
                    if isinstance(i, int):
                        fronts(i * PK + s)
                dve.wait_ge(dots_done, i + 1)
                weights_of(i)

            for i in range(2 * PH):
                dots(i, i // PH)
            with dve.Fori(2 * PH, HEADS) as i:
                dots(i, 2)

        @block.tensor
        def _(pe):
            mm = nc.tensor.matmul

            def start(name):
                b, turn = PLACE[name]
                if turn > 1:
                    pe.wait_ge(free[b], turn - 1)
                return bank[b]

            def end(ins, name):
                ins.then_inc(full[PLACE[name][0]], 1)

            def weights(chunk):
                s, count = landed[chunk]
                pe.wait_ge(w_in_slot[s], count)
                return W[s]

            def pairs_of(chunk):
                w = weights(chunk)
                if chunk not in SPLIT:
                    return [(XNT, w)]
                pe.wait_ge(split_done, 2 + SPLIT.index(chunk))
                wu, wl = WU[SPLIT.index(chunk) % 2], WL[landed[chunk][0]]
                return [(XNTU, wu), (XNTU, wl), (XNTL, wu)]

            def project_rows(name, pairs, t, n):
                pb = start(name)
                for c in range(KC):
                    for k, (x, w) in enumerate(pairs):
                        ins = mm(pb[:, 0:n], x[:, c, t * P:(t + 1) * P], w[:, c, 0:n], start=c + k == 0,
                                 stop=(c, k) == (KC - 1, len(pairs) - 1))
                end(ins, name)

            def project_channels(name, pairs, h):
                pb = start(name)
                for c in range(KC):
                    for k, (x, w) in enumerate(pairs):
                        ins = mm(pb[:, 0:TOK], w[:, c, h * P:(h + 1) * P], x[:, c, :], start=c + k == 0,
                                 stop=(c, k) == (KC - 1, len(pairs) - 1))
                end(ins, name)

            def transposes(name, sources):
                pb = start(name)
                for i, src in enumerate(sources):
                    rows = src.shape[1]
                    ins = nc.tensor.transpose(pb[0:rows, i * P:(i + 1) * P], src, IDENT)
                end(ins, name)

            pe.wait_ge(cst_in, 16)
            for t in range(NT):
                pe.wait_ge(xn_ready, t + 1)
                for g in range(2):
                    transposes(("xt", t, g), [XN[:, t, (4 * g + c) * P:(4 * g + c + 1) * P] for c in range(4)])
            pe.wait_ge(lb_in, 16)
            pb = start(("lb",))
            end(nc.tensor.transpose(pb[:, 0:8], LBRAW[:, :], IDENT[0:8, 0:8]), ("lb",))
            for t in range(NT):
                for g in range(2):
                    stored(pe, ("xt", t, g))
            for c, (chunk, n) in enumerate((("B0", 512), ("B1", 512), ("B2", 328))):
                w = pairs_of(chunk)
                for t in range(NT):
                    project_rows(("bp", t, c), w, t, n)
            w = pairs_of("AI")
            for t in range(NT):
                project_rows(("vp", t), w, t, 512)
            w = pairs_of("AF")
            for h in range(AH):
                project_channels(("fp", h), w, h)
            pe.wait_ge(rope_done, 1)
            for t in range(NT):
                flat = ZB[:, t, :, :].rearrange("p h d -> p (h d)")
                transposes(("tq", t), [flat[:, i * P:(i + 1) * P] for i in range(4)])
                transposes(("ti", t), [flat[:, (6 + i) * P:(7 + i) * P] for i in range(4)])
                transposes(("tk", t), [flat[:, i * P:(i + 1) * P] for i in (4, 5)])
            pe.wait_ge(kc_in, 16)
            for g in range(4):
                transposes(("kc", g), [KCN[:, 2 * g + i // 2, i % 2, :] for i in range(4)])
            stored(pe, ("tk", 1))
            for t in range(2):
                nk, per = (t + 1) * P, 4 // (t + 1)
                for par in range(2):
                    rows = slice(par * HD, (par + 1) * HD)
                    for g in range(t + 1):
                        pb = start(("dt", t, par, g))
                        for i in range(per):
                            ins = mm(pb[:, i * nk:(i + 1) * nk], IQTP[rows, g * per + i, t * P:(t + 1) * P],
                                     IKTP[rows, 0:nk], start=True, stop=True)
                        end(ins, ("dt", t, par, g))
            pe.wait_ge(ic_in, 32)
            for g in range(4):
                transposes(("ic", g), [ICN[:, 2 * g + i // 2, i % 2, :] for i in range(4)])
            w = pairs_of("AQ")
            for h in range(AH):
                project_channels(("qp", h), w, h)
            pe.wait_ge(wrep_done, 1)
            pb = start(("wt",))
            end(nc.tensor.transpose(pb[:, 0:P], WREP, IDENT), ("wt",))
            stored(pe, ("ic", 3))
            for b in range(BD_):
                pb = start(("ds", b))
                end(mm(pb[:, 0:KS], IQBD[:, b, :], IKTS[:, b, :], start=True, stop=True), ("ds", b))

            def logits(t):
                nk, per = (t + 1) * P, 4 // (t + 1)
                pe.wait_ge(pen_ready, t + 1)
                for kv in range(2):
                    rows = slice(kv * HD, (kv + 1) * HD)
                    for g in range(t + 1):
                        pb = start(("lg", t, kv, g))
                        mm(pb[:, :], IDENTB, wide(PEN[t][:, :], 1, per), start=True, stop=False)
                        for i in range(per):
                            ins = mm(pb[:, i * nk:(i + 1) * nk], QTP[rows, g * per + i, t * P:(t + 1) * P], KTP[rows, 0:nk],
                                     start=False, stop=i == per - 1)
                        end(ins, ("lg", t, kv, g))

            pe.wait_ge(bf_ready, 2)
            logits(0)
            stored(pe, ("ds", BD_ - 1))
            pe.wait_ge(wz_ready, 1)
            pb = start(("sc",))
            for b in range(BD_):
                ins = mm(pb[:, 0:KS], WZ[:, b, :], RS_[:, b, :], start=b == 0, stop=b == BD_ - 1)
            end(ins, ("sc",))
            logits(1)
            w = pairs_of("AG")
            for h in range(AH):
                project_channels(("gp", h), w, h)
            for t in range(2):
                pe.wait_ge(pnorm, t + 1)
                for kv in range(2):
                    for g in range(t + 1):
                        transposes(("pt", t, kv, g),
                                   [PP[t][:, kv * 4 + (g * 4 + i) // (t + 1), (i % (t + 1)) * P:(i % (t + 1) + 1) * P]
                                    for i in range(4)])
                stored(pe, ("pt", t, 1, t))
                pb = start(("pv", t))
                for kv in range(2):
                    for j in range(4):
                        for s in range(t + 1):
                            ins = mm(pb[kv * HD:(kv + 1) * HD, j * P:(j + 1) * P], VB[:, s, kv * HD:(kv + 1) * HD],
                                     PTP[t][:, (kv * 4 + j) * (t + 1) + s, :], start=s == 0, stop=s == t)
                end(ins, ("pv", t))
            pe.wait_ge(pen_ready, 3)
            pe.wait_ge(rep_in, 32)
            for b in range(BD_):
                pb = start(("lgs", b))
                mm(pb[:, 0:KS], REPB[:, b, :], PEN[2][:, :], start=True, stop=False)
                end(mm(pb[:, 0:KS], QBD[:, b, :], KTS[:, b, :], start=False, stop=True), ("lgs", b))

            def keys_and_dots(t):
                toks = slice(t * P, (t + 1) * P)
                transposes(("ke", t), [LF[:, h, toks] for h in range(AH)])
                pb = start(("at", t))
                for h in range(AH):
                    ins = mm(pb[:, h * P:(h + 1) * P], KT[:, h, toks], SQ[:, h, toks], start=True, stop=True)
                end(ins, ("at", t))

            pe.wait_ge(key_done, 1)
            keys_and_dots(0)
            pe.wait_ge(pnorm, 3)
            for b in range(BD_):
                transposes(("pts", b), [PS_[:, b, 0:P], PS_[:, b, P:2 * P], PS_[:, b, 2 * P:KS]])

            def sequence_values():
                stored(pe, ("pts", BD_ - 1))
                pe.wait_ge(vc_in, 16)
                pe.wait_ge(vn_in, 16 * BD_)
                pb = start(("pvs",))
                for b in range(BD_):
                    for kv in range(2):
                        cols = slice(kv * HD, (kv + 1) * HD)
                        dst = pb[cols, b * HD:(b + 1) * HD]
                        for s in range(2):
                            mm(dst, VC[:, b, s, cols], PTS[:, b, s, cols], start=s == 0, stop=False)
                        ins = mm(dst, VN[0:TS, b, cols], PTS[0:TS, b, 2, cols], start=False, stop=True)
                end(ins, ("pvs",))


            def small_weights(kind, t, n):
                if t == 0:
                    return weights(f"{'O' if kind == 'wo' else 'P'}{n // 4}")[:, :, n % 4 * P:(n % 4 + 1) * P]
                s, count = small_landed[(kind, t, n)]
                pe.wait_ge(wq_in[s], count)
                return WQ[s]

            def outer_products(t, slot):
                together = 4 if t == 0 else 1
                for n in range(0, 8, together):
                    yield slot + n
                    blocks = FIRST_BLOCKS[n:n + 4] if t == 0 else [n]
                    if n == 0:
                        stored(pe, ("ke", t))
                    banks = [start(("u", t, b)) for b in blocks]
                    for h in range(AH):
                        cols = slice(h * P, (h + 1) * P)
                        for b, pb in zip(blocks, banks):
                            rows = slice(32 * (b // 2), 32 * (b // 2) + 32)
                            ins = mm(pb[:, cols], KE[rows, b % 2, cols], AIV[rows, t, cols], start=True, stop=True)
                            if h == AH - 1:
                                end(ins, ("u", t, b))

            def front(t):
                toks = slice(t * P, (t + 1) * P)
                early = 0 if t else -2 * SLOTS
                yield early
                if t:
                    keys_and_dots(t)
                if t < 2:
                    yield from outer_products(t, early + 4)
                for n in range(4):
                    yield early + (13 if t < 2 else 6) + 3 * n
                    if n == 0:
                        stored(pe, ("at", t))
                        pe.wait_ge(att_zero, 2)
                        if t == 2:
                            pe.wait_ge(st_in, 16)
                        pb = start(("ot", t))
                        mm(pb[:, :], ZERO, wide(ZERO, 1, 4), start=True, stop=False)
                        for h in range(AH):
                            cols = slice(h * P, (h + 1) * P)
                            mm(pb[:, cols], AIV[:, t, cols], ATT[:, h, :], start=False, stop=False)
                    for b in (2 * n, 2 * n + 1):
                        if t == 0 and b == 0:
                            continue
                        if t < 2 and b:
                            stored(pe, ("u", t, b - 1))
                        for h in range(AH):
                            ins = mm(pb[:, h * P + b * BLK:h * P + (b + 1) * BLK], S[:, b, h, :],
                                     SQ[:, h, t * P + b * BLK:t * P + (b + 1) * BLK], start=False, stop=(b, h) == (7, AH - 1))
                end(ins, ("ot", t))
                yield early + (25 if t < 2 else 18)
                pe.wait_ge(osq_ready, t + 1)
                pb = start(("ss", t))
                end(mm(pb[:, :], ONES, OSQ, start=True, stop=True), ("ss", t))
                if t == 0:
                    sequence_values()
                if t == 2:
                    yield from outer_products(t, 19)
                for n in range(KC):
                    yield early + 29 + 3 * n // 2
                    if n == 0:
                        if t == 2:
                            stored(pe, ("pvs",))
                        pe.wait_ge(mixa_ready, t + 1)
                    w = small_weights("wo", t, n)
                    pb = start(("wo", t, n))
                    for c in range(KC):
                        ins = mm(pb[:, 0:P], (MIXA if c < 4 else MIXB)[:, c % 4, toks], w[:, c, :],
                                 start=c == 0, stop=c == KC - 1)
                    end(ins, ("wo", t, n))
                for g in range(2):
                    yield early + 44 + g
                    if g == 0:
                        pe.wait_ge(xn2_ready, t + 1)
                    transposes(("x2", t, g), [XN2[:, t % 2, (4 * g + c) * P:(4 * g + c + 1) * P] for c in range(4)])
                if t == 0:
                    pe.wait_ge(sk_in, 32)
                    for g in range(2):
                        transposes(("sk", g), [SKN[:, 4 * g + i, :] for i in range(4)])
                def queries(h):
                    w = small_weights("qq", t, h)
                    pb = start(("qq", t, h))
                    for c in range(KC):
                        ins = mm(pb[:, 0:P], w[:, c, :], XNT2[:, c, :], start=c == 0, stop=c == KC - 1)
                    end(ins, ("qq", t, h))

                for h in range(PH):
                    if h == 0:
                        yield early + query_slot(0)
                        stored(pe, ("x2", t, 0))
                        stored(pe, ("x2", t, 1))
                        queries(0)
                    elif h < PH - 1:
                        yield early + query_slot(h + 1)
                        queries(h + 1)
                    yield early + score_slot(h)
                    stored(pe, ("sk", 1))
                    stored(pe, ("qq", t, h))
                    for c in range(2):
                        rows = slice(c * HD, (c + 1) * HD)
                        pb = start(("se", t, h, c))
                        end(mm(pb[:, 0:P], QP[rows, h, :], SKT[rows, h, :], start=True, stop=True), ("se", t, h, c))
                    if h == 0:
                        yield early + query_slot(1)
                        queries(1)

            front0, front1, front2 = [in_slots(front(t)) for t in range(NT)]
            front0(-1)

            def fronts(slot):
                front0(slot)
                front1(slot - START[1])
                front2(slot - START[2])

            for b in (6, 7):
                last = [name for n, name in enumerate(ORDER) if n < LOOP_STARTS and PLACE[name][0] == b][-1]
                stored(pe, last)
            pe.wait_ge(att_zero, 2)
            fronts(PK - 1)

            def accumulate(i):
                for s in range(PK):
                    pe.wait_ge(v_got[s % RV], i * 32 + 16 * (s // RV + 1))
                    pe.wait_ge(diag_ready, i * PK + s + 1)
                    for n in range(2):
                        ins = mm(bank[6 + n][:, :], DIAG[:, s % ND, :], VBUF[s % RV][:, n * 512:(n + 1) * 512],
                                 start=False, stop=False)
                    ins.then_inc(v_free, 1)
                    if isinstance(i, int):
                        fronts((i + 1) * PK + s)

            for t in range(NT):
                if t:
                    pe.wait_ge(y_ready, 2 * t)
                for n in range(2):
                    ins = mm(bank[6 + n][:, :], IDENT, X[:, t, n * 512:(n + 1) * 512], start=True, stop=False)
                if t == 0:
                    ins.then_inc(v_free, RV)
                if t < 2:
                    for i in range(t * PH, (t + 1) * PH):
                        accumulate(i)
                else:
                    with pe.Fori(2 * PH, HEADS) as i:
                        accumulate(i)
                for n in range(2):
                    mm(bank[6 + n][:, :], ZERO, wide(ZERO, 1, 4), start=False, stop=True).then_inc(y_full, 1)


def constants():
    p, c = np.arange(P)[:, None], np.arange(P)[None, :]
    pos = np.stack([np.arange(P), P + np.arange(P), PAST + np.arange(P) % TS], 1).astype(np.float32)
    inv = (np.float32(500000.0) ** (-(np.arange(8, dtype=np.float32) * np.float32(2.0) / np.float32(16.0)))).astype(np.float32)
    ang = (pos[:, :, None] * inv).reshape(P, NT * 8)
    cst = np.zeros((P, C_END), np.float32)
    cst[:, C_ID:C_ID + P] = p == c
    cst[:, C_TT:C_TT + P] = p % TS == c % TS
    cst[:, C_ONE:C_ONE + P] = 1.0
    cst[:, C_SCAN:C_SCAN + TOK] = np.arange(TOK) % BLK != 0
    cst[:, C_COS:C_COS + NT * 8] = np.cos(ang)
    cst[:, C_SIN:C_SIN + NT * 8] = np.sin(ang)
    cst[:, C_IOTA:C_IOTA + PK] = np.arange(PK)
    cst[:, C_EVEN] = np.arange(P) // BLK % 2 == 0
    cst[:, C_ODD] = np.arange(P) // BLK % 2 == 1
    same = (p[:, :, None] // TS == np.arange(BD_)[None, :, None]) & (p[:, :, None] % TS == c[:, None, :] % TS)
    bmask = (p // BLK == c // BLK) & (p <= c)
    return {"cst": cst, "rep": same.astype(np.float32).reshape(P, BD_ * P), "bmask": bmask.astype(np.int32)}


INPUTS = ["x_prompt", "x_sample", "cache_k", "cache_v", "cache_kidx", "state_hgrn", "norm1", "w_in", "a_lb_raw",
          "a_gnorm", "b_qnorm", "b_knorm", "idx_knorm", "w_o", "norm2", "p_wq", "p_subkeys", "p_u", "p_v"]
OUTPUTS = {"y": (TOK, D), "nk_p": (2 * P, KVH * HD), "nv_p": (2 * P, KVH * HD), "ni_p": (2 * P, HD),
           "ns_p": (AH, P, P), "nk_s": (P, KVH * HD), "nv_s": (P, KVH * HD), "ni_s": (P, HD),
           "ns_s": (BD_, AH, P, P)}


def kernel(**inputs):
    import concourse.bacc as bacc
    from concourse.bass_utils import run_bass_kernel_spmd

    nc = bacc.Bacc("TRN2", target_bir_lowering=False, num_devices=1)
    arrays = {f"in_{n}": np.ascontiguousarray(inputs[n]) for n in INPUTS}
    arrays |= {f"in_{n}": v for n, v in constants().items()}
    a = {n[3:]: nc.dram_tensor(n, v.shape, mybir.dt.from_np(v.dtype), kind="ExternalInput").ap() for n, v in arrays.items()}
    a |= {n: nc.dram_tensor(f"out_{n}", shape, F32, kind="ExternalOutput").ap() for n, shape in OUTPUTS.items()}
    a["p_u"] = a["p_u"].rearrange("o e d -> (o e) d")
    a["p_v"] = a["p_v"].rearrange("o e d -> (o e) d")
    trunk_kernel(nc, a)
    r = run_bass_kernel_spmd(nc, [arrays], core_ids=[0]).results[0]
    o = {n: r[f"out_{n}"] for n in OUTPUTS}
    return (o["y"][0:2 * P].reshape(1, 2 * P, D), o["y"][2 * P:].reshape(BD_, TS, D),
            o["nk_p"].reshape(1, 1, 2 * P, KVH, HD), o["nv_p"].reshape(1, 1, 2 * P, KVH, HD),
            o["ni_p"].reshape(1, 1, 2 * P, HD), o["ns_p"].reshape(1, 1, AH, P, P),
            o["nk_s"].reshape(1, BD_, TS, KVH, HD), o["nv_s"].reshape(1, BD_, TS, KVH, HD),
            o["ni_s"].reshape(1, BD_, TS, HD), o["ns_s"].reshape(1, BD_, AH, P, P))
```
